# Optimizing a Trainium2 kernel written in Bass

```python
import jax, jax.numpy as jnp
from jax import lax
import numpy as np

D_MODEL = 1024
BATCH = 1
SEQ = 256
DEPTH = 2

D_MIX = D_MODEL
D_RG = D_MIX // 2
RG_BLOCKS = 8
RG_BLOCK_W = D_RG // RG_BLOCKS
CONV_W = 4
RG_C = 8.0
GLA_HEADS = 4
GLA_VD = D_MIX - D_RG
GLA_KD = GLA_VD // 2
GLA_DK = GLA_KD // GLA_HEADS
GLA_DV = GLA_VD // GLA_HEADS
GLA_RANK = 16
GLA_TAU = 16.0
GLA_CHUNK = 64
D_IN = 2 * D_RG + 2 * GLA_KD + 2 * GLA_VD + GLA_RANK
D_FF = 2816
N_EXPERTS = 8
TOP_K = 2
N_DENSE = (DEPTH + 1) // 2
N_MOE = DEPTH // 2
EPS = 1e-6


def rms_norm(x, g):
    x32 = x.astype(jnp.float32)
    y = x32 * lax.rsqrt(jnp.mean(jnp.square(x32), axis=-1, keepdims=True) + EPS)
    return (y * g.astype(jnp.float32)).astype(x.dtype)

def modulate(h, shift, scale):
    return h * (1.0 + scale) + shift

def causal_depthwise_conv(u, w, b):
    s = u.shape[1]
    up = jnp.pad(u, ((0, 0), (CONV_W - 1, 0), (0, 0)))
    out = b
    for tap in range(CONV_W):
        out = out + up[:, tap:tap + s] * w[tap]
    return out

def _linear_combine(c1, c2):
    a1, b1 = c1
    a2, b2 = c2
    return a1 * a2, a2 * b1 + b2

def rg_lru(u, wa, ba, wx, bx, lam):
    bsz, s, d = u.shape
    ub = u.reshape(bsz, s, RG_BLOCKS, RG_BLOCK_W)
    r = jax.nn.sigmoid((jnp.einsum('bsnd,nde->bsne', ub, wa).reshape(bsz, s, d) + ba).astype(jnp.float32))
    i = jax.nn.sigmoid((jnp.einsum('bsnd,nde->bsne', ub, wx).reshape(bsz, s, d) + bx).astype(jnp.float32))
    log_a = -RG_C * r * jax.nn.softplus(-lam.astype(jnp.float32))
    a = jnp.exp(log_a)
    mult = jnp.sqrt(-jnp.expm1(2.0 * log_a))
    first = (jnp.arange(s) == 0)[None, :, None]
    mult = jnp.where(first, 1.0, mult)
    b_term = mult * i * u.astype(jnp.float32)
    _, h = lax.associative_scan(_linear_combine, (a, b_term), axis=1)
    return h.astype(u.dtype)

def gla_chunked(q, k, v, log_f):
    out_dtype = v.dtype
    bsz, s, nh, dk = q.shape
    dv = v.shape[-1]
    n = s // GLA_CHUNK
    q = q.astype(jnp.float32) * (dk ** -0.5)
    k = k.astype(jnp.float32)
    v = v.astype(jnp.float32)
    q = q.reshape(bsz, n, GLA_CHUNK, nh, dk)
    k = k.reshape(bsz, n, GLA_CHUNK, nh, dk)
    v = v.reshape(bsz, n, GLA_CHUNK, nh, dv)
    b = jnp.cumsum(log_f.astype(jnp.float32).reshape(bsz, n, GLA_CHUNK, nh, dk), axis=2)
    b_last = b[:, :, -1]
    b_ref = b[:, :, GLA_CHUNK // 2 - 1:GLA_CHUNK // 2]
    q_loc = q * jnp.exp(b - b_ref)
    k_loc = k * jnp.exp(b_ref - b)
    scores = jnp.einsum('bnihd,bnjhd->bnhij', q_loc, k_loc)
    causal = jnp.tril(jnp.ones((GLA_CHUNK, GLA_CHUNK), dtype=bool))
    scores = jnp.where(causal, scores, 0.0)
    o_intra = jnp.einsum('bnhij,bnjhv->bnihv', scores, v)
    k_end = k * jnp.exp(b_last[:, :, None] - b)
    u_chunk = jnp.einsum('bnjhd,bnjhv->bnhdv', k_end, v)
    decay = jnp.exp(b_last)

    def step(state, inp):
        dec, upd = inp
        return dec[..., None] * state + upd, state

    init = jnp.zeros((bsz, nh, dk, dv), jnp.float32)
    _, states = lax.scan(step, init, (jnp.moveaxis(decay, 1, 0), jnp.moveaxis(u_chunk, 1, 0)))
    states = jnp.moveaxis(states, 0, 1)
    o_inter = jnp.einsum('bnihd,bnhdv->bnihv', q * jnp.exp(b), states)
    o = (o_intra + o_inter).reshape(bsz, s, nh, dv)
    return o.astype(out_dtype)

def gla_branch(q, k, v, g, f_low, wg2, bg, norm_g):
    bsz, s, _ = q.shape
    log_f = jax.nn.log_sigmoid((f_low @ wg2 + bg).astype(jnp.float32)) / GLA_TAU
    o = gla_chunked(q.reshape(bsz, s, GLA_HEADS, GLA_DK),
                    k.reshape(bsz, s, GLA_HEADS, GLA_DK),
                    v.reshape(bsz, s, GLA_HEADS, GLA_DV),
                    log_f.reshape(bsz, s, GLA_HEADS, GLA_DK))
    o = rms_norm(o, norm_g)
    return o.reshape(bsz, s, GLA_VD) * jax.nn.silu(g)

def hybrid_mixer(h, w_in, conv_w, conv_b, wa, ba, wx, bx, lam, wg2, bg, gla_g, w_out):
    z = h @ w_in
    splits = np.cumsum([D_RG, D_RG, GLA_KD, GLA_KD, GLA_VD, GLA_VD]).tolist()
    rg_x, rg_gate, q, k, v, g, f_low = jnp.split(z, splits, axis=-1)
    u = causal_depthwise_conv(rg_x, conv_w, conv_b)
    rg_out = rg_lru(u, wa, ba, wx, bx, lam) * jax.nn.gelu(rg_gate)
    gla_out = gla_branch(q, k, v, g, f_low, wg2, bg, gla_g)
    return jnp.concatenate([rg_out, gla_out], axis=-1) @ w_out

def swiglu(h, w1, w3, w2):
    return (jax.nn.silu(h @ w1) * (h @ w3)) @ w2

def moe_swiglu(h, router_w, w1, w3, w2):
    logits = (h @ router_w).astype(jnp.float32)
    top_v, top_i = lax.top_k(logits, TOP_K)
    probs = jax.nn.softmax(top_v, axis=-1)
    gates = jnp.sum(jax.nn.one_hot(top_i, N_EXPERTS, dtype=jnp.float32) * probs[..., None], axis=-2)
    gates = gates.astype(h.dtype)
    y = jnp.zeros_like(h)
    for e in range(N_EXPERTS):
        y = y + gates[..., e:e + 1] * swiglu(h, w1[e], w3[e], w2[e])
    return y

def first_inputs(seed: int = 0) -> dict:
    key = jax.random.key(seed)
    ks = jax.random.split(key, 32)

    def nrm(k, shape, scale):
        return scale * jax.random.normal(k, shape, jnp.float32)

    a0 = jax.random.uniform(ks[13], (DEPTH, D_RG), jnp.float32, 0.9, 0.999)
    a_root = a0 ** (1.0 / RG_C)
    rg_lambda = jnp.log(a_root) - jnp.log1p(-a_root)
    return {
        "x": nrm(ks[0], (BATCH, SEQ, D_MODEL), 1.0),
        "c": nrm(ks[1], (BATCH, D_MODEL), 1.0),
        "ada_w": nrm(ks[2], (DEPTH, D_MODEL, 6 * D_MODEL), 0.5 * D_MODEL ** -0.5),
        "ada_b": nrm(ks[3], (DEPTH, 6 * D_MODEL), 0.01),
        "norm_mix_g": 1.0 + nrm(ks[4], (DEPTH, D_MODEL), 0.05),
        "norm_ffn_g": 1.0 + nrm(ks[5], (DEPTH, D_MODEL), 0.05),
        "w_in": nrm(ks[6], (DEPTH, D_MODEL, D_IN), D_MODEL ** -0.5),
        "rg_conv_w": nrm(ks[7], (DEPTH, CONV_W, D_RG), CONV_W ** -0.5),
        "rg_conv_b": nrm(ks[8], (DEPTH, D_RG), 0.01),
        "rg_wa": nrm(ks[9], (DEPTH, RG_BLOCKS, RG_BLOCK_W, RG_BLOCK_W), RG_BLOCK_W ** -0.5),
        "rg_ba": nrm(ks[10], (DEPTH, D_RG), 0.01),
        "rg_wx": nrm(ks[11], (DEPTH, RG_BLOCKS, RG_BLOCK_W, RG_BLOCK_W), RG_BLOCK_W ** -0.5),
        "rg_bx": nrm(ks[12], (DEPTH, D_RG), 0.01),
        "rg_lambda": rg_lambda,
        "gla_wg2": nrm(ks[14], (DEPTH, GLA_RANK, GLA_KD), GLA_RANK ** -0.5),
        "gla_bg": nrm(ks[15], (DEPTH, GLA_KD), 0.1),
        "gla_norm_g": 1.0 + nrm(ks[16], (DEPTH, GLA_DV), 0.05),
        "w_out": nrm(ks[17], (DEPTH, D_MIX, D_MODEL), D_MIX ** -0.5),
        "ffn_w1": nrm(ks[18], (N_DENSE, D_MODEL, D_FF), D_MODEL ** -0.5),
        "ffn_w3": nrm(ks[19], (N_DENSE, D_MODEL, D_FF), D_MODEL ** -0.5),
        "ffn_w2": nrm(ks[20], (N_DENSE, D_FF, D_MODEL), D_FF ** -0.5),
        "router_w": nrm(ks[21], (N_MOE, D_MODEL, N_EXPERTS), D_MODEL ** -0.5),
        "moe_w1": nrm(ks[22], (N_MOE, N_EXPERTS, D_MODEL, D_FF), D_MODEL ** -0.5),
        "moe_w3": nrm(ks[23], (N_MOE, N_EXPERTS, D_MODEL, D_FF), D_MODEL ** -0.5),
        "moe_w2": nrm(ks[24], (N_MOE, N_EXPERTS, D_FF, D_MODEL), D_FF ** -0.5),
        "final_g": 1.0 + nrm(ks[25], (D_MODEL,), 0.05),
    }

def first_block(x, c, ada_w, ada_b, norm_mix_g, norm_ffn_g, w_in, rg_conv_w, rg_conv_b,
              rg_wa, rg_ba, rg_wx, rg_bx, rg_lambda, gla_wg2, gla_bg, gla_norm_g, w_out,
              ffn_w1, ffn_w3, ffn_w2, router_w, moe_w1, moe_w3, moe_w2, final_g):
    c_act = jax.nn.silu(c)
    for layer in range(DEPTH):
        mod = c_act @ ada_w[layer] + ada_b[layer]
        sh_m, sc_m, gt_m, sh_f, sc_f, gt_f = [m[:, None, :] for m in jnp.split(mod, 6, axis=-1)]
        h = modulate(rms_norm(x, norm_mix_g[layer]), sh_m, sc_m)
        mix = hybrid_mixer(h, w_in[layer], rg_conv_w[layer], rg_conv_b[layer],
                           rg_wa[layer], rg_ba[layer], rg_wx[layer], rg_bx[layer], rg_lambda[layer],
                           gla_wg2[layer], gla_bg[layer], gla_norm_g[layer], w_out[layer])
        x = x + gt_m * mix
        h = modulate(rms_norm(x, norm_ffn_g[layer]), sh_f, sc_f)
        j = layer // 2
        if layer % 2 == 0:
            f = swiglu(h, ffn_w1[j], ffn_w3[j], ffn_w2[j])
        else:
            f = moe_swiglu(h, router_w[j], moe_w1[j], moe_w3[j], moe_w2[j])
        x = x + gt_f * f
    return rms_norm(x, final_g)


CHUNK = 64
Q_BLOCK = 128

MLA_HEADS = 8
Q_LORA = 384
KV_LORA = 256
QK_NOPE = 64
QK_ROPE = 32
V_HEAD = 64
ROPE_THETA = 10000.0

MLSTM_HEADS = 8
MLSTM_HEAD_DIM = 64
MLSTM_W = MLSTM_HEADS * MLSTM_HEAD_DIM
MLSTM_CONV = 4

FFN_CONV = 3

MLA_W = MLA_HEADS * V_HEAD
IN_SIZES = (Q_LORA, KV_LORA, QK_ROPE,
            MLSTM_W, MLSTM_W, MLSTM_W, MLSTM_W,
            MLSTM_HEADS, MLSTM_HEADS,
            D_MODEL, D_MODEL)
IN_COLS = sum(IN_SIZES)


def _rmsnorm(x, w, eps=1e-6):
    x32 = x.astype(jnp.float32)
    y = x32 * lax.rsqrt(jnp.mean(x32 * x32, axis=-1, keepdims=True) + eps)
    return y.astype(x.dtype) * w

def _rope(x, positions):
    half = x.shape[-1] // 2
    inv = ROPE_THETA ** (-jnp.arange(half, dtype=jnp.float32) / half)
    ang = positions.astype(jnp.float32)[..., None] * inv
    if x.ndim == 4:
        ang = ang[:, :, None, :]
    cos = jnp.cos(ang).astype(x.dtype)
    sin = jnp.sin(ang).astype(x.dtype)
    x1, x2 = x[..., :half], x[..., half:]
    return jnp.concatenate([x1 * cos - x2 * sin, x2 * cos + x1 * sin], axis=-1)

def _causal_dwconv(x, w, b):
    k_w, ch = w.shape
    y = lax.conv_general_dilated(
        x, w[:, None, :].astype(x.dtype), window_strides=(1,),
        padding=[(k_w - 1, 0)], dimension_numbers=("NWC", "WIO", "NWC"),
        feature_group_count=ch)
    return y + b

def _mla_attention(q_nope, q_rope, k_nope, k_rope, v):
    s_len = q_nope.shape[1]
    scale = (QK_NOPE + QK_ROPE) ** -0.5
    outs = []
    for qb in range(s_len // Q_BLOCK):
        s0, e = qb * Q_BLOCK, (qb + 1) * Q_BLOCK
        sc = (jnp.einsum("bqhd,bkhd->bhqk", q_nope[:, s0:e], k_nope[:, :e])
              + jnp.einsum("bqhr,bkr->bhqk", q_rope[:, s0:e], k_rope[:, :e]))
        sc = sc.astype(jnp.float32) * scale
        q_chunk = (s0 + jnp.arange(Q_BLOCK)) // CHUNK
        k_chunk = jnp.arange(e) // CHUNK
        sc = jnp.where(k_chunk[None, :] <= q_chunk[:, None], sc, -jnp.inf)
        p = jax.nn.softmax(sc, axis=-1).astype(v.dtype)
        outs.append(jnp.einsum("bhqk,bkhd->bqhd", p, v[:, :e]))
    return jnp.concatenate(outs, axis=1)

def _mlstm_chunkwise(q, k, v, i_pre, log_f):
    bsz, s_len, nh, dk = q.shape
    dv = v.shape[-1]
    L = CHUNK
    nc = s_len // L
    f32 = jnp.float32

    def to_chunks(a):
        return jnp.moveaxis(a.astype(f32).reshape((bsz, nc, L) + a.shape[2:]), 1, 0)

    xs = tuple(to_chunks(a) for a in (q, k, v, i_pre, log_f))
    causal = jnp.tril(jnp.ones((L, L), dtype=bool))

    def step(carry, inp):
        C, n, m = carry
        qc, kc, vc, ic, fc = inp
        b = jnp.cumsum(fc, axis=1).transpose(0, 2, 1)
        ih = ic.transpose(0, 2, 1)
        log_d = jnp.where(causal, b[..., :, None] - b[..., None, :] + ih[..., None, :], -jnp.inf)
        log_inter = b + m[..., None]
        m_t = jnp.maximum(log_inter, jnp.max(log_d, axis=-1))
        w_intra = jnp.exp(log_d - m_t[..., None])
        w_inter = jnp.exp(log_inter - m_t)
        s = jnp.einsum("bthd,bshd->bhts", qc, kc) * w_intra
        num = (jnp.einsum("bhts,bshv->bhtv", s, vc)
               + w_inter[..., None] * jnp.einsum("bhvk,bthk->bhtv", C, qc))
        den = s.sum(-1) + w_inter * jnp.einsum("bhk,bthk->bht", n, qc)
        h = num / jnp.maximum(jnp.abs(den), jnp.exp(-m_t))[..., None]
        b_last = b[..., -1]
        log_w = b_last[..., None] - b + ih
        m_new = jnp.maximum(b_last + m, jnp.max(log_w, axis=-1))
        w_s = jnp.exp(log_w - m_new[..., None])
        decay = jnp.exp(b_last + m - m_new)
        C = decay[..., None, None] * C + jnp.einsum("bhs,bshv,bshk->bhvk", w_s, vc, kc)
        n = decay[..., None] * n + jnp.einsum("bhs,bshk->bhk", w_s, kc)
        return (C, n, m_new), h.transpose(0, 2, 1, 3)

    init = (jnp.zeros((bsz, nh, dv, dk), f32), jnp.zeros((bsz, nh, dk), f32),
            jnp.zeros((bsz, nh), f32))
    _, hs = lax.scan(step, init, xs)
    return jnp.moveaxis(hs, 0, 1).reshape(bsz, s_len, nh, dv).astype(v.dtype)

def _mixer(h, positions, w_in, q_norm_w, kv_norm_w, w_uq, w_ukv, conv_w, conv_b,
           gate_b, head_norm_w, w_br_mla, w_br_mlstm, w_out):
    bsz, s_len, _ = h.shape
    split_at = [int(s) for s in np.cumsum(IN_SIZES)[:-1]]
    proj = h @ w_in
    c_q, c_kv, k_rope, q_m, k_m, v_m, o_m, i_m, f_m, g_mla, g_mlstm = jnp.split(proj, split_at, axis=-1)

    q = (_rmsnorm(c_q, q_norm_w) @ w_uq).reshape(bsz, s_len, MLA_HEADS, QK_NOPE + QK_ROPE)
    q_nope, q_rope = q[..., :QK_NOPE], _rope(q[..., QK_NOPE:], positions)
    kv = (_rmsnorm(c_kv, kv_norm_w) @ w_ukv).reshape(bsz, s_len, MLA_HEADS, QK_NOPE + V_HEAD)
    k_nope, v = kv[..., :QK_NOPE], kv[..., QK_NOPE:]
    k_rope = _rope(k_rope, positions)
    y_mla = _mla_attention(q_nope, q_rope, k_nope, k_rope, v).reshape(bsz, s_len, MLA_W)

    qk = jax.nn.silu(_causal_dwconv(jnp.concatenate([q_m, k_m], axis=-1), conv_w, conv_b))
    q_m, k_m = jnp.split(qk, 2, axis=-1)
    i_pre, f_pre = jnp.split(jnp.concatenate([i_m, f_m], axis=-1) + gate_b, 2, axis=-1)
    hd = (bsz, s_len, MLSTM_HEADS, MLSTM_HEAD_DIM)
    hm = _mlstm_chunkwise(q_m.reshape(hd), k_m.reshape(hd) * (MLSTM_HEAD_DIM ** -0.5),
                          v_m.reshape(hd), i_pre.astype(jnp.float32),
                          jax.nn.log_sigmoid(f_pre.astype(jnp.float32)))
    hm = _rmsnorm(hm, head_norm_w.reshape(MLSTM_HEADS, MLSTM_HEAD_DIM))
    y_mlstm = jax.nn.sigmoid(o_m) * hm.reshape(bsz, s_len, MLSTM_W)

    merged = (jax.nn.sigmoid(g_mla) * (y_mla @ w_br_mla)
              + jax.nn.sigmoid(g_mlstm) * (y_mlstm @ w_br_mlstm))
    return merged @ w_out

def _conv_ffn(h, w_up, conv_w, conv_b, w_down):
    u = _causal_dwconv(h @ w_up, conv_w, conv_b)
    a, val = jnp.split(u, 2, axis=-1)
    return (jax.nn.gelu(a) * val) @ w_down

def second_inputs(seed: int = 0) -> dict:
    key = jax.random.key(seed)
    ks = jax.random.split(key, 32)
    f32 = jnp.float32

    def nrm(k, shape, scale):
        return jax.random.normal(k, shape, f32) * scale

    def gain(k, shape):
        return 1.0 + 0.02 * jax.random.normal(k, shape, f32)

    offsets = jax.random.randint(ks[2], (BATCH, 1), 0, 4096, dtype=jnp.int32)
    positions = offsets + jnp.arange(SEQ, dtype=jnp.int32)[None, :]
    gate_b = jnp.concatenate([
        0.1 * jax.random.normal(ks[12], (DEPTH, MLSTM_HEADS), f32),
        3.0 + 3.0 * jax.random.uniform(ks[13], (DEPTH, MLSTM_HEADS), f32)], axis=-1)
    return {
        "x": nrm(ks[0], (BATCH, SEQ, D_MODEL), 1.0),
        "c": nrm(ks[1], (BATCH, D_MODEL), 1.0),
        "positions": positions,
        "ada_w": nrm(ks[3], (DEPTH, D_MODEL, 6 * D_MODEL), 0.5 * D_MODEL ** -0.5),
        "ada_b": nrm(ks[4], (DEPTH, 6 * D_MODEL), 0.02),
        "norm_mix_w": gain(ks[5], (DEPTH, D_MODEL)),
        "w_in": nrm(ks[6], (DEPTH, D_MODEL, IN_COLS), D_MODEL ** -0.5),
        "q_norm_w": gain(ks[7], (DEPTH, Q_LORA)),
        "kv_norm_w": gain(ks[8], (DEPTH, KV_LORA)),
        "w_uq": nrm(ks[9], (DEPTH, Q_LORA, MLA_HEADS * (QK_NOPE + QK_ROPE)), Q_LORA ** -0.5),
        "w_ukv": nrm(ks[10], (DEPTH, KV_LORA, MLA_HEADS * (QK_NOPE + V_HEAD)), KV_LORA ** -0.5),
        "mlstm_conv_w": nrm(ks[11], (DEPTH, MLSTM_CONV, 2 * MLSTM_W), MLSTM_CONV ** -0.5),
        "mlstm_conv_b": nrm(ks[14], (DEPTH, 2 * MLSTM_W), 0.02),
        "mlstm_gate_b": gate_b,
        "mlstm_head_norm_w": gain(ks[15], (DEPTH, MLSTM_W)),
        "w_br_mla": nrm(ks[16], (DEPTH, MLA_W, D_MODEL), MLA_W ** -0.5),
        "w_br_mlstm": nrm(ks[17], (DEPTH, MLSTM_W, D_MODEL), MLSTM_W ** -0.5),
        "w_out": nrm(ks[18], (DEPTH, D_MODEL, D_MODEL), D_MODEL ** -0.5),
        "norm_ffn_w": gain(ks[19], (DEPTH, D_MODEL)),
        "ffn_w_up": nrm(ks[20], (DEPTH, D_MODEL, 2 * D_FF), D_MODEL ** -0.5),
        "ffn_conv_w": nrm(ks[21], (DEPTH, FFN_CONV, 2 * D_FF), FFN_CONV ** -0.5),
        "ffn_conv_b": nrm(ks[22], (DEPTH, 2 * D_FF), 0.02),
        "ffn_w_down": nrm(ks[23], (DEPTH, D_FF, D_MODEL), D_FF ** -0.5),
        "final_norm_w": gain(ks[24], (D_MODEL,)),
    }

def second_block(x, c, positions, ada_w, ada_b, norm_mix_w, w_in, q_norm_w, kv_norm_w,
              w_uq, w_ukv, mlstm_conv_w, mlstm_conv_b, mlstm_gate_b, mlstm_head_norm_w,
              w_br_mla, w_br_mlstm, w_out, norm_ffn_w, ffn_w_up, ffn_conv_w, ffn_conv_b,
              ffn_w_down, final_norm_w):
    c_act = jax.nn.silu(c)
    for l in range(DEPTH):
        mod = (c_act @ ada_w[l] + ada_b[l])[:, None, :]
        sh1, sc1, g1, sh2, sc2, g2 = jnp.split(mod, 6, axis=-1)
        h = _rmsnorm(x, norm_mix_w[l]) * (1 + sc1) + sh1
        x = x + g1 * _mixer(h, positions, w_in[l], q_norm_w[l], kv_norm_w[l], w_uq[l], w_ukv[l],
                            mlstm_conv_w[l], mlstm_conv_b[l], mlstm_gate_b[l],
                            mlstm_head_norm_w[l], w_br_mla[l], w_br_mlstm[l], w_out[l])
        h = _rmsnorm(x, norm_ffn_w[l]) * (1 + sc2) + sh2
        x = x + g2 * _conv_ffn(h, ffn_w_up[l], ffn_conv_w[l], ffn_conv_b[l], ffn_w_down[l])
    return _rmsnorm(x, final_norm_w)


def setup_inputs(seed=0):
    out = dict(first_inputs(seed))
    for name, value in second_inputs(seed + 1).items():
        if name != "x":
            out[name + "_2"] = value
    return out


def reference(
    x, c, ada_w, ada_b, norm_mix_g, norm_ffn_g, w_in, rg_conv_w, rg_conv_b, rg_wa, rg_ba, rg_wx,
    rg_bx, rg_lambda, gla_wg2, gla_bg, gla_norm_g, w_out, ffn_w1, ffn_w3, ffn_w2, router_w,
    moe_w1, moe_w3, moe_w2, final_g, c_2, positions_2, ada_w_2, ada_b_2, norm_mix_w_2, w_in_2,
    q_norm_w_2, kv_norm_w_2, w_uq_2, w_ukv_2, mlstm_conv_w_2, mlstm_conv_b_2, mlstm_gate_b_2,
    mlstm_head_norm_w_2, w_br_mla_2, w_br_mlstm_2, w_out_2, norm_ffn_w_2, ffn_w_up_2,
    ffn_conv_w_2, ffn_conv_b_2, ffn_w_down_2, final_norm_w_2,
):
    x = first_block(
        x, c, ada_w, ada_b, norm_mix_g, norm_ffn_g, w_in, rg_conv_w, rg_conv_b, rg_wa, rg_ba,
        rg_wx, rg_bx, rg_lambda, gla_wg2, gla_bg, gla_norm_g, w_out, ffn_w1, ffn_w3, ffn_w2,
        router_w, moe_w1, moe_w3, moe_w2, final_g,
    )
    return second_block(
        x, c_2, positions_2, ada_w_2, ada_b_2, norm_mix_w_2, w_in_2, q_norm_w_2, kv_norm_w_2,
        w_uq_2, w_ukv_2, mlstm_conv_w_2, mlstm_conv_b_2, mlstm_gate_b_2, mlstm_head_norm_w_2,
        w_br_mla_2, w_br_mlstm_2, w_out_2, norm_ffn_w_2, ffn_w_up_2, ffn_conv_w_2, ffn_conv_b_2,
        ffn_w_down_2, final_norm_w_2,
    )


_drawn_inputs = setup_inputs


def setup_inputs(seed=0):
    import zlib

    import numpy as np

    out = dict(_drawn_inputs(seed))
    spreads = {}
    factors = {'rg_conv_b': 4.186,
     'rg_ba': 8.0,
     'rg_bx': 8.0,
     'gla_bg': 3.702,
     'gla_norm_g': 3.716,
     'norm_mix_w_2': 8.0,
     'q_norm_w_2': 8.0,
     'kv_norm_w_2': 8.0,
     'mlstm_conv_b_2': 64.0,
     'mlstm_head_norm_w_2': 8.0,
     'norm_ffn_w_2': 5.994,
     'ffn_conv_b_2': 6.382,
     'final_norm_w_2': 8.128}
    for name, (base, spread) in spreads.items():
        noise = np.random.default_rng([zlib.crc32(name.encode()), seed]).standard_normal(out[name].shape)
        drawn = base * np.exp(spread * noise) if base else spread * noise
        out[name] = __import__('jax').numpy.asarray(drawn.astype(out[name].dtype))
    for name, factor in factors.items():
        out[name] = (out[name] * factor).astype(out[name].dtype)
    return out
```

```python
from collections import Counter
from contextlib import ExitStack

import numpy as np

import concourse.bass as bass
from concourse import mybir

F32 = mybir.dt.float32
I32 = mybir.dt.int32
U32 = mybir.dt.uint32
ALU = mybir.AluOpType
ACT = mybir.ActivationFunctionType
AX_X = mybir.AxisListType.X

P = 128
T = 256
TB = T // P
DM = 1024
KB = DM // P
EPS = 1e-6
DFF = 2816
EXPERTS = 8
CHUNK_COLS = 256
CHUNKS = DFF // CHUNK_COLS
MODS = 6 * KB

RING = 6
SLOT = 2048
ADA_SLOTS = 3
ADA_PER_LAYER = KB * ADA_SLOTS

BIG_NEG = -1.0e30
ROPE_THETA = 10000.0
QK_SCALE = 96.0 ** -0.5
TWO_PI_HI = 6.28125
TWO_PI_LO = float(2.0 * np.pi - 6.28125)
ROUND_MAGIC = 12582912.0
GLA_CHUNK = 64

C_ONES, C_IDENT, C_PAIR, C_GLA, C_CAUSAL, C_CHUNKMASK, C_SWAP, C_RESET, C_LT, C_INV = (
    0, 256, 384, 512, 640, 1024, 1408, 1536, 1792, 1856)
C_COLS = 1857

PACK1 = dict(ada_b=0, norm_mix=48, norm_ffn=56, conv_w=64, conv_b=80, ba=84, bx=88, lam=92, bg=96,
             gla_g=98, final=99)
PACK1_ROWS = 107
PACK2 = dict(ada_b=0, norm_mix=48, norm_ffn=56, q_norm=64, kv_norm=67, conv_w=69, conv_b=101,
             head_norm=109, final=113)
PACK2_ROWS = 121
FFN_FB = DFF // P
PACKF_ROWS = 4 * FFN_FB


SEMAPHORES = """
ada_done ada_used ang atok_psum attT_psum attT_sb att_exp att_max att_norm att_psum att_y b_ready
c8_ready c_act conv1 conv2 conv_a conv_last conv_v cq_sb cq_sq cqn cqstd cqsum_psum down_done em_row
exps_sb flow_sb g_ready gated gatesT_psum gatesT_sb gates_sb gbc_psum gbc_ready gelu_done gelu_sb
gm_sb h_ready hm_ready hsq_sb hstd hsum_psum k_sb kend_psum kend_sb kn_sb kr_sb krot_psum krot_sb
kt_sb lf_abs lf_exp lgt_exp m_rows mb_psum mod_psum mult_sb norm_mul norm_sq norm_std norm_sum
num_psum o_psum om_sb osq_sb ostd_sb osum_psum outT_psum out_sb params q_sb qkm_sb qn_sb qr_sb
qrot_psum qrot_sb rgchain_a rgchain_m rgchain_s ri_psum rope_ready router_psum s_psum sc_sb
scores_psum silu_done silug_sb sp_exp states_sb stored sw_ready u_ready units_used up_done upd_psum
v_sb va_sb vcol_psum vcol_ready vm_sb w_arg w_exp wout_psum x_psum x_ready ycat_ready yla_sb
yml_ready z_br z_cq z_flow z_g z_gate z_gm z_if z_k z_kr z_logf z_om z_q z_qm z_rgx z_ukn z_ukv
z_uqn z_uqr z_v z_vm zeroed
"""

F0 = {"dense": 0, "moe": FFN_FB, "conv0": FFN_FB * (1 + EXPERTS), "conv1": FFN_FB * (2 + EXPERTS)}

INPUTS = """
x c ada_w ada_b norm_mix_g norm_ffn_g w_in rg_conv_w rg_conv_b rg_wa rg_ba rg_wx rg_bx rg_lambda gla_wg2
gla_bg gla_norm_g w_out ffn_w1 ffn_w3 ffn_w2 router_w moe_w1 moe_w3 moe_w2 final_g c_2 positions_2 ada_w_2
ada_b_2 norm_mix_w_2 w_in_2 q_norm_w_2 kv_norm_w_2 w_uq_2 w_ukv_2 mlstm_conv_w_2 mlstm_conv_b_2
mlstm_gate_b_2 mlstm_head_norm_w_2 w_br_mla_2 w_br_mlstm_2 w_out_2 norm_ffn_w_2 ffn_w_up_2 ffn_conv_w_2
ffn_conv_b_2 ffn_w_down_2 final_norm_w_2
""".split()


GATE_ROWS = ("fb", "lf", "b", "a", "m", "mm", "em")


def constants():
    c = np.zeros((P, C_COLS), np.float32)
    r = np.arange(P)
    c[:, C_ONES:C_ONES + 256] = 1.0
    c[:, C_IDENT:C_IDENT + P] = np.eye(P)
    c[:, C_PAIR:C_PAIR + P] = (r[:, None] // 64) == (r[None, :] // 64)
    same = (r[:, None] // GLA_CHUNK) == (r[None, :] // GLA_CHUNK)
    c[:, C_GLA:C_GLA + P] = same & (r[:, None] <= r[None, :])
    tri = (r[:, None] <= r[None, :]).astype(np.float32)
    c[:, C_CAUSAL:C_CAUSAL + 384] = np.concatenate([tri, np.ones((P, P), np.float32), tri], 1)
    late = np.where((r[:, None] < 64) & (r[None, :] >= 64), BIG_NEG, 0.0)
    c[:, C_CHUNKMASK:C_CHUNKMASK + 384] = np.concatenate([late, np.zeros((P, P)), late], 1)
    half = r % 32
    for out in range(P):
        src = out + 16 if half[out] < 16 else out - 16
        c[src, C_SWAP + out] = -1.0 if half[out] < 16 else 1.0
    c[:, C_RESET:C_RESET + 256] = (np.arange(T) % GLA_CHUNK != 0)
    e, j = np.divmod(np.arange(64), 8)
    c[:, C_LT:C_LT + 64] = j < e
    c[:, C_INV] = np.float32(ROPE_THETA) ** (-(r % 16).astype(np.float32) / np.float32(16))
    sel = np.zeros((8, 8 * P + 4 * P), np.float32)
    for h in range(8):
        sel[h, h * P:(h + 1) * P] = 1.0
        sel[h, 8 * P + h * 64:8 * P + (h + 1) * 64] = 1.0
    return c, sel


def unit_plan():
    order = []
    for li in range(2):
        order += [("rgx", li, j) for j in range(2)] + [("flow", li, 0), ("q", li, 0), ("k", li, 0)]
        order += [("v", li, j) for j in range(2)] + [("gate", li, j) for j in range(2)]
        order += [("g", li, j) for j in range(2)] + [("wout", li, j) for j in range(4)]
        if li == 0:
            order += [(w, 0, c) for c in range(CHUNKS) for w in ("w1", "w3", "w2")]
        else:
            order += ["loop"]
    for li in range(2):
        order += [("kr", li, 0), ("cq", li, 0), ("cq", li, 1), ("ckv", li, 0), ("if", li, 0)]
        order += [("qm", li, 0), ("qm", li, 1), ("km", li, 0), ("km", li, 1)]
        order += [("uqn", li, 0), ("uqr", li, 0), ("ukv", li, 0)]
        order += [("vm", li, 0), ("vm", li, 1), ("om", li, 0), ("om", li, 1)]
        order += [("gmla", li, j) for j in range(4)] + [("gml", li, j) for j in range(4)]
        order += [("brmla", li, j) for j in range(2)] + [("brml", li, j) for j in range(2)]
        order += [("wout2", li, j) for j in range(4)]
        order += [(w, li, c) for c in range(CHUNKS) for w in ("u1", "u3", "u2")]
    pos, count, plan, loop = 0, [0] * RING, {}, None
    for key in order:
        if key == "loop":
            pad = -pos % RING
            loop = (pos, pos + pad, list(count))
            pos += pad + 3 * CHUNKS * EXPERTS
            count = [n + 3 * CHUNKS * EXPERTS // RING for n in count]
            continue
        parts = {"kr": 4, "if": 2, "uqn": 3, "uqr": 12, "ukv": 4}.get(key[0], 1)
        count[pos % RING] += parts
        plan[key] = (pos % RING, count[pos % RING], pos)
        pos += 1
    return order, plan, loop


def two_blocks(nc, d, out):
    order, plan, (pos_before_loop, loop_pos, loop_count) = unit_plan()
    PAIR_ITERS = CHUNKS * EXPERTS // 2
    FB_MOE = 2 * FFN_FB // 2

    ctx = ExitStack()
    with ctx:
        def sb(name, shape, dt=F32):
            return ctx.enter_context(nc.sbuf_tensor(name, shape, dt))

        def sem(name):
            return ctx.enter_context(nc.semaphore(name))

        ring = sb("ring", [P, RING, SLOT])
        ada_acc = sb("ada_acc", [P, ADA_SLOTS, SLOT])
        ada_in = sb("ada_in", [P, ADA_SLOTS, SLOT])
        x = sb("x", [P, KB, T])
        h = sb("h", [P, KB, T])
        const = sb("const", [P, C_COLS])
        sel = sb("sel", [8, 12 * P])
        vcol = sb("vcol", [P, 8, P])
        gate_w = sb("gate_w", [P, 2, 2, 4, P])
        wg2 = sb("wg2", [16, 2, T])
        router = sb("router", [P, KB, EXPERTS])
        gate_b = sb("gate_b", [8, 2, 2])
        c_col = sb("c_col", [P, 2, KB])
        mod = sb("mod", [P, MODS])
        scale_a = sb("scale_a", [P, 2, KB])
        small = sb("small", [P, 256])
        rope_cos = sb("rope_cos", [P, T])
        rope_sin = sb("rope_sin", [P, T])
        arena = sb("arena", [P, 13856])
        gate_rows = sb("gate_rows", [8, len(GATE_ROWS), T])
        bank = [ctx.enter_context(nc.psum_tensor(f"bank{i}", [P, 512], F32)) for i in range(8)]

        def region(start, cols):
            return arena[:, start:start + cols]

        ones = const[:, C_ONES:C_ONES + P]
        ident = const[:, C_IDENT:C_IDENT + P]

        names = SEMAPHORES.split()
        s = {n: sem(n) for n in names}
        slot_full = [sem(f"slot_full{i}") for i in range(RING)]
        ada_full = [sem(f"ada_full{i}") for i in range(ADA_SLOTS)]
        bank_free = [sem(f"bank_free{i}") for i in range(8)]
        act_chain, dve_chain = sem("act_chain"), sem("dve_chain")

        def rows(w):
            return w.rearrange("(k p) f -> p k f", p=P)

        win1 = [rows(d["w_in"][li]) for li in range(2)]
        win2 = [rows(d["w_in_2"][li]) for li in range(2)]
        cols1 = dict(rgx=0, gate=512, q=1024, k=1280, v=1536, g=2048, flow=2560)
        cols2 = dict(cq=0, ckv=384, kr=640, qm=672, km=1184, vm=1696, om=2208, gmla=2736, gml=3760)

        def slot_view(key, kbs, width):
            sl = ring[:, plan[key][0], 0:kbs * width]
            return sl.rearrange("p (k f) -> p k f", k=kbs)

        def ffn_src(names3, li, c):
            w1, w3, w2 = names3
            cs = slice(c * CHUNK_COLS, (c + 1) * CHUNK_COLS)
            return (rows(w1)[:, :, cs], rows(w3)[:, :, cs], rows(w2[cs, :]))

        M1 = {n: region(*v) for n, v in dict(
            u=(0, 1024), rr=(1024, 1024), ii=(2048, 1024), aa=(3072, 1024), mu=(4096, 1024), gg=(5120, 1024),
            q=(6144, 512), k=(6656, 512), vt=(7168, 1024), bb=(8192, 512), lf=(8704, 512), qloc=(9216, 512),
            kloc=(9728, 512), kend=(10240, 512), qint=(10752, 512), kt=(11264, 512), sc=(11776, 1024),
            st=(12800, 768), flow=(13568, 256), osq=(6144, 1024), ostd=(1024, 1024), on=(9216, 1024),
            silug=(10240, 1024)).items()}
        M2 = {n: region(*v) for n, v in dict(
            cq=(0, 768), ckv=(768, 512), csq=(1280, 1280), rs=(2560, 512), qn=(3072, 1024), qr=(4096, 512),
            qro=(4608, 512), kn=(5120, 1024), kr=(6144, 256), kro=(6400, 256), va=(6656, 1024),
            prob=(7680, 1024), pt=(8704, 768), yla=(9472, 1024), qkm=(10496, 2048), vt2=(12544, 1024),
            wm=(0, 768), sw=(768, 768), om=(1536, 1024), hm=(2560, 1024), hsq=(3584, 1024), hstd=(4608, 1024),
            yml=(5632, 1024), gm1=(6656, 2048), gm2=(10496, 2048), brt=(0, 2048), den=(13568, 256)).items()}
        MF = {n: region(*v) for n, v in dict(
            act=(3072, 512), gates_t=(4096, 256), gbc=(4352, 2048), cv=(6400, 1024)).items()}
        hidden = region(2560, 512).rearrange("p (i t) -> p i t", i=2)

        def grow(name):
            return gate_rows[:, GATE_ROWS.index(name), :]

        def param_loads():
            rows_in = region(0, 8 * P).rearrange("p (k f) -> p k f", k=8)
            loads = [(const[:, :], d["const_table"]), (sel[:, :], d["const_sel"])]

            def pack(i, row, vec):
                n = 1
                for extent in vec.shape:
                    n *= extent
                src = vec.rearrange("(r f) -> r f", f=P) if len(vec.shape) == 1 \
                    else vec.rearrange("t (r f) -> (t r) f", f=P)
                loads.append((rows_in[row:row + n // P, i, :], src))

            for li in range(2):
                for name, key in (("ada_b", "ada_b"), ("norm_mix_g", "norm_mix"), ("norm_ffn_g", "norm_ffn"),
                                  ("rg_conv_w", "conv_w"), ("rg_conv_b", "conv_b"), ("rg_ba", "ba"),
                                  ("rg_bx", "bx"), ("rg_lambda", "lam"), ("gla_bg", "bg"),
                                  ("gla_norm_g", "gla_g")):
                    pack(li, PACK1[key], d[name][li])
                pack(li, PACK1["final"], d["final_g"])
                for name, key in (("ada_b_2", "ada_b"), ("norm_mix_w_2", "norm_mix"),
                                  ("norm_ffn_w_2", "norm_ffn"), ("q_norm_w_2", "q_norm"),
                                  ("kv_norm_w_2", "kv_norm"), ("mlstm_conv_w_2", "conv_w"),
                                  ("mlstm_conv_b_2", "conv_b"), ("mlstm_head_norm_w_2", "head_norm")):
                    pack(2 + li, PACK2[key], d[name][li])
                pack(2 + li, PACK2["final"], d["final_norm_w_2"])
                pack(4 + 2 * li, 0, d["ffn_conv_w_2"][li, 0:2])
                pack(5 + 2 * li, 0, d["ffn_conv_w_2"][li, 2])
                pack(5 + 2 * li, 2 * FFN_FB, d["ffn_conv_b_2"][li])
                pack(4 + li, PACKF_ROWS, d["c" if li == 0 else "c_2"][0])
            loads.append((region(1024, TB * DM).rearrange("p (b f) -> p b f", b=TB),
                          d["x"][0].rearrange("(b p) f -> p b f", p=P)))
            loads.append((region(3072, T).bitcast(I32), d["positions_2"].to_broadcast([P, T])))
            loads.append((router[:, :, :], rows(d["router_w"][0])))
            for li in range(2):
                loads.append((wg2[:, li, :], d["gla_wg2"][li]))
                for n in range(2):
                    loads.append((gate_b[:, li, n:n + 1],
                                  d["mlstm_gate_b_2"][li, 8 * n:8 * n + 8].unsqueeze(1)))
            first_gate = len(loads)
            for li in range(2):
                for g, name in enumerate(("rg_wa", "rg_wx")):
                    for hh in range(2):
                        r = slice(64 * hh, 64 * hh + 64)
                        src = d[name][li].rearrange("(b two) d e -> two d b e", two=2)[hh]
                        loads.append((gate_w[r, li, g, :, r], src))
            return loads, first_gate

        PARAM_LOADS, FIRST_GATE_LOAD = param_loads()
        N_PARAMS = len(PARAM_LOADS)

        block = ctx.enter_context(nc.Block())

        @block.sync
        def _(sp):
            def load(key, dst, src):
                if plan[key][2] >= RING:
                    sp.wait_ge(s["units_used"], plan[key][2] - RING + 1)
                sp.dma_start(dst, src).then_inc(slot_full[plan[key][0]], 16)

            for key in order:
                if key == "loop":
                    w1 = d["moe_w1"][0].rearrange("e (k p) f -> e p k f", p=P)
                    w3 = d["moe_w3"][0].rearrange("e (k p) f -> e p k f", p=P)
                    w2 = d["moe_w2"][0].rearrange("e (c k p) f -> e c p k f", p=P, k=2)
                    with sp.Fori(0, EXPERTS // 2) as pair:
                        with sp.Fori(0, CHUNKS) as c:
                            for j in range(RING):
                                e, w = divmod(j, 3)
                                sp.wait_ge(s["units_used"],
                                           (pair * CHUNKS + c) * RING + (loop_pos + j - RING + 1))
                                if w < 2:
                                    dst = ring[:, j, :].rearrange("p (k f) -> p k f", k=KB)
                                    src = (w1, w3)[w][pair * 2 + e, :, :, bass.ds(c * CHUNK_COLS, CHUNK_COLS)]
                                else:
                                    dst = ring[:, j, :].rearrange("p (k f) -> p k f", k=2)
                                    src = w2[pair * 2 + e, c, :, :, :]
                                sp.dma_start(dst, src).then_inc(slot_full[j], 16)
                    continue
                kind, li, j = key
                if kind == "flow":
                    load(key, slot_view(key, KB, 16), win1[li][:, :, 2560:2576])
                elif kind in cols1:
                    c0 = cols1[kind] + 256 * j
                    load(key, slot_view(key, KB, 256), win1[li][:, :, c0:c0 + 256])
                elif kind in ("wout", "wout2"):
                    w = rows(d["w_out" if kind == "wout" else "w_out_2"][li])
                    load(key, slot_view(key, KB, 256), w[:, :, 256 * j:256 * j + 256])
                elif kind in ("w1", "w3", "w2", "u1", "u3", "u2"):
                    if kind[0] == "w":
                        srcs = ffn_src((d["ffn_w1"][0], d["ffn_w3"][0], d["ffn_w2"][0]), li, j)
                    else:
                        up = d["ffn_w_up_2"][li]
                        srcs = ffn_src((up[:, 0:DFF], up[:, DFF:2 * DFF], d["ffn_w_down_2"][li]), li, j)
                    w = dict(zip("132", range(3)))[kind[1]]
                    load(key, slot_view(key, *((KB, 256) if w < 2 else (2, DM))), srcs[w])
                elif kind == "cq":
                    width = 256 if j == 0 else 128
                    load(key, slot_view(key, KB, width), win2[li][:, :, 256 * j:256 * j + width])
                elif kind == "kr":
                    dst = slot_view(key, KB, P).rearrange("p k (r f) -> p k r f", r=4)
                    for r in range(4):
                        load(key, dst[:, :, r, :], win2[li][:, :, 640:672])
                elif kind == "if":
                    dst = slot_view(key, KB, 16)
                    for n, c0 in enumerate((2720, 2728)):
                        load(key, dst[:, :, 8 * n:8 * n + 8], win2[li][:, :, c0:c0 + 8])
                elif kind in cols2:
                    c0 = cols2[kind] + 256 * j
                    load(key, slot_view(key, KB, 256), win2[li][:, :, c0:c0 + 256])
                elif kind == "uqn":
                    dst = slot_view(key, 3, 512).rearrange("p k (h f) -> p k h f", h=8)
                    src = rows(d["w_uq_2"][li]).rearrange("p k (h f) -> p k h f", h=8)
                    for k in range(3):
                        load(key, dst[:, k], src[:, k, :, 0:64])
                elif kind == "uqr":
                    dst = slot_view(key, 3, 256).rearrange("p k (g c e f) -> p k g c e f", g=2, c=2, e=2)
                    src = rows(d["w_uq_2"][li]).rearrange("p k (g e c f) -> p k g c e f", g=2, c=2, e=2)
                    for k in range(3):
                        for g in range(2):
                            for c in range(2):
                                load(key, dst[:, k, g, c], src[:, k, g, c, :, 64:96])
                elif kind == "ukv":
                    dst = slot_view(key, 2, DM).rearrange("p k (w h f) -> p k w h f", w=2, h=8)
                    src = rows(d["w_ukv_2"][li]).rearrange("p k (h w f) -> p k w h f", h=8, w=2)
                    for k in range(2):
                        for w in range(2):
                            load(key, dst[:, k, w], src[:, k, w])
                elif kind in ("brmla", "brml"):
                    w = rows(d["w_br_mla_2" if kind == "brmla" else "w_br_mlstm_2"][li])
                    load(key, slot_view(key, 4, 512), w[:, :, 512 * j:512 * j + 512])
            for tb in range(TB):
                sp.wait_ge(s["out_sb"], 2 * (tb + 1))
                sp.dma_start(out[0, tb * P:(tb + 1) * P, :], region(2560 + tb * DM, DM)).then_inc(s["stored"], 16)
            sp.wait_ge(s["stored"], 16 * TB)

        @block.gpsimd
        def _(pool):
            nc.gpsimd.memset(gate_w[:, :, :, :, :], 0.0).then_inc(s["zeroed"], 1)
            for n in range(4 * ADA_PER_LAYER):
                layer, piece = divmod(n, ADA_PER_LAYER)
                kb, j = divmod(piece, ADA_SLOTS)
                if n >= ADA_SLOTS:
                    pool.wait_ge(s["ada_used"], n - ADA_SLOTS + 1)
                w = d["ada_w" if layer < 2 else "ada_w_2"][layer % 2]
                pool.dma_start(ada_in[:, j, :], w[kb * P:(kb + 1) * P, j * SLOT:(j + 1) * SLOT])\
                    .then_inc(ada_full[j], 16)

        @block.tensor
        def _(pe):
            got = Counter()
            fills = Counter()
            owed = []

            def need(name, n=1):
                got[name] += n
                pe.wait_ge(s[name], got[name])

            def fill(b, readers=1):
                if fills[b]:
                    pe.wait_ge(bank_free[b], fills[b])
                fills[b] += readers

            def mm(out, lhsT, rhs, start=True, stop=True, inc=None, shared=False):
                ins = nc.tensor.matmul(out, lhsT, rhs, start=start, stop=stop, skip_group_check=shared)
                if inc is not None:
                    ins.then_inc(s[inc], 1)
                elif owed:
                    ins.then_inc(s["units_used"], owed.pop())
                return ins

            def arrive(key):
                slot, count, _ = plan[key]
                pe.wait_ge(slot_full[slot], 16 * count)

            def project(key, b, kbs, moving, blocks, width=256, col=0, per_kb=None, inc=None):
                arrive(key)
                w = slot_view(key, kbs, width)
                for i in range(blocks):
                    m = min(P, width - i * P)
                    for kb in range(kbs):
                        if per_kb and i == 0:
                            need(per_kb)
                        last = i == blocks - 1 and kb == kbs - 1
                        mm(bank[b][0:m, col + i * T:col + (i + 1) * T], w[:, kb, i * P:i * P + m], moving(kb),
                           start=(kb == 0), stop=(kb == kbs - 1), inc=inc if last else None)
                owed.append(1)

            def project_tokens(kind, li, banks, inc):
                for b in banks:
                    fill(b)
                for j in range(2):
                    arrive((kind, li, j))
                    w = slot_view((kind, li, j), KB, 256)
                    for tb, b in enumerate(banks):
                        for kb in range(KB):
                            last = j == 1 and tb == TB - 1 and kb == KB - 1
                            mm(bank[b][:, j * 256:(j + 1) * 256], h[:, kb, tb * P:(tb + 1) * P], w[:, kb, :],
                               start=(kb == 0), stop=(kb == KB - 1), inc=inc if last else None)
                    owed.append(1)

            def hk(kb):
                return h[:, kb, :]

            def norm_sum():
                need("norm_sq")
                fill(7)
                sq = region(0, KB * T).rearrange("p (k t) -> p k t", k=KB)
                for kb in range(KB):
                    mm(bank[7][:, 0:T], ones, sq[:, kb, :], start=(kb == 0), stop=(kb == KB - 1),
                       inc="norm_sum" if kb == KB - 1 else None)

            def modulation():
                need("ada_done")
                fill(0)
                for j in range(MODS):
                    piece, c = divmod(j * P, SLOT)
                    mm(bank[0][:, j:j + 1], ada_acc[:, piece, c:c + P], ones[:, 0:1],
                       inc="mod_psum" if j == MODS - 1 else None)

            def start():
                pe.wait_ge(s["params"], 16 * N_PARAMS)
                rows_in = region(0, 8 * P).rearrange("p (k f) -> p k f", k=8)
                sizes = [PACK1_ROWS] * 2 + [PACK2_ROWS] * 2 + [PACKF_ROWS + KB] * 2 + [PACKF_ROWS] * 2
                for i, n in enumerate(sizes):
                    b = i // 4
                    if i % 4 == 0:
                        fill(b)
                    ins = nc.tensor.transpose(bank[b][:, (i % 4) * P:(i % 4) * P + n], rows_in[0:n, i, :],
                                              ident[0:n, 0:n])
                ins.then_inc(s["vcol_psum"], 1)
                xt = region(1024, TB * DM).rearrange("p (b f) -> p b f", b=TB)
                for g in range(4):
                    fill(2 + g)
                    for k in range(2):
                        for tb in range(TB):
                            kb = 2 * g + k
                            ins = nc.tensor.transpose(bank[2 + g][:, k * T + tb * P:k * T + (tb + 1) * P],
                                                      xt[:, tb, kb * P:(kb + 1) * P], ident)
                    ins.then_inc(s["x_psum"], 1)

            def mixer1(li):
                project_bank(("rgx", li, 0), 0, "z_rgx", per_kb="h_ready")
                project_bank(("rgx", li, 1), 1, "z_rgx")
                fill(2)
                project(("flow", li, 0), 2, KB, hk, 1, width=16, inc="z_flow")
                project_bank(("q", li, 0), 3, "z_q")
                project_bank(("k", li, 0), 5, "z_k")
                need("flow_sb")
                fill(4)
                for b2 in range(2):
                    mm(bank[4][:, b2 * T:(b2 + 1) * T], wg2[:, li, b2 * P:(b2 + 1) * P], M1["flow"][0:16, :],
                       inc="z_logf" if b2 else None)
                project_tokens("v", li, (6, 7), "z_v")
                need("u_ready")
                u = M1["u"].rearrange("p (b t) -> p b t", b=4)
                for g, banks in enumerate(((0, 1), (2, 3))):
                    for b4 in range(4):
                        if b4 % 2 == 0:
                            fill(banks[b4 // 2])
                        mm(bank[banks[b4 // 2]][:, (b4 % 2) * T:(b4 % 2 + 1) * T], gate_w[:, li, g, b4, :],
                           u[:, b4, :], inc="ri_psum" if b4 % 2 else None)
                project_bank(("gate", li, 0), 5, "z_gate")
                project_bank(("gate", li, 1), 4, "z_gate")
                need("kend_sb")
                fill(6)
                kend = M1["kend"].rearrange("p (b t) -> p b t", b=2)
                for tb in range(TB):
                    for pair in range(2):
                        ins = nc.tensor.transpose(bank[6][:, tb * 256 + pair * P:tb * 256 + (pair + 1) * P],
                                                  kend[:, pair, tb * P:(tb + 1) * P], ident)
                ins.then_inc(s["kend_psum"], 1)
                need("k_sb")
                qloc = M1["qloc"].rearrange("p (b t) -> p b t", b=2)
                kloc = M1["kloc"].rearrange("p (b t) -> p b t", b=2)
                for hh, b in enumerate((7, 0)):
                    fill(b)
                    r = slice(64 * hh, 64 * hh + 64)
                    for i in range(4):
                        pair, tb = divmod(i, 2)
                        mm(bank[b][:, i * P:(i + 1) * P], kloc[r, pair, tb * P:(tb + 1) * P],
                           qloc[r, pair, tb * P:(tb + 1) * P], inc="scores_psum" if i == 3 else None)
                need("kt_sb")
                need("v_sb")
                kt = M1["kt"].rearrange("p (b f) -> p b f", b=TB)
                vt = M1["vt"].rearrange("p (b f) -> p b f", b=TB)
                for n, b in enumerate((1, 2, 3)):
                    fill(b)
                    r = slice(64 * (n % 2), 64 * (n % 2) + 64)
                    for pair in range(2):
                        mm(bank[b][:, pair * 256:(pair + 1) * 256], kt[r, n // 2, pair * P:(pair + 1) * P],
                           vt[r, n // 2, pair * 256:(pair + 1) * 256], inc="upd_psum" if pair else None)
                project_bank(("g", li, 0), 5, "z_g")
                project_bank(("g", li, 1), 4, "z_g")
                need("sc_sb", 2)
                need("states_sb")
                sc = M1["sc"].rearrange("p (i q) -> p i q", i=8)
                st = M1["st"].rearrange("p (n b v) -> p n b v", n=3, b=2)
                qint = M1["qint"].rearrange("p (b t) -> p b t", b=2)
                for hh, b in enumerate((6, 7)):
                    fill(b)
                    r = slice(64 * hh, 64 * hh + 64)
                    for pair in range(2):
                        head = 2 * pair + hh
                        for tb in range(TB):
                            c0 = pair * T + tb * P
                            mm(bank[b][:, c0:c0 + P], vt[:, tb, head * P:(head + 1) * P],
                               sc[:, hh * 4 + pair * 2 + tb, :], start=(pair == 0 and tb == 0), stop=True,
                               shared=True)
                        for n in range(1, 4):
                            c0 = pair * T + n * GLA_CHUNK
                            mm(bank[b][:, c0:c0 + GLA_CHUNK], st[r, n - 1, pair, :],
                               qint[r, pair, n * GLA_CHUNK:(n + 1) * GLA_CHUNK], start=False, stop=True,
                               shared=True, inc="o_psum" if pair and n == 3 else None)
                need("osq_sb", 2)
                for half in range(2):
                    fill(half)
                    mm(bank[half][:, :], ones, M1["osq"][:, half * 512:(half + 1) * 512], inc="osum_psum")
                project_out("wout", li, (2, 3, 5, 4))

            def project_bank(key, b, inc, per_kb=None, readers=1):
                fill(b, readers)
                project(key, b, KB, hk, 2, per_kb=per_kb, inc=inc)

            def project_out(kind, li, banks):
                need("ycat_ready")
                for j, b in enumerate(banks):
                    fill(b)
                    project((kind, li, j), b, KB, hk, 2, inc="wout_psum")

            def mixer2(li):
                fill(3)
                project(("kr", li, 0), 3, KB, hk, 1, width=P, per_kb="h_ready", inc="z_kr")
                project_bank(("cq", li, 0), 0, "z_cq")
                fill(1)
                project(("cq", li, 1), 1, KB, hk, 1, width=P, inc="z_cq")
                project_bank(("ckv", li, 0), 2, "z_cq")
                fill(4)
                arrive(("if", li, 0))
                w = slot_view(("if", li, 0), KB, 16)
                for n in range(2):
                    for kb in range(KB):
                        mm(bank[4][0:8, n * T:(n + 1) * T], w[:, kb, 8 * n:8 * n + 8], hk(kb), start=(kb == 0),
                           stop=(kb == KB - 1), inc="z_if" if n and kb == KB - 1 else None)
                owed.append(1)
                project_bank(("qm", li, 0), 5, "z_qm")
                project_bank(("qm", li, 1), 6, "z_qm")
                project_bank(("km", li, 0), 7, "z_qm")
                need("cq_sq")
                fill(0)
                csq = M2["csq"].rearrange("p (b t) -> p b t", b=5)
                for b5 in range(5):
                    c0 = 0 if b5 < 3 else T
                    mm(bank[0][:, c0:c0 + T], ones, csq[:, b5, :], start=b5 in (0, 3), stop=b5 in (2, 4),
                       inc="cqsum_psum" if b5 == 4 else None)
                need("kr_sb")
                fill(1)
                mm(bank[1][:, 0:T], const[:, C_SWAP:C_SWAP + P], M2["kr"], inc="krot_psum")
                project_bank(("km", li, 1), 3, "z_qm")
                need("cqn")
                cq = M2["cq"].rearrange("p (b t) -> p b t", b=3)
                ckv = M2["ckv"].rearrange("p (b t) -> p b t", b=2)
                arrive(("uqn", li, 0))
                wn = slot_view(("uqn", li, 0), 3, 512)
                for pair in range(4):
                    b = (2, 4)[pair // 2]
                    if pair % 2 == 0:
                        fill(b)
                    for kb in range(3):
                        mm(bank[b][:, (pair % 2) * T:(pair % 2 + 1) * T], wn[:, kb, pair * P:(pair + 1) * P],
                           cq[:, kb, :], start=(kb == 0), stop=(kb == 2),
                           inc="z_uqn" if pair % 2 and kb == 2 else None)
                owed.append(1)
                arrive(("uqr", li, 0))
                wr = slot_view(("uqr", li, 0), 3, 256)
                fill(5)
                for g in range(2):
                    for kb in range(3):
                        mm(bank[5][:, g * T:(g + 1) * T], wr[:, kb, g * P:(g + 1) * P], cq[:, kb, :],
                           start=(kb == 0), stop=(kb == 2), inc="z_uqr" if g and kb == 2 else None)
                owed.append(1)
                arrive(("ukv", li, 0))
                wk = slot_view(("ukv", li, 0), 2, DM)
                for pair in range(4):
                    b = (6, 7)[pair // 2]
                    if pair % 2 == 0:
                        fill(b)
                    for kb in range(2):
                        mm(bank[b][:, (pair % 2) * T:(pair % 2 + 1) * T], wk[:, kb, pair * P:(pair + 1) * P],
                           ckv[:, kb, :], start=(kb == 0), stop=(kb == 1),
                           inc="z_ukn" if pair % 2 and kb == 1 else None)
                for tb in range(TB):
                    b = (0, 1)[tb]
                    fill(b)
                    for kb in range(2):
                        mm(bank[b][:, :], ckv[:, kb, tb * P:(tb + 1) * P], wk[:, kb, 512:1024],
                           start=(kb == 0), stop=(kb == 1), inc="z_ukv" if kb == 1 else None)
                owed.append(1)
                need("qr_sb")
                fill(3)
                mm(bank[3][:, :], const[:, C_SWAP:C_SWAP + P], M2["qr"], inc="qrot_psum")
                project_tokens("vm", li, (2, 4), "z_vm")
                project_bank(("om", li, 0), 5, "z_om")
                project_bank(("om", li, 1), 6, "z_om")

                need("qrot_sb")
                need("krot_sb")
                need("qn_sb", 2)
                need("kn_sb", 2)
                need("va_sb", 2)
                qn = M2["qn"].rearrange("p (b t) -> p b t", b=4)
                kn = M2["kn"].rearrange("p (b t) -> p b t", b=4)
                qro = M2["qro"].rearrange("p (b t) -> p b t", b=2)
                kro = M2["kro"]
                va = M2["va"].rearrange("p (b f) -> p b f", b=TB)

                def scores(head):
                    b = head % 2
                    fill(b)
                    r = slice(64 * (head % 2), 64 * (head % 2) + 64)
                    row = 64 * (head % 2) + 32 * (head % 4 // 2)
                    rr = slice(row, row + 32)
                    for qb in range(TB):
                        c0, keys = (0, P) if qb == 0 else (P, T)
                        mm(bank[b][:, c0:c0 + keys], qn[r, head // 2, qb * P:(qb + 1) * P],
                           kn[r, head // 2, 0:keys], start=(qb == 0), stop=False, shared=True)
                        mm(bank[b][:, c0:c0 + keys], qro[rr, head // 4, qb * P:(qb + 1) * P], kro[rr, 0:keys],
                           start=False, stop=True, shared=True, inc="att_psum" if qb else None)

                def weighted(head):
                    b = 3 if head % 2 else 7
                    fill(b)
                    need("att_norm")
                    prob = M2["prob"][:, (head % 2) * 512:(head % 2) * 512 + 384]
                    for i in range(3):
                        ins = nc.tensor.transpose(bank[b][:, i * P:(i + 1) * P], prob[:, i * P:(i + 1) * P], ident)
                    ins.then_inc(s["attT_psum"], 1)

                def values(head):
                    b = (2, 4)[(head // 2) % 2]
                    if head % 2 == 0:
                        fill(b)
                    need("attT_sb")
                    pt = M2["pt"][:, (head % 2) * 384:(head % 2) * 384 + 384]
                    r = slice(64 * (head % 2), 64 * (head % 2) + 64)
                    hv = slice(head * 64, head * 64 + 64)
                    mm(bank[b][r, 0:P], va[:, 0, hv], pt[:, 0:P], start=True, stop=True, shared=True)
                    mm(bank[b][r, P:T], va[:, 0, hv], pt[:, P:T], start=False, stop=False, shared=True)
                    mm(bank[b][r, P:T], va[:, 1, hv], pt[:, T:384], start=False, stop=True, shared=True,
                       inc="att_y" if head % 2 else None)

                for step in range(10):
                    if step < 8:
                        scores(step)
                    if 1 <= step < 9:
                        weighted(step - 1)
                    if step >= 2:
                        values(step - 2)

                need("m_rows")
                fill(5)
                for tb in range(TB):
                    ins = nc.tensor.transpose(bank[5][:, tb * 8:tb * 8 + 8], grow("a")[:, tb * P:(tb + 1) * P],
                                              ident[0:8, 0:8])
                ins.then_inc(s["atok_psum"], 1)
                need("vm_sb", 2)
                need("qkm_sb", 4)
                need("em_row")
                qk = M2["qkm"].rearrange("p (b t) -> p b t", b=8)
                vt = M2["vt2"].rearrange("p (b f) -> p b f", b=TB)

                def log_weights(head):
                    b = head % 2
                    fill(b)
                    for c0, t0 in ((0, 0), (T, P)):
                        mm(bank[b][:, c0:c0 + T - t0], sel[:, head * P:(head + 1) * P], grow("m")[:, t0:T],
                           inc="mb_psum" if t0 else None)

                def products(head):
                    b = 6 if head % 2 else 7
                    fill(b)
                    r = slice(64 * (head % 2), 64 * (head % 2) + 64)
                    mm(bank[b][:, 0:T], qk[r, 4 + head // 2, 0:P], qk[r, head // 2, :])
                    mm(bank[b][:, T:384], qk[r, 4 + head // 2, P:T], qk[r, head // 2, P:T], inc="s_psum")

                def combine(head):
                    b = (2, 4)[(head // 2) % 2]
                    be = (3, 5)[(head // 2) % 2]
                    if head % 2 == 0:
                        fill(b)
                        fill(be)
                        pair = head // 2
                        mm(bank[be][:, 0:T], sel[:, 8 * P + pair * P:8 * P + (pair + 1) * P], grow("em"))
                    need("sw_ready")
                    sw = M2["sw"][:, (head % 2) * 384:(head % 2) * 384 + 384]
                    r = slice(64 * (head % 2), 64 * (head % 2) + 64)
                    for c0, lhs in ((0, lambda tb: vt[:, tb, head * 64:head * 64 + 64]),
                                    (T, lambda tb: ones[:, 0:64])):
                        mm(bank[b][r, c0:c0 + T], lhs(0), sw[:, 0:T], start=(c0 == 0), stop=False, shared=True)
                        mm(bank[b][r, c0 + P:c0 + T], lhs(1), sw[:, T:384], start=False, stop=True, shared=True,
                           inc="num_psum" if c0 else None)

                for step in range(9):
                    if step < 8:
                        log_weights(step)
                        products(step)
                    if step >= 1:
                        combine(step - 1)
                for j, b in enumerate((0, 1, 6, 7)):
                    project_bank(("gmla", li, j), b, "z_gm")
                need("hsq_sb")
                for half in range(2):
                    b = (2, 4)[half]
                    fill(b)
                    mm(bank[b][:, :], const[:, C_PAIR:C_PAIR + P], M2["hsq"][:, half * 512:(half + 1) * 512],
                       inc="hsum_psum")
                for j, b in enumerate((3, 5, 0, 1)):
                    project_bank(("gml", li, j), b, "z_gm")
                for kind, src, banks in (("brmla", "yla", (2, 4, 6, 7)), ("brml", "yml", (3, 5, 0, 1))):
                    need("yla_sb" if kind == "brmla" else "yml_ready", 4 if kind == "brmla" else 1)
                    y = M2[src].rearrange("p (b t) -> p b t", b=4)
                    for j in range(2):
                        arrive((kind, li, j))
                        w = slot_view((kind, li, j), 4, 512)
                        for i in range(4):
                            b = banks[j * 2 + i // 2]
                            if i % 2 == 0:
                                fill(b)
                            for kb in range(4):
                                mm(bank[b][:, (i % 2) * T:(i % 2 + 1) * T], w[:, kb, i * P:(i + 1) * P], y[:, kb, :],
                                   start=(kb == 0), stop=(kb == 3), inc="z_br" if i % 2 and kb == 3 else None)
                        owed.append(1)
                project_out("wout2", li, (2, 4, 6, 7))

            def up(slots, fb2, b):
                for w in range(2):
                    wv = ring[:, slots[w], :].rearrange("p (k f) -> p k f", k=KB)
                    for kb in range(KB):
                        mm(bank[b + w][:, 0:T], wv[:, kb, fb2 * P:(fb2 + 1) * P], hk(kb), start=(kb == 0),
                           stop=(kb == KB - 1), inc="up_done" if w and kb == KB - 1 else None)

            def down(slot, fb2, g, first, last):
                wv = ring[:, slot, :].rearrange("p (k f) -> p k f", k=2)
                for k in range(KB):
                    mm(bank[4 + k // 2][:, (k % 2) * T:(k % 2 + 1) * T], wv[:, fb2, k * P:(k + 1) * P], g,
                       start=(first and k % 2 == 0), stop=last, shared=True,
                       inc="down_done" if k == KB - 1 else None)

            def ffn(kind, li, f0):
                for b in range(8):
                    fill(b, readers=b // 4)
                need("h_ready", KB)
                for f in range(FFN_FB + 1):
                    if f < FFN_FB:
                        c, fb2 = divmod(f, 2)
                        keys = [(kind + n, li, c) for n in "13"]
                        if fb2 == 0:
                            for key in keys:
                                arrive(key)
                        if f >= 2:
                            pe.wait_ge(s["g_ready"], f0 + f - 1)
                        up([plan[k][0] for k in keys], fb2, 2 * (f % 2))
                        if fb2 == 1:
                            owed.append(2)
                    if f >= 1:
                        c, fb2 = divmod(f - 1, 2)
                        key = (kind + "2", li, c)
                        if fb2 == 0:
                            arrive(key)
                        pe.wait_ge(s["g_ready"], f0 + f)
                        down(plan[key][0], fb2, hidden[:, (f - 1) % 2, :], f == 1, f == FFN_FB)
                        if fb2 == 1:
                            owed.append(1)

            def moe_gates():
                for b in range(8):
                    fill(b, readers=0)
                need("h_ready", KB)
                fill(0)
                for tb in range(TB):
                    for kb in range(KB):
                        mm(bank[0][:, tb * 8:tb * 8 + 8], h[:, kb, tb * P:(tb + 1) * P], router[:, kb, :],
                           start=(kb == 0), stop=(kb == KB - 1),
                           inc="router_psum" if tb and kb == KB - 1 else None)
                need("gates_sb")
                fill(1)
                for tb in range(TB):
                    ins = nc.tensor.transpose(bank[1][0:8, tb * P:(tb + 1) * P], small[:, 64 + tb * 8:72 + tb * 8],
                                              ident)
                ins.then_inc(s["gatesT_psum"], 1)
                need("gatesT_sb")
                for e in range(EXPERTS):
                    if e % 2 == 0:
                        fill(2 + e // 2)
                    mm(bank[2 + e // 2][:, (e % 2) * T:(e % 2 + 1) * T], sel[:, e * P:(e + 1) * P],
                       MF["gates_t"][0:8, :], inc="gbc_psum" if e % 2 else None)
                for b in range(8):
                    fill(b, readers=b // 4)

            def moe(f0):
                slots = ((0, 1, 2), (0, 1, 2), (3, 4, 5), (3, 4, 5))
                if loop_pos > pos_before_loop:
                    owed.append(loop_pos - pos_before_loop)

                def up_j(j, it, base):
                    if j % 2 == 0:
                        for w in range(2):
                            sl = slots[j][w]
                            pe.wait_ge(slot_full[sl], (it + (loop_count[sl] + 1)) * 16)
                    pe.wait_ge(s["g_ready"], it * 4 + (base + j - 1))
                    up(slots[j], j % 2, 2 * (j % 2))
                    if j % 2:
                        owed.append(2)

                def down_j(j, it, base, first=False, last=False):
                    if j % 2 == 0:
                        sl = slots[j][2]
                        pe.wait_ge(slot_full[sl], (it + (loop_count[sl] + 1)) * 16)
                    pe.wait_ge(s["g_ready"], it * 4 + (base + j + 1))
                    down(slots[j][2], j % 2, hidden[:, j % 2, :], first, last)
                    if j % 2:
                        owed.append(1)

                def one_pass(it, base, first=False, last=False):
                    for j in range(4):
                        if j < 3:
                            up_j(j + 1, it, base)
                        elif not last:
                            up_j(0, it + 1, base)
                        down_j(j, it, base, first and j == 0, last and j == 3)

                up_j(0, 0, f0)
                one_pass(0, f0, first=True)
                with pe.Fori(1, PAIR_ITERS - 1) as it:
                    one_pass(it, f0)
                one_pass(PAIR_ITERS - 1, f0, last=True)

            start()
            modulation()
            norm_sum()
            mixer1(0)
            norm_sum()
            ffn("w", 0, 0)
            modulation()
            norm_sum()
            mixer1(1)
            norm_sum()
            moe_gates()
            moe(F0["moe"])
            norm_sum()
            modulation()
            norm_sum()
            mixer2(0)
            norm_sum()
            ffn("u", 0, F0["conv0"])
            modulation()
            norm_sum()
            mixer2(1)
            norm_sum()
            ffn("u", 1, F0["conv1"])
            norm_sum()
            pe.wait_ge(s["x_ready"], 11 * KB)
            for tb in range(TB):
                for g in range(2):
                    b = tb * 2 + g
                    fill(b)
                    for k in range(4):
                        ins = nc.tensor.transpose(bank[b][:, k * P:(k + 1) * P],
                                                  x[:, 4 * g + k, tb * P:(tb + 1) * P], ident)
                    ins.then_inc(s["outT_psum"], 1)

        @block.scalar
        def _(act):
            got = Counter()
            chain = Counter()

            def need(name, n=1):
                got[name] += n
                act.wait_ge(s[name], got[name])

            def settle(ins):
                chain["act"] += 1
                ins.then_inc(act_chain, 1)
                act.wait_ge(act_chain, chain["act"])

            def tell(ins, name, *banks):
                settle(ins)
                if name:
                    act.sem_inc(s[name], 1)
                for b in banks:
                    act.sem_inc(bank_free[b], 1)

            def func(out, in_, f, **kw):
                return nc.scalar.activation(out, in_, f, **kw)

            def start():
                for n, (dst, src) in enumerate(PARAM_LOADS):
                    if n == FIRST_GATE_LOAD:
                        act.wait_ge(s["zeroed"], 1)
                    act.dma_start(dst, src).then_inc(s["params"], 16)
                act.wait_ge(s["params"], 16 * N_PARAMS)
                need("vcol_ready")
                tell(func(c_col[:, :, :], vcol[:, 4:6, PACKF_ROWS:PACKF_ROWS + KB], ACT.Silu), "c_act")
                need("ang", 2)
                func(rope_sin[:, :], region(3328, T), ACT.Sin)
                settle(func(rope_cos[:, :], region(3584, T), ACT.Sin))
                act.sem_inc(s["rope_ready"], 1)

            def norm(biases):
                need("x_ready", KB)
                sq = region(0, KB * T)
                tell(func(sq, x[:, :, :].rearrange("p k t -> p (k t)"), ACT.Square), "norm_sq")
                need("norm_sum")
                tell(func(region(2304, T), bank[7][:, 0:T], ACT.Sqrt, scale=1.0 / DM, bias=EPS), "norm_std", 7)
                if biases is not None:
                    for kb in range(KB):
                        need("norm_mul")
                        func(h[:, kb, :], h[:, kb, :], ACT.Identity,
                             bias=mod[:, biases + kb:biases + kb + 1]).then_inc(s["h_ready"], 1)

            def mixer1(li):
                v = vcol[:, li, :]
                u = M1["u"].rearrange("p (b t) -> p b t", b=4)
                for g in range(2):
                    need("z_rgx")
                    for i in range(2):
                        b4 = 2 * g + i
                        ins = func(u[:, b4, :], bank[g][:, i * T:(i + 1) * T], ACT.Identity,
                                   scale=v[:, PACK1["conv_w"] + 12 + b4:PACK1["conv_w"] + 13 + b4],
                                   bias=v[:, PACK1["conv_b"] + b4:PACK1["conv_b"] + b4 + 1])
                    tell(ins, "conv1")
                need("z_flow")
                tell(func(M1["flow"][0:16, :], bank[2][0:16, 0:T], ACT.Copy), "flow_sb", 2)
                need("z_q")
                tell(func(M1["q"], bank[3][:, :], ACT.Copy, scale=0.125), "q_sb", 3)
                need("lf_abs")
                settle(func(M1["lf"], M1["lf"], ACT.Exp, scale=-1.0))
                tell(func(M1["lf"], M1["lf"], ACT.Ln, bias=1.0), "lf_exp")
                need("z_v")
                for tb in range(TB):
                    settle(func(M1["vt"][:, tb * 512:(tb + 1) * 512], bank[6 + tb][:, :], ACT.Copy))
                    act.sem_inc(bank_free[6 + tb], 1)
                act.sem_inc(s["v_sb"], 1)
                need("c8_ready")
                settle(func(small[:, 4:8], small[:, 4:8], ACT.Exp, scale=-1.0))
                tell(func(small[:, 4:8], small[:, 4:8], ACT.Ln, bias=1.0), "sp_exp")
                need("b_ready")
                func(M1["kloc"], M1["qloc"], ACT.Exp, scale=-1.0)
                settle(func(M1["kend"], M1["kend"], ACT.Exp))
                settle(func(M1["qloc"], M1["qloc"], ACT.Exp))
                func(M1["qint"], M1["bb"], ACT.Exp)
                bb = M1["bb"].rearrange("p (c t) -> p c t", t=GLA_CHUNK)
                tell(func(small[:, 16:24], bb[:, :, GLA_CHUNK - 1], ACT.Exp), "exps_sb")
                rr = M1["rr"].rearrange("p (b t) -> p b t", b=4)
                ii = M1["ii"].rearrange("p (b t) -> p b t", b=4)
                for g, (dst, bias) in enumerate(((rr, "ba"), (ii, "bx"))):
                    for half in range(2):
                        need("ri_psum")
                        b = 2 * g + half
                        for i in range(2):
                            b4 = 2 * half + i
                            ins = func(dst[:, b4, :], bank[b][:, i * T:(i + 1) * T], ACT.Sigmoid,
                                       bias=v[:, PACK1[bias] + b4:PACK1[bias] + b4 + 1])
                        tell(ins, None, b)
                need("rgchain_a")
                aa = M1["aa"].rearrange("p (b t) -> p b t", b=4)
                mu = M1["mu"].rearrange("p (b t) -> p b t", b=4)
                for b4 in range(4):
                    func(aa[:, b4, :], rr[:, b4, :], ACT.Exp, scale=small[:, 8 + b4:9 + b4])
                for b4 in range(4):
                    ins = func(mu[:, b4, :], rr[:, b4, :], ACT.Tanh, scale=small[:, 12 + b4:13 + b4])
                tell(ins, "rgchain_m")
                need("rgchain_s")
                tell(func(M1["mu"], M1["mu"], ACT.Sqrt), "mult_sb")
                need("kend_psum")
                tell(func(M1["kt"], bank[6][:, :], ACT.Copy), "kt_sb", 6)
                for half, b in enumerate((5, 4)):
                    need("z_gate")
                    tell(func(M1["gg"][:, half * 512:(half + 1) * 512], bank[b][:, :], ACT.Gelu_apprx_tanh),
                         "gelu_sb", b)
                for half in range(2):
                    need("o_psum")
                    tell(func(M1["osq"][:, half * 512:(half + 1) * 512], bank[6 + half][:, :], ACT.Square),
                         "osq_sb")
                for half, b in enumerate((5, 4)):
                    need("z_g")
                    tell(func(M1["silug"][:, half * 512:(half + 1) * 512], bank[b][:, :], ACT.Silu),
                         "silug_sb", b)
                for half in range(2):
                    need("osum_psum")
                    tell(func(M1["ostd"][:, half * 512:(half + 1) * 512], bank[half][:, :], ACT.Sqrt,
                              scale=1.0 / P, bias=EPS), "ostd_sb", half)

            def mixer2(li):
                v = vcol[:, 2 + li, :]
                need("z_kr")
                tell(func(M2["kr"], bank[3][:, 0:T], ACT.Copy), "kr_sb", 3)
                need("cq_sb", 3)
                tell(func(M2["csq"], region(0, 1280), ACT.Square), "cq_sq")
                need("lf_abs")
                settle(func(grow("lf"), grow("lf"), ACT.Exp, scale=-1.0))
                tell(func(grow("lf"), grow("lf"), ACT.Ln, bias=1.0), "lf_exp")
                qk = M2["qkm"].rearrange("p (b t) -> p b t", b=8)
                for g, b in enumerate((5, 6, 7)):
                    conv_last_tap(v, qk, g, b)
                need("cqsum_psum")
                settle(func(M2["rs"][:, 0:T], bank[0][:, 0:T], ACT.Sqrt, scale=1.0 / 384, bias=EPS))
                tell(func(M2["rs"][:, T:2 * T], bank[0][:, T:2 * T], ACT.Sqrt, scale=1.0 / 256, bias=EPS),
                     "cqstd", 0)
                conv_last_tap(v, qk, 3, 3)
                need("m_rows")
                tell(func(grow("em"), grow("mm"), ACT.Exp, scale=-1.0), "em_row")
                for half, b in enumerate((2, 4)):
                    need("z_uqn")
                    tell(func(M2["qn"][:, half * 512:(half + 1) * 512], bank[b][:, :], ACT.Copy), "qn_sb", b)
                need("z_uqr")
                tell(func(M2["qr"], bank[5][:, :], ACT.Copy), "qr_sb", 5)
                for half, b in enumerate((6, 7)):
                    need("z_ukn")
                    tell(func(M2["kn"][:, half * 512:(half + 1) * 512], bank[b][:, :], ACT.Copy), "kn_sb", b)
                for tb in range(TB):
                    need("z_ukv")
                    tell(func(M2["va"][:, tb * 512:(tb + 1) * 512], bank[tb][:, :], ACT.Copy), "va_sb", tb)
                need("z_vm")
                for tb, b in enumerate((2, 4)):
                    tell(func(M2["vt2"][:, tb * 512:(tb + 1) * 512], bank[b][:, :], ACT.Copy), "vm_sb", b)
                for half, b in enumerate((5, 6)):
                    need("z_om")
                    tell(func(M2["om"][:, half * 512:(half + 1) * 512], bank[b][:, :], ACT.Sigmoid), "om_sb", b)
                for g in range(4):
                    need("conv2")
                    tell(func(qk[:, 2 * g:2 * g + 2, :], qk[:, 2 * g:2 * g + 2, :], ACT.Silu), "qkm_sb")
                for head in range(8):
                    need("att_max")
                    o = (head % 2) * 512
                    col = 96 + 8 * (head % 2)
                    for qb in range(TB):
                        c0, n = (o, P) if qb == 0 else (o + P, T)
                        ins = func(M2["prob"][:, c0:c0 + n], M2["prob"][:, c0:c0 + n], ACT.Exp,
                                   bias=small[:, col + qb:col + qb + 1],
                                   accum_out=small[:, col + 2 + qb:col + 3 + qb])
                    tell(ins, "att_exp")
                    need("attT_psum")
                    b = 3 if head % 2 else 7
                    pt = M2["pt"][:, (head % 2) * 384:(head % 2) * 384 + 384]
                    tell(func(pt, bank[b][:, 0:384], ACT.Copy), "attT_sb", b)
                for head in range(8):
                    need("w_arg")
                    wm = M2["wm"][:, (head % 2) * 384:(head % 2) * 384 + 384]
                    tell(func(wm, wm, ACT.Exp, scale=-1.0), "w_exp")
                need("hm_ready", 4)
                tell(func(M2["hsq"], M2["hm"], ACT.Square), "hsq_sb")
                for j, b in enumerate((0, 1, 6, 7)):
                    need("z_gm")
                    tell(func(M2["gm1"][:, j * 512:(j + 1) * 512], bank[b][:, :], ACT.Sigmoid), "gm_sb", b)
                for half in range(2):
                    need("hsum_psum")
                    b = (2, 4)[half]
                    tell(func(M2["hstd"][:, half * 512:(half + 1) * 512], bank[b][:, :], ACT.Sqrt,
                              scale=1.0 / 64, bias=EPS), "hstd", b)
                for j, b in enumerate((3, 5, 0, 1)):
                    need("z_gm")
                    tell(func(M2["gm2"][:, j * 512:(j + 1) * 512], bank[b][:, :], ACT.Sigmoid), "gm_sb", b)

            def conv_last_tap(v, qk, g, b):
                need("z_qm")
                for i in range(2):
                    b8 = 2 * g + i
                    ins = func(qk[:, b8, :], bank[b][:, i * T:(i + 1) * T], ACT.Identity,
                               scale=v[:, PACK2["conv_w"] + 24 + b8:PACK2["conv_w"] + 25 + b8],
                               bias=v[:, PACK2["conv_b"] + b8:PACK2["conv_b"] + b8 + 1])
                tell(ins, "conv_last")

            def ffn(f0):
                for f in range(FFN_FB):
                    act.wait_ge(s["up_done"], f0 + f + 1)
                    if f >= 2:
                        act.wait_ge(s["g_ready"], f0 + f - 1)
                    func(MF["act"][:, (f % 2) * T:(f % 2 + 1) * T], bank[2 * (f % 2)][:, 0:T], ACT.Silu)\
                        .then_inc(s["silu_done"], 1)

            def moe_gates():
                need("lgt_exp")
                tell(func(small[:, 48:64], small[:, 48:64], ACT.Exp), "sp_exp")
                for j in range(4):
                    need("gbc_psum")
                    tell(func(MF["gbc"][:, j * 512:(j + 1) * 512], bank[2 + j][:, :], ACT.Copy), "gbc_ready", 2 + j)

            def moe(f0):
                with act.Fori(0, PAIR_ITERS) as it:
                    for j in range(4):
                        act.wait_ge(s["up_done"], it * 4 + (f0 + j + 1))
                        act.wait_ge(s["g_ready"], it * 4 + (f0 + j - 1))
                        func(MF["act"][:, (j % 2) * T:(j % 2 + 1) * T], bank[2 * (j % 2)][:, 0:T], ACT.Silu)\
                            .then_inc(s["silu_done"], 1)

            def conv_ffn(li, f0):
                t1, t2 = vcol[:, 4 + 2 * li, :], vcol[:, 5 + 2 * li, :]
                s0 = f0 - F0["conv0"]
                def taps(f):
                    act.wait_ge(s["up_done"], f0 + f + 1)
                    if f >= 2:
                        act.wait_ge(s["g_ready"], f0 + f - 1)
                    for w in range(2):
                        blk = w * FFN_FB + f
                        ins = func(MF["cv"][:, (2 * (f % 2) + w) * T:(2 * (f % 2) + w + 1) * T],
                                   bank[2 * (f % 2) + w][:, 0:T], ACT.Identity,
                                   scale=t2[:, blk:blk + 1],
                                   bias=t2[:, 2 * FFN_FB + blk:2 * FFN_FB + blk + 1])
                    ins.then_inc(s["conv_a"], 1)
                def gelu(f):
                    act.wait_ge(s["conv_v"], s0 + f + 1)
                    c0 = 2 * (f % 2) * T
                    func(MF["cv"][:, c0:c0 + T], MF["cv"][:, c0:c0 + T], ACT.Gelu_apprx_tanh)\
                        .then_inc(s["gelu_done"], 1)
                for f in range(FFN_FB):
                    taps(f)
                    gelu(f)

            start()
            norm(0)
            mixer1(0)
            norm(24)
            ffn(0)
            norm(0)
            mixer1(1)
            norm(24)
            moe_gates()
            moe(F0["moe"])
            norm(None)
            norm(0)
            mixer2(0)
            norm(24)
            conv_ffn(0, F0["conv0"])
            norm(0)
            mixer2(1)
            norm(24)
            conv_ffn(1, F0["conv1"])
            norm(None)

        @block.vector
        def _(dve):
            got = Counter()
            chain = Counter()

            def need(name, n=1):
                got[name] += n
                dve.wait_ge(s[name], got[name])

            def settle(ins):
                chain["dve"] += 1
                ins.then_inc(dve_chain, 1)
                dve.wait_ge(dve_chain, chain["dve"])

            def tell(ins, name, *banks):
                settle(ins)
                if name:
                    dve.sem_inc(s[name], 1)
                for b in banks:
                    dve.sem_inc(bank_free[b], 1)

            def tt(out, a, b, op):
                return nc.vector.tensor_tensor(out, a, b, op)

            def ts(out, a, s1, op0, s2=None, op1=None):
                if op1 is None:
                    return nc.vector.tensor_scalar(out, a, s1, None, op0)
                return nc.vector.tensor_scalar(out, a, s1, s2, op0, op1)

            def stt(out, a, sc, b, op0, op1):
                return nc.vector.scalar_tensor_tensor(out, a, sc, b, op0, op1)

            def ada_piece(n):
                layer, piece = divmod(n, ADA_PER_LAYER)
                kb, j = divmod(piece, ADA_SLOTS)
                dve.wait_ge(ada_full[j], 16 * (layer * KB + kb + 1))
                scalar = c_col[:, layer // 2, kb:kb + 1]
                if kb == 0:
                    ins = ts(ada_acc[:, j, :], ada_in[:, j, :], scalar, ALU.mult)
                else:
                    dve.wait_ge(s["ada_used"], n - ADA_SLOTS + 1)
                    ins = stt(ada_acc[:, j, :], ada_in[:, j, :], scalar, ada_acc[:, j, :], ALU.mult, ALU.add)
                ins.then_inc(s["ada_used"], 1)

            def ada_finish(layer):
                dve.wait_ge(s["ada_used"], (layer + 1) * ADA_PER_LAYER)
                dve.sem_inc(s["ada_done"], 1)

            def modulation(layer):
                need("mod_psum")
                pack = (PACK1, PACK2)[layer // 2]
                v = vcol[:, layer, :]
                tell(tt(mod[:, :], bank[0][:, 0:MODS], v[:, 0:MODS], ALU.add), None, 0)
                for i, g in enumerate(("norm_mix", "norm_ffn")):
                    ins = stt(scale_a[:, i, :], mod[:, 24 * i + 8:24 * i + 16], 1.0, v[:, pack[g]:pack[g] + 8],
                              ALU.add, ALU.mult)
                settle(ins)

            def norm(scale, out, inc):
                need("norm_std")
                settle(nc.vector.reciprocal(region(2048, T), region(2304, T)))
                for kb in range(KB):
                    stt(out[:, kb, :], x[:, kb, :], scale[:, kb:kb + 1], region(2048, T), ALU.mult, ALU.mult)\
                        .then_inc(s[inc], 1)

            def start():
                need("vcol_psum")
                packs = [bank[i][:, :].rearrange("p (k f) -> p k f", k=4) for i in range(2)]
                for k, lo, n in ((0, 0, PACK1_ROWS), (0, 2, PACK2_ROWS), (1, 0, PACKF_ROWS + KB), (1, 2, PACKF_ROWS)):
                    ins = nc.vector.tensor_copy(vcol[:, 4 * k + lo:4 * k + lo + 2, 0:n], packs[k][:, lo:lo + 2, 0:n])
                tell(ins, "vcol_ready", 0, 1)
                for g in range(4):
                    need("x_psum")
                    settle(nc.vector.tensor_copy(x[:, 2 * g:2 * g + 2, :],
                                                 bank[2 + g][:, :].rearrange("p (k t) -> p k t", k=2)))
                    dve.sem_inc(bank_free[2 + g], 1)
                    dve.sem_inc(s["x_ready"], 2)
                posf, ang, turns, cosa, flag = (region(3072 + 256 * i, T) for i in (3, 1, 4, 2, 5))
                settle(nc.vector.tensor_copy(posf, region(3072, T).bitcast(I32)))
                settle(ts(ang, posf, const[:, C_INV:C_INV + 1], ALU.mult))
                settle(ts(turns, ang, float(1.0 / (2.0 * np.pi)), ALU.mult, ROUND_MAGIC, ALU.add))
                settle(ts(turns, turns, ROUND_MAGIC, ALU.subtract))
                settle(stt(ang, turns, -TWO_PI_HI, ang, ALU.mult, ALU.add))
                settle(stt(ang, turns, -TWO_PI_LO, ang, ALU.mult, ALU.add))
                settle(ts(cosa, ang, float(np.pi / 2), ALU.add))
                settle(ts(flag, cosa, float(np.pi), ALU.is_gt))
                settle(stt(cosa, flag, float(-2.0 * np.pi), cosa, ALU.mult, ALU.add))
                tell(ts(cosa, cosa, 3.1415925, ALU.min, -3.1415925, ALU.max), "ang")
                tell(ts(ang, ang, 3.1415925, ALU.min, -3.1415925, ALU.max), "ang")
                need("c_act")
                for n in range(ADA_PER_LAYER):
                    ada_piece(n)
                ada_finish(0)

            def log_sigmoid(dst, ax, xb, e_name="lf_exp"):
                tell(stt(ax, xb, -1.0, xb, ALU.mult, ALU.max), "lf_abs")
                need(e_name)
                settle(stt(dst, xb, 0.0, ax, ALU.min, ALU.subtract))

            def mixer1(li):
                v = vcol[:, li, :]
                u = M1["u"].rearrange("p (b t) -> p b t", b=4)
                col = lambda name, i: v[:, PACK1[name] + i:PACK1[name] + i + 1]
                nc.vector.memset(M1["sc"], 0.0)
                for g in range(2):
                    need("conv1")
                    need("z_rgx")
                    for lag in (1, 2, 3):
                        for i in range(2):
                            b4 = 2 * g + i
                            ins = stt(u[:, b4, lag:T], bank[g][:, i * T:(i + 1) * T - lag],
                                      col("conv_w", (3 - lag) * 4 + b4), u[:, b4, lag:T], ALU.mult, ALU.add)
                        settle(ins)
                    dve.sem_inc(bank_free[g], 1)
                dve.sem_inc(s["u_ready"], 1)
                need("z_logf")
                fx = M1["bb"]
                for b2 in range(2):
                    ins = ts(fx[:, b2 * T:(b2 + 1) * T], bank[4][:, b2 * T:(b2 + 1) * T], col("bg", b2), ALU.add)
                tell(ins, None, 4)
                log_sigmoid(M1["lf"], M1["lf"], fx)
                settle(ts(M1["lf"], M1["lf"], 1.0 / 16.0, ALU.mult))
                for b2 in range(2):
                    ins = nc.vector.tensor_tensor_scan(M1["bb"][:, b2 * T:(b2 + 1) * T],
                                                       const[:, C_RESET:C_RESET + T],
                                                       M1["lf"][:, b2 * T:(b2 + 1) * T], 0.0, ALU.mult, ALU.add)
                settle(ins)
                lam = v[:, PACK1["lam"]:PACK1["lam"] + 4]
                tell(stt(small[:, 4:8], lam, -1.0, lam, ALU.mult, ALU.max), "c8_ready")
                bb = M1["bb"].rearrange("p (c t) -> p c t", t=GLA_CHUNK)
                view = lambda name: M1[name].rearrange("p (c t) -> p c t", t=GLA_CHUNK)
                tt(view("qloc"), bb, bb[:, :, GLA_CHUNK // 2 - 1:GLA_CHUNK // 2].to_broadcast([P, 8, GLA_CHUNK]),
                   ALU.subtract)
                tell(stt(view("kend"), bb, -1.0, bb[:, :, GLA_CHUNK - 1:].to_broadcast([P, 8, GLA_CHUNK]),
                         ALU.mult, ALU.add), "b_ready")
                need("sp_exp")
                settle(ts(small[:, 0:4], lam, -1.0, ALU.mult, 0.0, ALU.max))
                settle(tt(small[:, 0:4], small[:, 0:4], small[:, 4:8], ALU.add))
                ts(small[:, 8:12], small[:, 0:4], -8.0, ALU.mult)
                tell(ts(small[:, 12:16], small[:, 0:4], 8.0, ALU.mult), "rgchain_a")
                need("z_k")
                tell(nc.vector.tensor_copy(M1["k"], bank[5][:, :]), None, 5)
                need("exps_sb")
                need("q_sb")
                tell(tt(M1["kend"], M1["kend"], M1["k"], ALU.mult), "kend_sb")
                tt(M1["kloc"], M1["kloc"], M1["k"], ALU.mult)
                tt(M1["qloc"], M1["qloc"], M1["q"], ALU.mult)
                tell(tt(M1["qint"], M1["qint"], M1["q"], ALU.mult), "k_sb")
                need("rgchain_m")
                settle(ts(M1["gg"], M1["mu"], 1.0, ALU.add))
                settle(nc.vector.reciprocal(M1["gg"], M1["gg"]))
                settle(stt(M1["mu"], M1["mu"], 2.0, M1["gg"], ALU.mult, ALU.mult))
                tell(ts(M1["mu"], M1["mu"], 1e-30, ALU.max), "rgchain_s")
                for half, b in enumerate((7, 0)):
                    need("scores_psum")
                    mask = const[:, C_GLA:C_GLA + P].bitcast(U32).unsqueeze(1).to_broadcast([P, 4, P])
                    tell(nc.vector.copy_predicated(
                        M1["sc"].rearrange("p (i q) -> p i q", i=8)[:, 4 * half:4 * half + 4, :], mask,
                        bank[b][:, :].rearrange("p (i q) -> p i q", i=4)), "sc_sb", b)
                st = M1["st"].rearrange("p (n b v) -> p n b v", n=3, b=2)
                for n, b in enumerate((1, 2, 3)):
                    need("upd_psum")
                    for pair in range(2):
                        for hh in range(2):
                            r = slice(64 * hh, 64 * hh + 64)
                            upd = bank[b][r, pair * 256 + hh * P:pair * 256 + (hh + 1) * P]
                            if n == 0:
                                ins = nc.vector.tensor_copy(st[r, 0, pair, :], upd)
                            else:
                                ins = stt(st[r, n, pair, :], st[r, n - 1, pair, :],
                                          small[r, 16 + pair * 4 + n:17 + pair * 4 + n], upd, ALU.mult, ALU.add)
                    tell(ins, None, b)
                dve.sem_inc(s["states_sb"], 1)
                need("mult_sb")
                mu = M1["mu"].rearrange("p (b t) -> p b t", b=4)
                nc.vector.memset(mu[:, :, 0], 1.0)
                settle(tt(M1["u"], M1["u"], M1["ii"], ALU.mult))
                settle(tt(M1["u"], M1["u"], M1["mu"], ALU.mult))
                for b4 in range(4):
                    sl = slice(b4 * T, (b4 + 1) * T)
                    ins = nc.vector.tensor_tensor_scan(M1["mu"][:, sl], M1["aa"][:, sl], M1["u"][:, sl], 0.0,
                                                       ALU.mult, ALU.add)
                settle(ins)
                need("gelu_sb", 2)
                need("silug_sb", 2)
                hh1 = h[:, 0:4, :].rearrange("p k t -> p (k t)")
                settle(tt(hh1, M1["mu"], M1["gg"], ALU.mult))
                for hh in range(2):
                    need("ostd_sb")
                    sl = slice(hh * 512, (hh + 1) * 512)
                    settle(nc.vector.reciprocal(M1["ostd"][:, sl], M1["ostd"][:, sl]))
                    tell(stt(M1["on"][:, sl], bank[6 + hh][:, :], col("gla_g", 0), M1["ostd"][:, sl],
                             ALU.mult, ALU.mult), None, 6 + hh)
                    for pair in range(2):
                        head = 2 * pair + hh
                        ins = tt(h[:, 4 + head, :], M1["on"][:, (2 * hh + pair) * T:(2 * hh + pair + 1) * T],
                                 M1["silug"][:, head * T:(head + 1) * T], ALU.mult)
                tell(ins, "ycat_ready")
                residual((2, 3, 5, 4), 16, "wout_psum")

            def residual(banks, gate_col, name):
                for j, b in enumerate(banks):
                    if name:
                        need(name)
                    for i in range(2):
                        k = 2 * j + i
                        ins = stt(x[:, k, :], bank[b][:, i * T:(i + 1) * T], mod[:, gate_col + k:gate_col + k + 1],
                                  x[:, k, :], ALU.mult, ALU.add)
                    settle(ins)
                    dve.sem_inc(bank_free[b], 1)
                    dve.sem_inc(s["x_ready"], 2)

            def mixer2(li):
                v = vcol[:, 2 + li, :]
                col = lambda name, i: v[:, PACK2[name] + i:PACK2[name] + i + 1]
                for b, dst in ((0, M2["cq"][:, 0:512]), (1, M2["cq"][:, 512:768]), (2, M2["ckv"])):
                    need("z_cq")
                    tell(nc.vector.tensor_copy(dst, bank[b][:, 0:dst.shape[1]]), "cq_sb", b)
                need("z_if")
                settle(ts(grow("fb"), bank[4][0:8, T:2 * T], gate_b[:, li, 1:2], ALU.add))
                log_sigmoid(grow("lf"), grow("lf"), grow("fb"))
                one8 = const[0:8, C_ONES:C_ONES + T]
                settle(nc.vector.tensor_tensor_scan(grow("b"), one8, grow("lf"), 0.0, ALU.mult, ALU.add))
                tell(stt(grow("a"), bank[4][0:8, 0:T], gate_b[:, li, 0:1], grow("b"), ALU.add, ALU.subtract), None, 4)
                settle(nc.vector.tensor_tensor_scan(grow("m"), one8, grow("a"), 0.0, ALU.mult, ALU.max))
                tell(tt(grow("mm"), grow("b"), grow("m"), ALU.add), "m_rows")
                qk = M2["qkm"].rearrange("p (b t) -> p b t", b=8)
                for g, b in enumerate((5, 6, 7)):
                    conv_taps(v, qk, g, b)
                need("cqstd")
                settle(nc.vector.reciprocal(M2["rs"], M2["rs"]))
                for b5 in range(5):
                    src = M2["cq"][:, b5 * T:(b5 + 1) * T] if b5 < 3 else M2["ckv"][:, (b5 - 3) * T:(b5 - 2) * T]
                    w = col("q_norm", b5) if b5 < 3 else col("kv_norm", b5 - 3)
                    ins = stt(src, src, w, M2["rs"][:, 0:T] if b5 < 3 else M2["rs"][:, T:2 * T],
                              ALU.mult, ALU.mult)
                tell(ins, "cqn")
                conv_taps(v, qk, 3, 3)
                if li == 0:
                    need("rope_ready")
                need("kr_sb")
                need("krot_psum")
                settle(tt(M2["kro"], M2["kr"], rope_cos[:, :], ALU.mult))
                tell(tt(M2["kr"], bank[1][:, 0:T], rope_sin[:, :], ALU.mult), None, 1)
                tell(tt(M2["kro"], M2["kro"], M2["kr"], ALU.add), "krot_sb")
                need("qr_sb")
                need("qrot_psum")
                for g in range(2):
                    sl = slice(g * T, (g + 1) * T)
                    settle(tt(M2["qro"][:, sl], M2["qr"][:, sl], rope_cos[:, :], ALU.mult))
                    ins = tt(M2["qr"][:, sl], bank[3][:, sl], rope_sin[:, :], ALU.mult)
                tell(ins, None, 3)
                tell(tt(M2["qro"], M2["qro"], M2["qr"], ALU.add), "qrot_sb")

                def masked(head):
                    need("att_psum")
                    o = (head % 2) * 512
                    b = head % 2
                    c = 96 + 8 * (head % 2)
                    tell(stt(M2["prob"][:, o:o + 384], bank[b][:, 0:384], QK_SCALE,
                             const[:, C_CHUNKMASK:C_CHUNKMASK + 384], ALU.mult, ALU.add), None, b)
                    for qb in range(TB):
                        c0, n = (o, P) if qb == 0 else (o + P, T)
                        ins = nc.vector.tensor_reduce(small[:, c + 4 + qb:c + 5 + qb], M2["prob"][:, c0:c0 + n],
                                                      AX_X, ALU.max)
                    settle(ins)
                    tell(ts(small[:, c:c + 2], small[:, c + 4:c + 6], -1.0, ALU.mult), "att_max")

                def normalised(head):
                    need("att_exp")
                    o = (head % 2) * 512
                    c = 96 + 8 * (head % 2)
                    settle(nc.vector.reciprocal(small[:, c + 6:c + 8], small[:, c + 2:c + 4]))
                    ts(M2["prob"][:, o:o + P], M2["prob"][:, o:o + P], small[:, c + 6:c + 7], ALU.mult)
                    tell(ts(M2["prob"][:, o + P:o + 384], M2["prob"][:, o + P:o + 384], small[:, c + 7:c + 8],
                            ALU.mult), "att_norm")

                def attended(head):
                    if head % 2:
                        pair = head // 2
                        need("att_y")
                        b = (2, 4)[pair % 2]
                        tell(nc.vector.tensor_copy(M2["yla"][:, pair * T:(pair + 1) * T], bank[b][:, 0:T]),
                             "yla_sb", b)

                for step in range(10):
                    if step < 8:
                        masked(step)
                    if 1 <= step < 9:
                        normalised(step - 1)
                    if step >= 2:
                        attended(step - 2)

                need("atok_psum")
                tell(nc.vector.tensor_copy(small[:, 112:128], bank[5][:, 0:16]), None, 5)

                def log_weights(head):
                    need("mb_psum")
                    b = head % 2
                    wm = M2["wm"][:, (head % 2) * 384:(head % 2) * 384 + 384]
                    ts(wm[:, 0:T], bank[b][:, 0:T], small[:, 112 + head:113 + head], ALU.subtract, 0.0, ALU.max)
                    tell(ts(wm[:, T:384], bank[b][:, T:384], small[:, 120 + head:121 + head], ALU.subtract,
                            0.0, ALU.max), "w_arg", b)

                def weights(head):
                    need("w_exp")
                    need("s_psum")
                    wm = M2["wm"][:, (head % 2) * 384:(head % 2) * 384 + 384]
                    sw = M2["sw"][:, (head % 2) * 384:(head % 2) * 384 + 384]
                    b = 6 if head % 2 else 7
                    settle(tt(wm, wm, const[:, C_CAUSAL:C_CAUSAL + 384], ALU.mult))
                    tell(stt(sw, bank[b][:, 0:384], 0.125, wm, ALU.mult, ALU.mult), "sw_ready", b)

                def outputs(pair):
                    need("num_psum", 2)
                    b, be = (2, 4)[pair % 2], (3, 5)[pair % 2]
                    den, hm = M2["den"], M2["hm"][:, pair * T:(pair + 1) * T]
                    settle(ts(hm, bank[b][:, T:2 * T], -1.0, ALU.mult))
                    settle(tt(den, bank[b][:, T:2 * T], hm, ALU.max))
                    tell(tt(den, den, bank[be][:, 0:T], ALU.max), None, be)
                    settle(nc.vector.reciprocal(den, den))
                    tell(tt(hm, bank[b][:, 0:T], den, ALU.mult), "hm_ready", b)

                for step in range(10):
                    if step < 8:
                        log_weights(step)
                    if 1 <= step < 9:
                        weights(step - 1)
                    if step >= 3 and step % 2 == 1:
                        outputs((step - 3) // 2)
                need("om_sb", 2)
                for half in range(2):
                    need("hstd")
                    sl = slice(half * 512, (half + 1) * 512)
                    settle(nc.vector.reciprocal(M2["hstd"][:, sl], M2["hstd"][:, sl]))
                    for i in range(2):
                        pair = 2 * half + i
                        sp2 = slice(pair * T, (pair + 1) * T)
                        ins = stt(M2["yml"][:, sp2], M2["hm"][:, sp2], col("head_norm", pair),
                                  M2["hstd"][:, sp2], ALU.mult, ALU.mult)
                    settle(ins)
                    ins = tt(M2["yml"][:, sl], M2["yml"][:, sl], M2["om"][:, sl], ALU.mult)
                tell(ins, "yml_ready")
                need("gm_sb", 4)
                for j, b in enumerate((2, 4, 6, 7)):
                    need("z_br")
                    sl = slice(j * 512, (j + 1) * 512)
                    tell(tt(M2["brt"][:, sl], bank[b][:, :], M2["gm1"][:, sl], ALU.mult), None, b)
                need("gm_sb", 4)
                for j, b in enumerate((3, 5, 0, 1)):
                    need("z_br")
                    sl = slice(j * 512, (j + 1) * 512)
                    tell(tt(M2["gm2"][:, sl], bank[b][:, :], M2["gm2"][:, sl], ALU.mult), None, b)
                    ins = tt(h[:, 2 * j:2 * j + 2, :].rearrange("p k t -> p (k t)"), M2["gm2"][:, sl],
                             M2["brt"][:, sl], ALU.add)
                tell(ins, "ycat_ready")
                residual((2, 4, 6, 7), 16, "wout_psum")

            def conv_taps(v, qk, g, b):
                need("conv_last")
                for lag in (1, 2, 3):
                    for i in range(2):
                        b8 = 2 * g + i
                        ins = stt(qk[:, b8, lag:T], bank[b][:, i * T:(i + 1) * T - lag],
                                  v[:, PACK2["conv_w"] + (3 - lag) * 8 + b8:PACK2["conv_w"] + (3 - lag) * 8 + b8 + 1],
                                  qk[:, b8, lag:T], ALU.mult, ALU.add)
                    settle(ins)
                dve.sem_inc(s["conv2"], 1)
                dve.sem_inc(bank_free[b], 1)

            def ffn(f0, ada_layer):
                pieces = iter(range(ada_layer * ADA_PER_LAYER, (ada_layer + 1) * ADA_PER_LAYER))
                for f in range(FFN_FB):
                    dve.wait_ge(s["silu_done"], f0 + f + 1)
                    if f >= 2:
                        dve.wait_ge(s["down_done"], f0 + f - 1)
                    tt(hidden[:, f % 2, :], MF["act"][:, (f % 2) * T:(f % 2 + 1) * T],
                       bank[2 * (f % 2) + 1][:, 0:T], ALU.mult).then_inc(s["g_ready"], 1)
                    for n in range(2 if f >= FFN_FB - 2 else 1):
                        ada_piece(next(pieces))
                ada_finish(ada_layer)
                dve.wait_ge(s["down_done"], f0 + FFN_FB)
                residual((4, 5, 6, 7), 40, None)

            def moe_gates():
                need("router_psum")
                L = small[:, 32:48]
                tell(nc.vector.tensor_copy(L, bank[0][:, 0:16]), None, 0)
                ltm = const[:, C_LT:C_LT + 64].rearrange("p (e j) -> p e j", e=8)
                for tb in range(TB):
                    l = small[:, 32 + 8 * tb:40 + 8 * tb]
                    lj = l.unsqueeze(1).to_broadcast([P, 8, 8])
                    le = l.unsqueeze(2).to_broadcast([P, 8, 8])
                    gt = small[:, 128:192].rearrange("p (e j) -> p e j", e=8)
                    eq = small[:, 192:256].rearrange("p (e j) -> p e j", e=8)
                    tt(gt, lj, le, ALU.is_gt)
                    settle(tt(eq, lj, le, ALU.is_equal))
                    settle(tt(eq, eq, ltm, ALU.mult))
                    settle(tt(gt, gt, eq, ALU.add))
                    settle(nc.vector.tensor_reduce(small[:, 80:88], gt, AX_X, ALU.add))
                    settle(ts(small[:, 64 + 8 * tb:72 + 8 * tb], small[:, 80:88], 1.5, ALU.is_lt))
                    settle(nc.vector.tensor_reduce(small[:, 88:89], l, AX_X, ALU.max))
                    settle(ts(small[:, 48 + 8 * tb:56 + 8 * tb], l, small[:, 88:89], ALU.subtract))
                dve.sem_inc(s["lgt_exp"], 1)
                need("sp_exp")
                settle(tt(small[:, 64:80], small[:, 64:80], small[:, 48:64], ALU.mult))
                settle(nc.vector.tensor_reduce(small[:, 88:90], small[:, 64:80].rearrange("p (b e) -> p b e", b=2),
                                               AX_X, ALU.add))
                settle(nc.vector.reciprocal(small[:, 90:92], small[:, 88:90]))
                for tb in range(TB):
                    g = small[:, 64 + 8 * tb:72 + 8 * tb]
                    ins = ts(g, g, small[:, 90 + tb:91 + tb], ALU.mult)
                tell(ins, "gates_sb")
                need("gatesT_psum")
                tell(nc.vector.tensor_copy(MF["gates_t"][0:8, :], bank[1][0:8, 0:T]), "gatesT_sb", 1)
                need("gbc_ready", 4)

            def moe(f0):
                n0 = 2 * ADA_PER_LAYER

                def one_pass(pair, c, ada_kb=None):
                    it = pair * CHUNKS + c
                    for j in range(4):
                        dve.wait_ge(s["silu_done"], it * 4 + (f0 + j + 1))
                        act_j = MF["act"][:, (j % 2) * T:(j % 2 + 1) * T]
                        nc.vector.tensor_tensor(act_j, act_j, MF["gbc"][:, bass.ds((pair * 2 + j // 2) * T, T)],
                                                ALU.mult).then_inc(s["gated"], 1)
                        dve.wait_ge(s["gated"], it * 4 + (j + 1))
                        dve.wait_ge(s["down_done"], it * 4 + (f0 + j - 1))
                        nc.vector.tensor_tensor(hidden[:, j % 2, :], act_j, bank[2 * (j % 2) + 1][:, 0:T],
                                                ALU.mult).then_inc(s["g_ready"], 1)
                        if ada_kb is not None and j < ADA_SLOTS:
                            dve.wait_ge(ada_full[j], (ada_kb + (2 * KB + 1)) * 16)
                            dve.wait_ge(s["ada_used"], ada_kb * ADA_SLOTS + (n0 + j - ADA_SLOTS + 1))
                            nc.vector.scalar_tensor_tensor(
                                ada_acc[:, j, :], ada_in[:, j, :], c_col[:, 1, bass.ds(ada_kb, 1)],
                                ada_acc[:, j, :], ALU.mult, ALU.add).then_inc(s["ada_used"], 1)

                for n in range(ADA_SLOTS):
                    ada_piece(n0 + n)
                with dve.Fori(0, KB - 1) as c:
                    one_pass(0, c, c + 1)
                with dve.Fori(KB - 1, CHUNKS) as c:
                    one_pass(0, c)
                with dve.Fori(1, EXPERTS // 2) as pair:
                    with dve.Fori(0, CHUNKS) as c:
                        one_pass(pair, c)
                ada_finish(2)
                dve.wait_ge(s["down_done"], f0 + PAIR_ITERS * 4)
                residual((4, 5, 6, 7), 40, None)

            def conv_ffn(li, f0, ada_layer):
                t1, t2 = vcol[:, 4 + 2 * li, :], vcol[:, 5 + 2 * li, :]
                c0 = f0 - F0["conv0"]
                pieces = iter(range(0) if ada_layer is None else
                              range(ada_layer * ADA_PER_LAYER, (ada_layer + 1) * ADA_PER_LAYER))

                def taps(f):
                    dve.wait_ge(s["conv_a"], c0 + f + 1)
                    for lag in (1, 2):
                        for w in range(2):
                            i = 2 * (f % 2) + w
                            blk = (2 - lag) * 2 * FFN_FB + w * FFN_FB + f
                            ins = stt(MF["cv"][:, i * T + lag:(i + 1) * T], bank[i][:, 0:T - lag],
                                      t1[:, blk:blk + 1], MF["cv"][:, i * T + lag:(i + 1) * T],
                                      ALU.mult, ALU.add)
                        if lag == 1:
                            settle(ins)
                    ins.then_inc(s["conv_v"], 1)

                for f in range(FFN_FB):
                    taps(f)
                    for n in range(2 if f >= FFN_FB - 2 else 1):
                        for piece in (next(pieces, None),):
                            if piece is not None:
                                ada_piece(piece)
                    dve.wait_ge(s["gelu_done"], c0 + f + 1)
                    if f >= 2:
                        dve.wait_ge(s["down_done"], f0 + f - 1)
                    i = 2 * (f % 2)
                    tt(hidden[:, f % 2, :], MF["cv"][:, i * T:(i + 1) * T], MF["cv"][:, (i + 1) * T:(i + 2) * T],
                       ALU.mult).then_inc(s["g_ready"], 1)
                if ada_layer is not None:
                    ada_finish(ada_layer)
                dve.wait_ge(s["down_done"], f0 + FFN_FB)
                residual((4, 5, 6, 7), 40, None)

            start()
            modulation(0)
            norm(scale_a[:, 0, :], h, "norm_mul")
            mixer1(0)
            norm(scale_a[:, 1, :], h, "norm_mul")
            ffn(0, 1)
            modulation(1)
            norm(scale_a[:, 0, :], h, "norm_mul")
            mixer1(1)
            norm(scale_a[:, 1, :], h, "norm_mul")
            moe_gates()
            moe(F0["moe"])
            norm(vcol[:, 1, PACK1["final"]:PACK1["final"] + KB], x, "x_ready")
            modulation(2)
            norm(scale_a[:, 0, :], h, "norm_mul")
            mixer2(0)
            norm(scale_a[:, 1, :], h, "norm_mul")
            conv_ffn(0, F0["conv0"], 3)
            modulation(3)
            norm(scale_a[:, 0, :], h, "norm_mul")
            mixer2(1)
            norm(scale_a[:, 1, :], h, "norm_mul")
            conv_ffn(1, F0["conv1"], None)
            norm(vcol[:, 3, PACK2["final"]:PACK2["final"] + KB], x, "x_ready")
            for b in range(4):
                need("outT_psum")
                tell(nc.vector.tensor_copy(region(2560 + b * 512, 512), bank[b][:, :]), "out_sb", b)


def kernel(**inputs):
    import concourse.bacc as bacc
    from concourse.bass_utils import run_bass_kernel_spmd

    nc = bacc.Bacc("TRN2", target_bir_lowering=False, num_devices=1)
    arrays = {name: np.ascontiguousarray(inputs[name]) for name in INPUTS}
    arrays["const_table"], arrays["const_sel"] = constants()
    aps = {}
    for name, a in arrays.items():
        aps[name] = nc.dram_tensor("in_" + name, a.shape, mybir.dt.from_np(a.dtype), kind="ExternalInput").ap()
    out = nc.dram_tensor("result", (1, T, DM), F32, kind="ExternalOutput").ap()
    two_blocks(nc, aps, out)
    r = run_bass_kernel_spmd(nc, [{"in_" + name: a for name, a in arrays.items()}], core_ids=[0])
    return r.results[0]["result"]
```

```python
from collections import Counter
from contextlib import ExitStack

import numpy as np

import concourse.bass as bass
from concourse import mybir

F32 = mybir.dt.float32
F32R = mybir.dt.float32r
I32 = mybir.dt.int32
U32 = mybir.dt.uint32
ALU = mybir.AluOpType
ACT = mybir.ActivationFunctionType
AX_X = mybir.AxisListType.X

P = 128
T = 256
TB = T // P
DM = 1024
KB = DM // P
EPS = 1e-6
DFF = 2816
EXPERTS = 8
CHUNK_COLS = 256
CHUNKS = DFF // CHUNK_COLS
MODS = 6 * KB
MOD_PARTS = ((0, 2 * KB), (2 * KB, MODS))

RING = 6
SLOT = 2048
ADA_SLOTS = 3
ADA_PER_LAYER = KB * ADA_SLOTS
ADA_AT = [1, 2, 1, 2] + [1] * 18

BIG_NEG = -1.0e30
ROPE_THETA = 10000.0
QK_SCALE = 96.0 ** -0.5
TWO_PI_HI = 6.28125
TWO_PI_LO = float(2.0 * np.pi - 6.28125)
ROUND_MAGIC = 12582912.0
GLA_CHUNK = 64

C_ONES, C_IDENT, C_PAIR, C_GLA, C_CAUSAL, C_CHUNKMASK, C_SWAP, C_RESET, C_LT, C_INV, C_RANK = (
    0, 256, 384, 512, 640, 1024, 1408, 1536, 1792, 1856, 1857)
C_COLS = 1985
C_ZERO = C_CHUNKMASK + P

PACK1 = dict(ada_b=0, norm_mix=48, norm_ffn=56, conv_w=64, conv_b=80, ba=84, bx=88, lam=92, bg=96,
             gla_g=98, final=99)
PACK1_ROWS = 107
PACK2 = dict(ada_b=0, norm_mix=48, norm_ffn=56, q_norm=64, kv_norm=67, conv_w=69, conv_b=101,
             head_norm=109, final=113)
PACK2_ROWS = 121
FFN_FB = DFF // P
PACKF_ROWS = 4 * FFN_FB


SEMAPHORES = """
first_in c_psum mask_sb rank_psum route_ready htok_psum htok_sb spread_ready spreadT_psum spreadT_sb
pick_ready hx_psum hx_a hx_d hxs_ready y_free_a y_free_d scattered ada_done ada_used ang atok_psum
attT_psum attT_sb att_exp att_max att_norm att_psum att_y b_ready c8_ready c_act conv1 conv2 conv_a
conv_last conv_v cq_sb cq_sq cqn cqstd cqsum_psum down_done em_row exps_sb flow_sb g_ready gated
gatesT_psum gatesT_sb gates_sb gbc_psum gbc_ready gelu_done gelu_sb gm_sb h_ready hm_ready k_sb kend_psum
kend_sb kn_sb kr_sb kt_sb lf_abs lf_exp lgt_exp m_rows mb_psum mod_psum mult_sb norm_mul norm_sq norm_std
norm_sum o_psum outT_psum out_sb params q_sb qkm_sb qn_sb qr_sb rgchain_v rgchain_m ri_psum rope_ready
router_psum scores_psum silu_done sp_exp states_sb stored u_ready units_used up_done v_sb va_sb vcol_psum
vcol_ready w_arg w_exp wout_psum x_psum x_ready ycat_ready yla_sb yml_ready z_br z_cq z_gate z_gm z_k z_q
z_qm z_rgx z_ukn z_ukv z_uqn z_uqr z_v zeroed headsq_sb headsum_psum outgate_sb scores_sb z_loggate
z_outgate z_narrow heads_psum headstd_sb split_hi split_lo h_lo rot_psum rot_sb down_hi down_lo
"""

F0 = {"dense": 0, "moe": FFN_FB, "conv0": FFN_FB * (1 + EXPERTS), "conv1": FFN_FB * (2 + EXPERTS)}

INPUTS = """
x c ada_w ada_b norm_mix_g norm_ffn_g w_in rg_conv_w rg_conv_b rg_wa rg_ba rg_wx rg_bx rg_lambda gla_wg2
gla_bg gla_norm_g w_out ffn_w1 ffn_w3 ffn_w2 router_w moe_w1 moe_w3 moe_w2 final_g c_2 positions_2 ada_w_2
ada_b_2 norm_mix_w_2 w_in_2 q_norm_w_2 kv_norm_w_2 w_uq_2 w_ukv_2 mlstm_conv_w_2 mlstm_conv_b_2
mlstm_gate_b_2 mlstm_head_norm_w_2 w_br_mla_2 w_br_mlstm_2 w_out_2 norm_ffn_w_2 ffn_w_up_2 ffn_conv_w_2
ffn_conv_b_2 ffn_w_down_2 final_norm_w_2
""".split()


GATE_ROWS = ("fb", "lf", "b", "a", "m", "mm", "em")


def constants():
    c = np.zeros((P, C_COLS), np.float32)
    r = np.arange(P)
    c[:, C_ONES:C_ONES + 256] = 1.0
    c[:, C_IDENT:C_IDENT + P] = np.eye(P)
    c[:, C_PAIR:C_PAIR + P] = (r[:, None] // 64) == (r[None, :] // 64)
    same = (r[:, None] // GLA_CHUNK) == (r[None, :] // GLA_CHUNK)
    c[:, C_GLA:C_GLA + P] = same & (r[:, None] <= r[None, :])
    tri = (r[:, None] <= r[None, :]).astype(np.float32)
    c[:, C_CAUSAL:C_CAUSAL + 384] = np.concatenate([tri, np.ones((P, P), np.float32), tri], 1)
    late = np.where((r[:, None] < 64) & (r[None, :] >= 64), BIG_NEG, 0.0)
    c[:, C_CHUNKMASK:C_CHUNKMASK + 384] = np.concatenate([late, np.zeros((P, P)), late], 1)
    half = r % 32
    for out in range(P):
        src = out + 16 if half[out] < 16 else out - 16
        c[src, C_SWAP + out] = -1.0 if half[out] < 16 else 1.0
    c[:, C_RESET:C_RESET + 256] = (np.arange(T) % GLA_CHUNK != 0)
    e, j = np.divmod(np.arange(64), 8)
    c[:, C_LT:C_LT + 64] = j < e
    c[:, C_INV] = np.float32(ROPE_THETA) ** (-(r % 16).astype(np.float32) / np.float32(16))
    c[:, C_RANK:C_RANK + P] = np.arange(1, P + 1)
    sel = np.zeros((8, 8 * P + 4 * P), np.float32)
    for h in range(8):
        sel[h, h * P:(h + 1) * P] = 1.0
        sel[h, 8 * P + h * 64:8 * P + (h + 1) * 64] = 1.0
    return c, sel


def unit_plan():
    order = []
    for li in range(2):
        order += [("rgx", li, j) for j in range(2)] + [("flow", li, 0), ("q", li, 0), ("k", li, 0)]
        order += [("v", li, j) for j in range(2)] + [("gate", li, j) for j in range(2)]
        order += [("g", li, j) for j in range(2)] + [("wout", li, j) for j in range(4)]
        if li == 0:
            order += [(w, 0, c) for c in range(CHUNKS) for w in ("w1", "w3", "w2")]
        else:
            order += ["loop"]
    for li in range(2):
        order += [("kr", li, 0), ("cq", li, 0), ("cq", li, 1), ("ckv", li, 0), ("if", li, 0)]
        order += [("qm", li, 0), ("qm", li, 1), ("km", li, 0), ("km", li, 1)]
        order += [("uqn", li, 0), ("uqr", li, 0), ("ukv", li, 0)]
        order += [("vm", li, 0), ("vm", li, 1), ("om", li, 0), ("om", li, 1)]
        order += [("gmla", li, j) for j in range(4)] + [("gml", li, j) for j in range(4)]
        order += [("brmla", li, j) for j in range(2)] + [("brml", li, j) for j in range(2)]
        order += [("wout2", li, j) for j in range(4)]
        order += [(w, li, c) for c in range(CHUNKS) for w in ("u1", "u3", "u2")]
    pos, count, plan, loop = 0, [0] * RING, {}, None
    for key in order:
        if key == "loop":
            pad = -pos % RING
            loop = (pos, pos + pad, list(count))
            pos += pad + 3 * CHUNKS * EXPERTS
            count = [n + 3 * CHUNKS * EXPERTS // RING for n in count]
            continue
        parts = {"kr": 4, "if": 2, "uqn": 3, "uqr": 12, "ukv": 4}.get(key[0], 1)
        count[pos % RING] += parts
        plan[key] = (pos % RING, count[pos % RING], pos)
        pos += 1
    return order, plan, loop


def two_blocks(nc, d, out):
    order, plan, (pos_before_loop, loop_pos, loop_count) = unit_plan()
    PAIR_ITERS = CHUNKS * EXPERTS // 2

    ctx = ExitStack()
    with ctx:
        def sb(name, shape, dt=F32):
            return ctx.enter_context(nc.sbuf_tensor(name, shape, dt))

        def sem(name):
            return ctx.enter_context(nc.semaphore(name))

        at = {}

        def sb_at(name, shape):
            at[name] = -(-nc.sbuf_base // 32) * 32
            return sb(name, shape)

        ring = sb_at("ring", [P, RING, SLOT])
        ada_acc = sb("ada_acc", [P, ADA_SLOTS, SLOT])
        ada_in = sb("ada_in", [P, ADA_SLOTS, SLOT])
        x = sb("x", [P, KB, T])
        h = sb_at("h", [P, KB, T])
        const = sb("const", [P, C_COLS])
        sel = sb("sel", [8, 12 * P])
        vcol = sb("vcol", [P, 8, P])
        gate_w = sb_at("gate_w", [P, 2, 2, 4, P])
        wg2 = sb("wg2", [16, 2, T])
        router = sb("router", [P, KB, EXPERTS])
        gate_b = sb("gate_b", [8, 2, 2])
        c_col = sb("c_col", [P, 2, KB])
        mod = sb("mod", [P, MODS])
        scale_a = sb("scale_a", [P, 2, KB])
        small = sb("small", [P, 256])
        rope_cos = sb("rope_cos", [P, T])
        rope_sin = sb("rope_sin", [P, T])
        route = sb("route", [1, 1], I32)
        gate_rows = sb("gate_rows", [8, len(GATE_ROWS), T])
        arena = sb_at("arena", [P, 14592])
        bank = [ctx.enter_context(nc.psum_tensor(f"bank{i}", [P, 512], F32)) for i in range(8)]

        def region(start, cols):
            return arena[:, start:start + cols]

        ones = const[:, C_ONES:C_ONES + P]
        ident = const[:, C_IDENT:C_IDENT + P]

        names = SEMAPHORES.split()
        s = {n: sem(n) for n in names}
        slot_full = [sem(f"slot_full{i}") for i in range(RING)]
        ada_full = [sem(f"ada_full{i}") for i in range(ADA_SLOTS)]
        bank_free = [sem(f"bank_free{i}") for i in range(8)]
        act_chain, dve_chain = sem("act_chain"), sem("dve_chain")

        def rows(w):
            return w.rearrange("(k p) f -> p k f", p=P)

        win1 = [rows(d["w_in"][li]) for li in range(2)]
        win2 = [rows(d["w_in_2"][li]) for li in range(2)]
        cols1 = dict(rgx=0, gate=512, q=1024, k=1280, v=1536, g=2048, flow=2560)
        cols2 = dict(cq=0, ckv=384, kr=640, qm=672, km=1184, vm=1696, om=2208, gmla=2736, gml=3760)

        def slot_view(key, kbs, width):
            sl = ring[:, plan[key][0], 0:kbs * width]
            return sl.rearrange("p (k f) -> p k f", k=kbs)

        def ffn_src(names3, li, c):
            w1, w3, w2 = names3
            cs = slice(c * CHUNK_COLS, (c + 1) * CHUNK_COLS)
            return (rows(w1)[:, :, cs], rows(w3)[:, :, cs], rows(w2[cs, :]))

        M1 = {n: region(*v) for n, v in dict(
            u=(0, 1024), rr=(1024, 1024), ii=(2048, 1024), aa=(3072, 1024), mu=(4096, 1024), gg=(5120, 1024),
            q=(6144, 512), k=(6656, 512), vt=(7168, 1024), bb=(8192, 512), lf=(8704, 512), qloc=(9216, 512),
            kloc=(9728, 512), kend=(10240, 512), qint=(10752, 512), kt=(11264, 512), sc=(11776, 1024),
            st=(12800, 768), flow=(13568, 256), rec=(6144, 1024), osq=(6144, 1024),
            ostd=(1024, 1024), on=(9216, 1024),
            silug=(10240, 1024)).items()}
        M2 = {n: region(*v) for n, v in dict(
            cq=(0, 768), ckv=(768, 512), csq=(1280, 1280), rs=(2560, 512), qn=(3072, 1024), qr=(4096, 512),
            qro=(4608, 512), kn=(5120, 1024), kr=(6144, 256), kro=(6400, 256), va=(6656, 1024),
            prob=(7680, 1024), pt=(8704, 768), yla=(9472, 1024), qkm=(10496, 2048), vt2=(12544, 1024),
            wm=(0, 768), sw=(768, 768), om=(1536, 1024), hm=(2560, 1024), hsq=(3584, 1024), hstd=(4608, 1024),
            yml=(5632, 1024), gm1=(6656, 2048), gm2=(10496, 2048), brt=(0, 2048), den=(13568, 256)).items()}
        MF = {n: region(*v) for n, v in dict(
            act=(3072, 512), gates_t=(4096, 256), gbc=(4352, 2048), cv=(6400, 1024)).items()}
        def rounded(name, shape, place, col=0):
            return nc.alloc_sbuf_tensor_at(name, shape, F32R, offset=at[place] + 4 * col)

        h_hi = rounded("h_hi", [P, KB, T], "arena", 4352)
        h_low = rounded("h_low", [P, KB, T], "h")
        w_hi = [rounded(f"w_hi{i}", [P, SLOT], "arena", c)[:, :] for i, c in enumerate((7424, 9472, 11520, 0))]
        w_low = rounded("w_low", [P, RING, SLOT], "ring")
        hidden_hi = rounded("hidden_hi", [P, 2, T], "arena", 3584)
        hidden_low = rounded("hidden_low", [P, 2, T], "arena", 2560)
        even = rounded("down_hi_even", [P, DM], "arena", 13568)
        down_hi_ffn = (even, rounded("down_hi_ffn", [P, DM], "arena", 6400))
        down_hi_conv = (even, rounded("down_hi_conv", [P, DM], "gate_w"))
        down_hi_moe = [rounded(f"down_hi_moe{i}", [P, DM], "h", i * DM) for i in range(2)]
        hid_hi = rounded("hid_hi", [P, 2, P], "gate_w", DM)
        hid_low = rounded("hid_low", [P, 2, P], "arena", 2048)
        MS = {n: region(*v) for n, v in dict(
            htok=(0, 2048), y=(0, 1024), hid=(2048, 256), act=(2304, 256), spread_t=(2560, 2048),
            hx=(4608, 8192)).items()}
        hxs = [region(1024, 1024).rearrange("p (k q) -> p k q", k=KB),
               region(12800, 1024).rearrange("p (k q) -> p k q", k=KB)]
        by_slot = h[:, :, :].rearrange("p k t -> p (k t)").rearrange("p (b f) -> p b f", b=TB)
        hidden = region(2560, 512).rearrange("p (i t) -> p i t", i=2)

        def grow(name):
            return gate_rows[:, GATE_ROWS.index(name), :]

        c_rows = region(4608, P)

        def ada_place(n):
            layer, m = divmod(n, ADA_PER_LAYER)
            return (layer, m % KB, m // KB) if layer == 0 else (layer, m // ADA_SLOTS, m % ADA_SLOTS)

        def param_loads():
            rows_in = region(0, 8 * P).rearrange("p (k f) -> p k f", k=8)
            first = [(c_rows[0:KB, :], d["c"][0].rearrange("(r f) -> r f", f=P)),
                     (c_rows[KB:2 * KB, :], d["c_2"][0].rearrange("(r f) -> r f", f=P)),
                     (const[:, :], d["const_table"])]
            loads = [(region(1024, TB * DM).rearrange("p (b f) -> p b f", b=TB),
                      d["x"][0].rearrange("(b p) f -> p b f", p=P)),
                     (sel[:, :], d["const_sel"])]

            def pack(i, row, vec):
                n = 1
                for extent in vec.shape:
                    n *= extent
                src = vec.rearrange("(r f) -> r f", f=P) if len(vec.shape) == 1 \
                    else vec.rearrange("t (r f) -> (t r) f", f=P)
                loads.append((rows_in[row:row + n // P, i, :], src))

            for li in range(2):
                for name, key in (("ada_b", "ada_b"), ("norm_mix_g", "norm_mix"), ("norm_ffn_g", "norm_ffn"),
                                  ("rg_conv_w", "conv_w"), ("rg_conv_b", "conv_b"), ("rg_ba", "ba"),
                                  ("rg_bx", "bx"), ("rg_lambda", "lam"), ("gla_bg", "bg"),
                                  ("gla_norm_g", "gla_g")):
                    pack(li, PACK1[key], d[name][li])
                pack(li, PACK1["final"], d["final_g"])
                for name, key in (("ada_b_2", "ada_b"), ("norm_mix_w_2", "norm_mix"),
                                  ("norm_ffn_w_2", "norm_ffn"), ("q_norm_w_2", "q_norm"),
                                  ("kv_norm_w_2", "kv_norm"), ("mlstm_conv_w_2", "conv_w"),
                                  ("mlstm_conv_b_2", "conv_b"), ("mlstm_head_norm_w_2", "head_norm")):
                    pack(2 + li, PACK2[key], d[name][li])
                pack(2 + li, PACK2["final"], d["final_norm_w_2"])
                pack(4 + 2 * li, 0, d["ffn_conv_w_2"][li, 0:2])
                pack(5 + 2 * li, 0, d["ffn_conv_w_2"][li, 2])
                pack(5 + 2 * li, 2 * FFN_FB, d["ffn_conv_b_2"][li])
            loads.append((region(3072, T).bitcast(I32), d["positions_2"].to_broadcast([P, T])))
            loads.append((router[:, :, :], rows(d["router_w"][0])))
            for li in range(2):
                loads.append((wg2[:, li, :], d["gla_wg2"][li]))
                for n in range(2):
                    loads.append((gate_b[:, li, n:n + 1],
                                  d["mlstm_gate_b_2"][li, 8 * n:8 * n + 8].unsqueeze(1)))
            first_gate = len(loads)
            for li in range(2):
                for g, name in enumerate(("rg_wa", "rg_wx")):
                    for hh in range(2):
                        r = slice(64 * hh, 64 * hh + 64)
                        src = d[name][li].rearrange("(b two) d e -> two d b e", two=2)[hh]
                        loads.append((gate_w[r, li, g, :, r], src))
            return first, loads, first_gate

        FIRST_LOADS, PARAM_LOADS, FIRST_GATE_LOAD = param_loads()
        N_PARAMS = len(PARAM_LOADS)

        block = ctx.enter_context(nc.Block())

        @block.sync
        def _(sp):
            def load(key, dst, src):
                if plan[key][2] >= RING:
                    sp.wait_ge(s["units_used"], plan[key][2] - RING + 1)
                sp.dma_start(dst, src).then_inc(slot_full[plan[key][0]], 16)

            for key in order:
                if key == order[2]:
                    for n, (dst, src) in enumerate(PARAM_LOADS):
                        if n == FIRST_GATE_LOAD:
                            sp.wait_ge(s["zeroed"], 1)
                        sp.dma_start(dst, src).then_inc(s["params"], 16)
                if key == "loop":
                    w1 = d["moe_w1"][0].rearrange("e (k p) f -> e p k f", p=P)
                    w3 = d["moe_w3"][0].rearrange("e (k p) f -> e p k f", p=P)
                    w2 = d["moe_w2"][0].rearrange("e (c k p) f -> e c p k f", p=P, k=2)

                    def expert_unit(slot, ex, c):
                        if slot % 3 < 2:
                            dst = ring[:, slot, :].rearrange("p (k f) -> p k f", k=KB)
                            src = (w1, w3)[slot % 3][ex, :, :, bass.ds(c * CHUNK_COLS, CHUNK_COLS)]
                        else:
                            dst = ring[:, slot, :].rearrange("p (k f) -> p k f", k=2)
                            src = w2[ex, c, :, :, :]
                        sp.dma_start(dst, src).then_inc(slot_full[slot], 16)

                    for slot in range(3):
                        sp.wait_ge(s["units_used"], loop_pos + slot - RING + 1)
                        expert_unit(slot, 0, 0)
                    sp.wait_ge(s["route_ready"], 1)
                    most = sp.value_load(route[0:1, 0:1])

                    def gathered_pair(pair, first_pair=False):
                        for n in range(2 * CHUNKS):
                            i, c = divmod(n, CHUNKS)
                            for slot in range(3 * (n % 2), 3 * (n % 2) + 3):
                                if first_pair and n == 0:
                                    continue
                                if first_pair and n == 1:
                                    sp.wait_ge(s["units_used"], loop_pos + slot - RING + 1)
                                else:
                                    sp.wait_ge(s["up_done" if slot % 3 < 2 else "down_done"],
                                               pair * (4 * CHUNKS) + (F0["moe"] + 2 * n - 2))
                                expert_unit(slot, pair * 2 + i, c)

                    def dense_pass(pair, c, slots=range(RING)):
                        for slot in slots:
                            sp.wait_ge(s["units_used"],
                                       (pair * CHUNKS + c) * RING + (loop_pos + slot - RING + 1))
                            expert_unit(slot, pair * 2 + slot // 3, c)

                    with sp.If(most < P + 1):
                        gathered_pair(0, first_pair=True)
                        with sp.Fori(1, EXPERTS // 2) as pair:
                            gathered_pair(pair)
                    with sp.Else():
                        dense_pass(0, 0, range(3, RING))
                        with sp.Fori(1, CHUNKS) as c:
                            dense_pass(0, c)
                        with sp.Fori(1, EXPERTS // 2) as pair:
                            with sp.Fori(0, CHUNKS) as c:
                                dense_pass(pair, c)
                    continue
                kind, li, j = key
                if kind == "flow":
                    load(key, slot_view(key, KB, 16), win1[li][:, :, 2560:2576])
                elif kind in cols1:
                    c0 = cols1[kind] + 256 * j
                    load(key, slot_view(key, KB, 256), win1[li][:, :, c0:c0 + 256])
                elif kind in ("wout", "wout2"):
                    w = rows(d["w_out" if kind == "wout" else "w_out_2"][li])
                    load(key, slot_view(key, KB, 256), w[:, :, 256 * j:256 * j + 256])
                elif kind in ("w1", "w3", "w2", "u1", "u3", "u2"):
                    if kind[0] == "w":
                        srcs = ffn_src((d["ffn_w1"][0], d["ffn_w3"][0], d["ffn_w2"][0]), li, j)
                    else:
                        up = d["ffn_w_up_2"][li]
                        srcs = ffn_src((up[:, 0:DFF], up[:, DFF:2 * DFF], d["ffn_w_down_2"][li]), li, j)
                    w = dict(zip("132", range(3)))[kind[1]]
                    load(key, slot_view(key, *((KB, 256) if w < 2 else (2, DM))), srcs[w])
                elif kind == "cq":
                    width = 256 if j == 0 else 128
                    load(key, slot_view(key, KB, width), win2[li][:, :, 256 * j:256 * j + width])
                elif kind == "kr":
                    dst = slot_view(key, KB, P).rearrange("p k (r f) -> p k r f", r=4)
                    for r in range(4):
                        load(key, dst[:, :, r, :], win2[li][:, :, 640:672])
                elif kind == "if":
                    dst = slot_view(key, KB, 16)
                    for n, c0 in enumerate((2720, 2728)):
                        load(key, dst[:, :, 8 * n:8 * n + 8], win2[li][:, :, c0:c0 + 8])
                elif kind in cols2:
                    c0 = cols2[kind] + 256 * j
                    load(key, slot_view(key, KB, 256), win2[li][:, :, c0:c0 + 256])
                elif kind == "uqn":
                    dst = slot_view(key, 3, 512).rearrange("p k (h f) -> p k h f", h=8)
                    src = rows(d["w_uq_2"][li]).rearrange("p k (h f) -> p k h f", h=8)
                    for k in range(3):
                        load(key, dst[:, k], src[:, k, :, 0:64])
                elif kind == "uqr":
                    dst = slot_view(key, 3, 256).rearrange("p k (g c e f) -> p k g c e f", g=2, c=2, e=2)
                    src = rows(d["w_uq_2"][li]).rearrange("p k (g e c f) -> p k g c e f", g=2, c=2, e=2)
                    for k in range(3):
                        for g in range(2):
                            for c in range(2):
                                load(key, dst[:, k, g, c], src[:, k, g, c, :, 64:96])
                elif kind == "ukv":
                    dst = slot_view(key, 2, DM).rearrange("p k (w h f) -> p k w h f", w=2, h=8)
                    src = rows(d["w_ukv_2"][li]).rearrange("p k (h w f) -> p k w h f", h=8, w=2)
                    for k in range(2):
                        for w in range(2):
                            load(key, dst[:, k, w], src[:, k, w])
                elif kind in ("brmla", "brml"):
                    w = rows(d["w_br_mla_2" if kind == "brmla" else "w_br_mlstm_2"][li])
                    load(key, slot_view(key, 4, 512), w[:, :, 512 * j:512 * j + 512])
            for tb in range(TB):
                sp.wait_ge(s["out_sb"], 2 * (tb + 1))
                sp.dma_start(out[0, tb * P:(tb + 1) * P, :], region(2560 + tb * DM, DM)).then_inc(s["stored"], 16)
            sp.wait_ge(s["stored"], 16 * TB)

        @block.gpsimd
        def _(pool):
            nc.gpsimd.memset(gate_w[:, :, :, :, :], 0.0).then_inc(s["zeroed"], 1)
            for n in range(4 * ADA_PER_LAYER):
                layer, kb, j = ada_place(n)
                slot = n % ADA_SLOTS
                if n >= ADA_SLOTS:
                    pool.wait_ge(s["ada_used"], n - ADA_SLOTS + 1)
                w = d["ada_w" if layer < 2 else "ada_w_2"][layer % 2]
                pool.dma_start(ada_in[:, slot, :], w[kb * P:(kb + 1) * P, j * SLOT:(j + 1) * SLOT])\
                    .then_inc(ada_full[slot], 16)

        @block.tensor
        def _(pe):
            got = Counter()
            fills = Counter()
            owed = []

            def need(name, n=1):
                got[name] += n
                pe.wait_ge(s[name], got[name])

            def fill(b, readers=1):
                if fills[b]:
                    pe.wait_ge(bank_free[b], fills[b])
                fills[b] += readers

            def mm(out, lhsT, rhs, start=True, stop=True, inc=None, shared=False):
                ins = nc.tensor.matmul(out, lhsT, rhs, start=start, stop=stop, skip_group_check=shared)
                if inc is not None:
                    ins.then_inc(s[inc], 1)
                elif owed:
                    ins.then_inc(s["units_used"], owed.pop())
                return ins

            def arrive(key):
                slot, count, _ = plan[key]
                pe.wait_ge(slot_full[slot], 16 * count)

            def project(key, b, kbs, moving, blocks, width=256, col=0, per_kb=None, inc=None):
                arrive(key)
                w = slot_view(key, kbs, width)
                for i in range(blocks):
                    m = min(P, width - i * P)
                    for kb in range(kbs):
                        if per_kb and i == 0:
                            need(per_kb)
                        last = i == blocks - 1 and kb == kbs - 1
                        mm(bank[b][0:m, col + i * T:col + (i + 1) * T], w[:, kb, i * P:i * P + m], moving(kb),
                           start=(kb == 0), stop=(kb == kbs - 1), inc=inc if last else None)
                owed.append(1)

            def project_tokens(kind, li, banks, inc):
                for b in banks:
                    fill(b)
                for j in range(2):
                    arrive((kind, li, j))
                    w = slot_view((kind, li, j), KB, 256)
                    for tb, b in enumerate(banks):
                        for kb in range(KB):
                            last = j == 1 and tb == TB - 1 and kb == KB - 1
                            mm(bank[b][:, j * 256:(j + 1) * 256], h[:, kb, tb * P:(tb + 1) * P], w[:, kb, :],
                               start=(kb == 0), stop=(kb == KB - 1), inc=inc if last else None)
                    owed.append(1)

            def hk(kb):
                return h[:, kb, :]

            def norm_sum():
                need("norm_sq")
                fill(7)
                sq = region(0, KB * T).rearrange("p (k t) -> p k t", k=KB)
                for kb in range(KB):
                    mm(bank[7][:, 0:T], ones, sq[:, kb, :], start=(kb == 0), stop=(kb == KB - 1),
                       inc="norm_sum" if kb == KB - 1 else None)

            def modulation(b, j0=MOD_PARTS[0][0], j1=MOD_PARTS[0][1]):
                for j in range(j0, j1):
                    piece, c = divmod(j * P, SLOT)
                    mm(bank[b][:, j:j + 1], ada_acc[:, piece, c:c + P], ones[:, 0:1],
                       inc="mod_psum" if j + 1 in (MOD_PARTS[0][1], MOD_PARTS[1][1]) else None)

            def start_modulation():
                need("ada_done")
                fill(0)
                modulation(0)

            def start():
                pe.wait_ge(s["first_in"], 16 * len(FIRST_LOADS))
                fill(6)
                nc.tensor.transpose(bank[6][:, 0:2 * KB], c_rows[0:2 * KB, :], ident[0:2 * KB, 0:2 * KB])\
                    .then_inc(s["c_psum"], 1)
                pe.wait_ge(s["params"], 16 * N_PARAMS)
                xt = region(1024, TB * DM).rearrange("p (b f) -> p b f", b=TB)
                for g in range(4):
                    fill(2 + g)
                    for k in range(2):
                        for tb in range(TB):
                            kb = 2 * g + k
                            ins = nc.tensor.transpose(bank[2 + g][:, k * T + tb * P:k * T + (tb + 1) * P],
                                                      xt[:, tb, kb * P:(kb + 1) * P], ident)
                    ins.then_inc(s["x_psum"], 1)
                rows_in = region(0, 8 * P).rearrange("p (k f) -> p k f", k=8)
                sizes = [PACK1_ROWS] * 2 + [PACK2_ROWS] * 2 + [PACKF_ROWS] * 4
                for i, n in enumerate(sizes):
                    b = i // 4
                    if i % 4 == 0:
                        fill(b)
                    ins = nc.tensor.transpose(bank[b][:, (i % 4) * P:(i % 4) * P + n], rows_in[0:n, i, :],
                                              ident[0:n, 0:n])
                ins.then_inc(s["vcol_psum"], 1)

            def mixer1(li):
                project_bank(("rgx", li, 0), 0, "z_rgx", per_kb="h_ready")
                project_bank(("rgx", li, 1), 1, "z_rgx")
                fill(2)
                project(("flow", li, 0), 2, KB, hk, 1, width=16, inc="z_narrow")
                project_bank(("q", li, 0), 3, "z_q")
                project_bank(("k", li, 0), 5, "z_k")
                need("flow_sb")
                fill(4)
                for b2 in range(2):
                    mm(bank[4][:, b2 * T:(b2 + 1) * T], wg2[:, li, b2 * P:(b2 + 1) * P], M1["flow"][0:16, :],
                       inc="z_loggate" if b2 else None)
                project_tokens("v", li, (6, 7), "z_v")
                need("u_ready")
                u = M1["u"].rearrange("p (b t) -> p b t", b=4)
                for g, banks in enumerate(((0, 1), (2, 3))):
                    for b4 in range(4):
                        if b4 % 2 == 0:
                            fill(banks[b4 // 2])
                        mm(bank[banks[b4 // 2]][:, (b4 % 2) * T:(b4 % 2 + 1) * T], gate_w[:, li, g, b4, :],
                           u[:, b4, :], inc="ri_psum" if b4 % 2 else None)
                project_bank(("gate", li, 0), 5, "z_gate")
                project_bank(("gate", li, 1), 4, "z_gate")
                need("kend_sb")
                fill(6)
                kend = M1["kend"].rearrange("p (b t) -> p b t", b=2)
                for tb in range(TB):
                    for pair in range(2):
                        ins = nc.tensor.transpose(bank[6][:, tb * 256 + pair * P:tb * 256 + (pair + 1) * P],
                                                  kend[:, pair, tb * P:(tb + 1) * P], ident)
                ins.then_inc(s["kend_psum"], 1)
                need("k_sb")
                qloc = M1["qloc"].rearrange("p (b t) -> p b t", b=2)
                kloc = M1["kloc"].rearrange("p (b t) -> p b t", b=2)
                for hh, b in enumerate((7, 0)):
                    fill(b)
                    r = slice(64 * hh, 64 * hh + 64)
                    for i in range(4):
                        pair, tb = divmod(i, 2)
                        mm(bank[b][:, i * P:(i + 1) * P], kloc[r, pair, tb * P:(tb + 1) * P],
                           qloc[r, pair, tb * P:(tb + 1) * P], inc="scores_psum" if i == 3 else None)
                need("kt_sb")
                need("v_sb")
                kt = M1["kt"].rearrange("p (b f) -> p b f", b=TB)
                vt = M1["vt"].rearrange("p (b f) -> p b f", b=TB)
                for n, b in enumerate((1, 2, 3)):
                    fill(b)
                    r = slice(64 * (n % 2), 64 * (n % 2) + 64)
                    for pair in range(2):
                        mm(bank[b][:, pair * 256:(pair + 1) * 256], kt[r, n // 2, pair * P:(pair + 1) * P],
                           vt[r, n // 2, pair * 256:(pair + 1) * 256], inc="heads_psum" if pair else None)
                project_bank(("g", li, 0), 5, "z_outgate")
                project_bank(("g", li, 1), 4, "z_outgate")
                need("scores_sb", 2)
                need("states_sb")
                sc = M1["sc"].rearrange("p (i q) -> p i q", i=8)
                st = M1["st"].rearrange("p (n b v) -> p n b v", n=3, b=2)
                qint = M1["qint"].rearrange("p (b t) -> p b t", b=2)
                for hh, b in enumerate((6, 7)):
                    fill(b)
                    r = slice(64 * hh, 64 * hh + 64)
                    for pair in range(2):
                        head = 2 * pair + hh
                        for tb in range(TB):
                            c0 = pair * T + tb * P
                            mm(bank[b][:, c0:c0 + P], vt[:, tb, head * P:(head + 1) * P],
                               sc[:, hh * 4 + pair * 2 + tb, :], start=(pair == 0 and tb == 0), stop=True,
                               shared=True)
                        for n in range(1, 4):
                            c0 = pair * T + n * GLA_CHUNK
                            mm(bank[b][:, c0:c0 + GLA_CHUNK], st[r, n - 1, pair, :],
                               qint[r, pair, n * GLA_CHUNK:(n + 1) * GLA_CHUNK], start=False, stop=True,
                               shared=True, inc="o_psum" if pair and n == 3 else None)
                if li == 0:
                    need("ada_done")
                fill(2)
                modulation(2, MOD_PARTS[1][0], MOD_PARTS[1][0] + KB)
                need("headsq_sb", 2)
                for half in range(2):
                    fill(half)
                    mm(bank[half][:, :], ones, M1["osq"][:, half * 512:(half + 1) * 512], inc="headsum_psum")
                modulation(2, MOD_PARTS[1][0] + KB, MODS)
                project_out("wout", li, (2, 3, 5, 4))

            def project_bank(key, b, inc, per_kb=None, readers=1):
                fill(b, readers)
                project(key, b, KB, hk, 2, per_kb=per_kb, inc=inc)

            def project_out(kind, li, banks):
                need("ycat_ready")
                for j, b in enumerate(banks):
                    fill(b)
                    project((kind, li, j), b, KB, hk, 2, inc="wout_psum")

            def mixer2(li):
                fill(3)
                project(("kr", li, 0), 3, KB, hk, 1, width=P, per_kb="h_ready", inc="z_narrow")
                project_bank(("cq", li, 0), 0, "z_cq")
                fill(1)
                project(("cq", li, 1), 1, KB, hk, 1, width=P, inc="z_cq")
                project_bank(("ckv", li, 0), 2, "z_cq")
                fill(4)
                arrive(("if", li, 0))
                w = slot_view(("if", li, 0), KB, 16)
                for n in range(2):
                    for kb in range(KB):
                        mm(bank[4][0:8, n * T:(n + 1) * T], w[:, kb, 8 * n:8 * n + 8], hk(kb), start=(kb == 0),
                           stop=(kb == KB - 1), inc="z_loggate" if n and kb == KB - 1 else None)
                owed.append(1)
                project_bank(("qm", li, 0), 5, "z_qm")
                project_bank(("qm", li, 1), 6, "z_qm")
                project_bank(("km", li, 0), 7, "z_qm")
                need("cq_sq")
                fill(0)
                csq = M2["csq"].rearrange("p (b t) -> p b t", b=5)
                for b5 in range(5):
                    c0 = 0 if b5 < 3 else T
                    mm(bank[0][:, c0:c0 + T], ones, csq[:, b5, :], start=b5 in (0, 3), stop=b5 in (2, 4),
                       inc="cqsum_psum" if b5 == 4 else None)
                need("kr_sb")
                fill(1)
                mm(bank[1][:, 0:T], const[:, C_SWAP:C_SWAP + P], M2["kr"], inc="rot_psum")
                project_bank(("km", li, 1), 3, "z_qm")
                need("cqn")
                cq = M2["cq"].rearrange("p (b t) -> p b t", b=3)
                ckv = M2["ckv"].rearrange("p (b t) -> p b t", b=2)
                arrive(("uqn", li, 0))
                wn = slot_view(("uqn", li, 0), 3, 512)
                for pair in range(4):
                    b = (2, 4)[pair // 2]
                    if pair % 2 == 0:
                        fill(b)
                    for kb in range(3):
                        mm(bank[b][:, (pair % 2) * T:(pair % 2 + 1) * T], wn[:, kb, pair * P:(pair + 1) * P],
                           cq[:, kb, :], start=(kb == 0), stop=(kb == 2),
                           inc="z_uqn" if pair % 2 and kb == 2 else None)
                owed.append(1)
                arrive(("uqr", li, 0))
                wr = slot_view(("uqr", li, 0), 3, 256)
                fill(5)
                for g in range(2):
                    for kb in range(3):
                        mm(bank[5][:, g * T:(g + 1) * T], wr[:, kb, g * P:(g + 1) * P], cq[:, kb, :],
                           start=(kb == 0), stop=(kb == 2), inc="z_uqr" if g and kb == 2 else None)
                owed.append(1)
                arrive(("ukv", li, 0))
                wk = slot_view(("ukv", li, 0), 2, DM)
                for pair in range(4):
                    b = (6, 7)[pair // 2]
                    if pair % 2 == 0:
                        fill(b)
                    for kb in range(2):
                        mm(bank[b][:, (pair % 2) * T:(pair % 2 + 1) * T], wk[:, kb, pair * P:(pair + 1) * P],
                           ckv[:, kb, :], start=(kb == 0), stop=(kb == 1),
                           inc="z_ukn" if pair % 2 and kb == 1 else None)
                for tb in range(TB):
                    b = (0, 1)[tb]
                    fill(b)
                    for kb in range(2):
                        mm(bank[b][:, :], ckv[:, kb, tb * P:(tb + 1) * P], wk[:, kb, 512:1024],
                           start=(kb == 0), stop=(kb == 1), inc="z_ukv" if kb == 1 else None)
                owed.append(1)
                need("qr_sb")
                fill(3)
                mm(bank[3][:, :], const[:, C_SWAP:C_SWAP + P], M2["qr"], inc="rot_psum")
                project_tokens("vm", li, (2, 4), "z_v")
                project_bank(("om", li, 0), 5, "z_outgate")
                project_bank(("om", li, 1), 6, "z_outgate")

                need("rot_sb")
                need("rot_sb")
                need("qn_sb", 2)
                need("kn_sb", 2)
                need("va_sb", 2)
                qn = M2["qn"].rearrange("p (b t) -> p b t", b=4)
                kn = M2["kn"].rearrange("p (b t) -> p b t", b=4)
                qro = M2["qro"].rearrange("p (b t) -> p b t", b=2)
                kro = M2["kro"]
                va = M2["va"].rearrange("p (b f) -> p b f", b=TB)

                def scores(head):
                    b = head % 2
                    fill(b)
                    r = slice(64 * (head % 2), 64 * (head % 2) + 64)
                    row = 64 * (head % 2) + 32 * (head % 4 // 2)
                    rr = slice(row, row + 32)
                    for qb in range(TB):
                        c0, keys = (0, P) if qb == 0 else (P, T)
                        mm(bank[b][:, c0:c0 + keys], qn[r, head // 2, qb * P:(qb + 1) * P],
                           kn[r, head // 2, 0:keys], start=(qb == 0), stop=False, shared=True)
                        mm(bank[b][:, c0:c0 + keys], qro[rr, head // 4, qb * P:(qb + 1) * P], kro[rr, 0:keys],
                           start=False, stop=True, shared=True, inc="att_psum" if qb else None)

                def weighted(head):
                    b = 3 if head % 2 else 7
                    fill(b)
                    need("att_norm")
                    prob = M2["prob"][:, (head % 2) * 512:(head % 2) * 512 + 384]
                    for i in range(3):
                        ins = nc.tensor.transpose(bank[b][:, i * P:(i + 1) * P], prob[:, i * P:(i + 1) * P], ident)
                    ins.then_inc(s["attT_psum"], 1)

                def values(head):
                    b = (2, 4)[(head // 2) % 2]
                    if head % 2 == 0:
                        fill(b)
                    need("attT_sb")
                    pt = M2["pt"][:, (head % 2) * 384:(head % 2) * 384 + 384]
                    r = slice(64 * (head % 2), 64 * (head % 2) + 64)
                    hv = slice(head * 64, head * 64 + 64)
                    mm(bank[b][r, 0:P], va[:, 0, hv], pt[:, 0:P], start=True, stop=True, shared=True)
                    mm(bank[b][r, P:T], va[:, 0, hv], pt[:, P:T], start=False, stop=False, shared=True)
                    mm(bank[b][r, P:T], va[:, 1, hv], pt[:, T:384], start=False, stop=True, shared=True,
                       inc="att_y" if head % 2 else None)

                fill(5)
                for step in range(10):
                    if step < 8:
                        scores(step)
                        modulation(5, MOD_PARTS[1][0] + 4 * step, MOD_PARTS[1][0] + 4 * step + 4)
                    if 1 <= step < 9:
                        weighted(step - 1)
                    if step >= 2:
                        values(step - 2)

                need("m_rows")
                fill(5)
                for tb in range(TB):
                    ins = nc.tensor.transpose(bank[5][:, tb * 8:tb * 8 + 8], grow("a")[:, tb * P:(tb + 1) * P],
                                              ident[0:8, 0:8])
                ins.then_inc(s["atok_psum"], 1)
                need("v_sb", 2)
                need("qkm_sb", 4)
                need("em_row")
                qk = M2["qkm"].rearrange("p (b t) -> p b t", b=8)
                vt = M2["vt2"].rearrange("p (b f) -> p b f", b=TB)

                def log_weights(head):
                    b = head % 2
                    fill(b)
                    for c0, t0 in ((0, 0), (T, P)):
                        mm(bank[b][:, c0:c0 + T - t0], sel[:, head * P:(head + 1) * P], grow("m")[:, t0:T],
                           inc="mb_psum" if t0 else None)

                def products(head):
                    b = 6 if head % 2 else 7
                    fill(b)
                    r = slice(64 * (head % 2), 64 * (head % 2) + 64)
                    mm(bank[b][:, 0:T], qk[r, 4 + head // 2, 0:P], qk[r, head // 2, :])
                    mm(bank[b][:, T:384], qk[r, 4 + head // 2, P:T], qk[r, head // 2, P:T], inc="scores_psum")

                def combine(head):
                    b = (2, 4)[(head // 2) % 2]
                    be = (3, 5)[(head // 2) % 2]
                    if head % 2 == 0:
                        fill(b)
                        fill(be)
                        pair = head // 2
                        mm(bank[be][:, 0:T], sel[:, 8 * P + pair * P:8 * P + (pair + 1) * P], grow("em"))
                    need("scores_sb")
                    sw = M2["sw"][:, (head % 2) * 384:(head % 2) * 384 + 384]
                    r = slice(64 * (head % 2), 64 * (head % 2) + 64)
                    for c0, lhs in ((0, lambda tb: vt[:, tb, head * 64:head * 64 + 64]),
                                    (T, lambda tb: ones[:, 0:64])):
                        mm(bank[b][r, c0:c0 + T], lhs(0), sw[:, 0:T], start=(c0 == 0), stop=False, shared=True)
                        mm(bank[b][r, c0 + P:c0 + T], lhs(1), sw[:, T:384], start=False, stop=True, shared=True,
                           inc="heads_psum" if c0 else None)

                for step in range(9):
                    if step < 8:
                        log_weights(step)
                        products(step)
                    if step >= 1:
                        combine(step - 1)
                for j, b in enumerate((0, 1, 6, 7)):
                    project_bank(("gmla", li, j), b, "z_gm")
                need("headsq_sb")
                for half in range(2):
                    b = (2, 4)[half]
                    fill(b)
                    mm(bank[b][:, :], const[:, C_PAIR:C_PAIR + P], M2["hsq"][:, half * 512:(half + 1) * 512],
                       inc="headsum_psum")
                for j, b in enumerate((3, 5, 0, 1)):
                    project_bank(("gml", li, j), b, "z_gm")
                for kind, src, banks in (("brmla", "yla", (2, 4, 6, 7)), ("brml", "yml", (3, 5, 0, 1))):
                    need("yla_sb" if kind == "brmla" else "yml_ready", 4 if kind == "brmla" else 1)
                    y = M2[src].rearrange("p (b t) -> p b t", b=4)
                    for j in range(2):
                        arrive((kind, li, j))
                        w = slot_view((kind, li, j), 4, 512)
                        for i in range(4):
                            b = banks[j * 2 + i // 2]
                            if i % 2 == 0:
                                fill(b)
                            for kb in range(4):
                                mm(bank[b][:, (i % 2) * T:(i % 2 + 1) * T], w[:, kb, i * P:(i + 1) * P], y[:, kb, :],
                                   start=(kb == 0), stop=(kb == 3), inc="z_br" if i % 2 and kb == 3 else None)
                        owed.append(1)
                project_out("wout2", li, (2, 4, 6, 7))

            def up(slots, fb2, b):
                for w in range(2):
                    wv = ring[:, slots[w], :].rearrange("p (k f) -> p k f", k=KB)
                    for kb in range(KB):
                        mm(bank[b + w][:, 0:T], wv[:, kb, fb2 * P:(fb2 + 1) * P], hk(kb), start=(kb == 0),
                           stop=(kb == KB - 1), inc="up_done" if w and kb == KB - 1 else None)

            def up_split(chunk, slots, fb2, b, first=False):
                for w in range(2):
                    hi = w_hi[(2 * chunk + w) % 4].rearrange("p (k f) -> p k f", k=KB)
                    low = w_low[:, slots[w], :].rearrange("p (k f) -> p k f", k=KB)
                    cols = slice(fb2 * P, (fb2 + 1) * P)
                    for kb in range(KB):
                        if first and w == 0:
                            need("h_ready")
                        mm(bank[b + w][:, 0:T], hi[:, kb, cols], h_hi[:, kb, :], start=(kb == 0), stop=False)
                        mm(bank[b + w][:, 0:T], low[:, kb, cols], h_hi[:, kb, :], start=False, stop=False)
                    if first and w == 0:
                        need("h_lo")
                    for kb in range(KB):
                        mm(bank[b + w][:, 0:T], hi[:, kb, cols], h_low[:, kb, :], start=False, stop=(kb == KB - 1),
                           inc="up_done" if w and kb == KB - 1 else None)

            def down(slot, fb2, g, first, last):
                wv = ring[:, slot, :].rearrange("p (k f) -> p k f", k=2)
                for k in range(KB):
                    mm(bank[4 + k // 2][:, (k % 2) * T:(k % 2 + 1) * T], wv[:, fb2, k * P:(k + 1) * P], g,
                       start=(first and k % 2 == 0), stop=last, shared=True,
                       inc="down_done" if k == KB - 1 else None)

            def down_split(slot, fb2, n, w_hi2, first, last):
                low = w_low[:, slot, :].rearrange("p (k f) -> p k f", k=2)
                for k in range(KB):
                    cols = slice(k * P, (k + 1) * P)
                    out = bank[4 + k // 2][:, (k % 2) * T:(k % 2 + 1) * T]
                    mm(out, w_hi2[:, cols], hidden_hi[:, n, :], start=(first and k % 2 == 0), stop=False, shared=True)
                    mm(out, low[:, fb2, cols], hidden_hi[:, n, :], start=False, stop=False, shared=True)
                    mm(out, w_hi2[:, cols], hidden_low[:, n, :], start=False, stop=last, shared=True,
                       inc="down_done" if k == KB - 1 else None)

            def ffn(kind, li, f0):
                for b in range(8):
                    fill(b, readers=b // 4)
                for f in range(FFN_FB + 1):
                    if f < FFN_FB:
                        c, fb2 = divmod(f, 2)
                        keys = [(kind + n, li, c) for n in "13"]
                        if fb2 == 0:
                            need("split_lo", 2)
                        if f >= 2:
                            pe.wait_ge(s["g_ready"], f0 + f - 1)
                        up_split(c, [plan[k][0] for k in keys], fb2, 2 * (f % 2), first=(f == 0))
                        if fb2 == 1:
                            owed.append(2)
                    if f >= 1:
                        c, fb2 = divmod(f - 1, 2)
                        pe.wait_ge(s["down_lo"], f0 + f)
                        down_split(plan[(kind + "2", li, c)][0], fb2, (f - 1) % 2,
                                   (down_hi_ffn if kind == "w" else down_hi_conv)[(f - 1) % 2], f == 1, f == FFN_FB)
                        if fb2 == 1:
                            owed.append(1)

            def moe_route():
                for b in range(8):
                    fill(b, readers=0)
                need("h_ready", KB)
                fill(0)
                for tb in range(TB):
                    for kb in range(KB):
                        mm(bank[0][:, tb * 8:tb * 8 + 8], h[:, kb, tb * P:(tb + 1) * P], router[:, kb, :],
                           start=(kb == 0), stop=(kb == KB - 1),
                           inc="router_psum" if tb and kb == KB - 1 else None)
                assert not owed
                for tb in range(TB):
                    for half in range(2):
                        for k in range(4):
                            ins = nc.tensor.transpose(bank[2 + 2 * tb + half][:, k * P:(k + 1) * P],
                                                      h[:, 4 * half + k, tb * P:(tb + 1) * P], ident)
                        ins.then_inc(s["htok_psum"], 1)
                need("mask_sb")
                fill(1)
                upto = const[:, C_CAUSAL:C_CAUSAL + P]
                m0, m1 = small[:, 96:104], small[:, 104:112]
                mm(bank[1][:, 0:8], upto, m0)
                mm(bank[1][:, 8:16], ones, m0, stop=False)
                mm(bank[1][:, 8:16], upto, m1, start=False)
                mm(bank[1][:, 16:24], ones, m0, stop=False)
                mm(bank[1][:, 16:24], ones, m1, start=False, inc="rank_psum")
                need("htok_sb", 4)
                for b in range(4):
                    mm(bank[4 + b][:, :], const[:, C_ZERO:C_ZERO + P], const[:, 0:512],
                       inc="scattered" if b == 3 else None)
                need("route_ready")
                for b in range(8):
                    fill(b, readers=b // 4)
                if loop_pos > pos_before_loop:
                    pe.sem_inc(s["units_used"], loop_pos - pos_before_loop)

            def dense_gates():
                need("gates_sb")
                for tb in range(TB):
                    ins = nc.tensor.transpose(bank[1][0:8, tb * P:(tb + 1) * P], small[:, 64 + tb * 8:72 + tb * 8],
                                              ident)
                ins.then_inc(s["gatesT_psum"], 1)
                need("gatesT_sb")
                for e in range(EXPERTS):
                    mm(bank[2 + e // 2][:, (e % 2) * T:(e % 2 + 1) * T], sel[:, e * P:(e + 1) * P],
                       MF["gates_t"][0:8, :], inc="gbc_psum" if e % 2 else None)
                need("gbc_ready", 4)

            def moe_gathered(f0):
                need("spread_ready")
                for e in range(EXPERTS):
                    for tb in range(TB):
                        ins = nc.tensor.transpose(bank[e // 2][:, (e % 2) * T + tb * P:(e % 2) * T + (tb + 1) * P],
                                                  by_slot[:, tb, e * P:(e + 1) * P], ident)
                    if e % 2:
                        ins.then_inc(s["spreadT_psum"], 1)
                need("pick_ready")
                need("spreadT_sb", 4)
                htok = MS["htok"].rearrange("p (b f) -> p b f", b=TB)
                for n in range(16):
                    kb, g = divmod(n, 2)
                    if n >= 4:
                        pe.wait_ge(s[("hx_a", "hx_d")[n % 2]], (n - 4) // 2 + 1)
                    for tb in range(TB):
                        mm(bank[n % 4][:, :], htok[:, tb, kb * P:(kb + 1) * P], by_slot[:, tb, g * 512:(g + 1) * 512],
                           start=(tb == 0), stop=(tb == 1), inc="hx_psum" if tb else None)

                def up_s(pair, n):
                    i, f = divmod(n, FFN_FB)
                    slot = 3 * ((n // 2) % 2)
                    if f == 0:
                        pe.wait_ge(s["hxs_ready"], pair * 2 + (i + 1))
                    if n % 2 == 0:
                        for w in range(2):
                            pe.wait_ge(slot_full[slot + w], (pair * CHUNKS + (loop_count[slot + w] + n // 4 + 1)) * 16)
                    pe.wait_ge(s["g_ready"], pair * (2 * FFN_FB) + (f0 + n - 1))
                    for w in range(2):
                        wv = ring[:, slot + w, :].rearrange("p (k f) -> p k f", k=KB)
                        for kb in range(KB):
                            mm(bank[n % 2][:, w * P:(w + 1) * P], wv[:, kb, (n % 2) * P:(n % 2 + 1) * P],
                               hxs[i % 2][:, kb, :], start=(kb == 0), stop=(kb == KB - 1),
                               inc="up_done" if w and kb == KB - 1 else None)

                def down_s(pair, n):
                    i, f = divmod(n, FFN_FB)
                    slot = 3 * ((n // 2) % 2) + 2
                    if f == 0:
                        pe.wait_ge(s["y_free_a"], pair * 2 + (i + 1))
                        pe.wait_ge(s["y_free_d"], pair * 2 + (i + 1))
                    pe.wait_ge(s["down_lo"], pair * (2 * FFN_FB) + (f0 + n + 1))
                    low = w_low[:, slot, :].rearrange("p (k f) -> p k f", k=2)
                    for half in range(2):
                        cols = slice(half * 512, (half + 1) * 512)
                        mm(bank[2 + half][:, :], hid_hi[:, n % 2, :], down_hi_moe[n % 2][:, cols],
                           start=(f == 0), stop=False)
                        mm(bank[2 + half][:, :], hid_hi[:, n % 2, :], low[:, n % 2, cols], start=False, stop=False)
                        mm(bank[2 + half][:, :], hid_low[:, n % 2, :], down_hi_moe[n % 2][:, cols], start=False,
                           stop=(f == FFN_FB - 1), inc="down_done" if half else None)

                def spread(pair, i):
                    pe.wait_ge(s["y_free_a"], pair * 2 + (i + 2))
                    pe.wait_ge(s["y_free_d"], pair * 2 + (i + 2))
                    for k in range(KB):
                        mm(bank[4 + k // 2][:, (k % 2) * T:(k % 2 + 1) * T], MS["y"][:, k * P:(k + 1) * P],
                           MS["spread_t"][:, bass.ds((pair * 2 + i) * T, T)], start=False, stop=True, shared=True,
                           inc="scattered" if k == KB - 1 else None)

                def expert_pair(pair, last=False):
                    for n in range(2 * FFN_FB):
                        down_s(pair, n)
                        if not (last and n + 2 >= 2 * FFN_FB):
                            up_s(pair, n + 2)
                        if n % FFN_FB == FFN_FB - 1:
                            spread(pair, n // FFN_FB)

                pe.wait_ge(s["hx_d"], 8)
                up_s(0, 0)
                up_s(0, 1)
                with pe.Fori(0, EXPERTS // 2 - 1) as pair:
                    expert_pair(pair)
                expert_pair(EXPERTS // 2 - 1, last=True)
                pe.wait_ge(s["scattered"], EXPERTS + 1)
                pe.sem_inc(s["units_used"], 3 * CHUNKS * EXPERTS)

            def moe_dense(f0):
                slots = ((0, 1, 2), (0, 1, 2), (3, 4, 5), (3, 4, 5))

                def up_j(j, it, base):
                    if j % 2 == 0:
                        for w in range(2):
                            sl = slots[j][w]
                            pe.wait_ge(slot_full[sl], (it + (loop_count[sl] + 1)) * 16)
                    pe.wait_ge(s["g_ready"], it * 4 + (base + j - 1))
                    up(slots[j], j % 2, 2 * (j % 2))
                    if j % 2:
                        owed.append(2)

                def down_j(j, it, base, first=False, last=False):
                    if j % 2 == 0:
                        sl = slots[j][2]
                        pe.wait_ge(slot_full[sl], (it + (loop_count[sl] + 1)) * 16)
                    pe.wait_ge(s["g_ready"], it * 4 + (base + j + 1))
                    down(slots[j][2], j % 2, hidden[:, j % 2, :], first, last)
                    if j % 2:
                        owed.append(1)

                def one_pass(it, base, first=False, last=False):
                    for j in range(4):
                        if j < 3:
                            up_j(j + 1, it, base)
                        elif not last:
                            up_j(0, it + 1, base)
                        down_j(j, it, base, first and j == 0, last and j == 3)

                up_j(0, 0, f0)
                one_pass(0, f0, first=True)
                with pe.Fori(1, PAIR_ITERS - 1) as it:
                    one_pass(it, f0)
                one_pass(PAIR_ITERS - 1, f0, last=True)
                pe.wait_ge(s["down_done"], f0 + 4 * PAIR_ITERS)
                while owed:
                    pe.sem_inc(s["units_used"], owed.pop())

            def moe():
                most = pe.value_load(route[0:1, 0:1])
                with pe.If(most < P + 1):
                    moe_gathered(F0["moe"])
                with pe.Else():
                    dense_gates()
                    moe_dense(F0["moe"])

            start()
            norm_sum()
            start_modulation()
            mixer1(0)
            norm_sum()
            ffn("w", 0, 0)
            start_modulation()
            norm_sum()
            mixer1(1)
            norm_sum()
            moe_route()
            moe()
            norm_sum()
            start_modulation()
            norm_sum()
            mixer2(0)
            norm_sum()
            ffn("u", 0, F0["conv0"])
            start_modulation()
            norm_sum()
            mixer2(1)
            norm_sum()
            ffn("u", 1, F0["conv1"])
            norm_sum()
            pe.wait_ge(s["x_ready"], 11 * KB)
            for tb in range(TB):
                for g in range(2):
                    b = tb * 2 + g
                    fill(b)
                    for k in range(4):
                        ins = nc.tensor.transpose(bank[b][:, k * P:(k + 1) * P],
                                                  x[:, 4 * g + k, tb * P:(tb + 1) * P], ident)
                    ins.then_inc(s["outT_psum"], 1)

        @block.scalar
        def _(act):
            got = Counter()
            chain = Counter()

            def need(name, n=1):
                got[name] += n
                act.wait_ge(s[name], got[name])

            def settle(ins):
                chain["act"] += 1
                ins.then_inc(act_chain, 1)
                act.wait_ge(act_chain, chain["act"])

            def tell(ins, name, *banks):
                settle(ins)
                if name:
                    act.sem_inc(s[name], 1)
                for b in banks:
                    act.sem_inc(bank_free[b], 1)

            def func(out, in_, f, **kw):
                return nc.scalar.activation(out, in_, f, **kw)

            def start():
                for dst, src in FIRST_LOADS:
                    act.dma_start(dst, src).then_inc(s["first_in"], 16)
                need("c_psum")
                tell(func(c_col[:, :, :].rearrange("p l k -> p (l k)"), bank[6][:, 0:2 * KB], ACT.Silu), "c_act", 6)
                act.wait_ge(s["params"], 16 * N_PARAMS)
                need("vcol_ready")
                need("ang", 2)
                func(rope_sin[:, :], region(3328, T), ACT.Sin)
                settle(func(rope_cos[:, :], region(3584, T), ACT.Sin))
                act.sem_inc(s["rope_ready"], 1)

            def split_high(kind, li, chunk):
                if chunk < CHUNKS:
                    for w in range(2):
                        slot, count, _ = plan[(kind + "13"[w], li, chunk)]
                        act.wait_ge(slot_full[slot], 16 * count)
                        func(w_hi[(2 * chunk + w) % 4], ring[:, slot, :], ACT.Copy).then_inc(s["split_hi"], 1)

            def down_rows_high(kind, li, f, f0):
                slot, count, _ = plan[(kind + "2", li, f // 2)]
                if f % 2 == 0:
                    act.wait_ge(slot_full[slot], 16 * count)
                if f >= 2:
                    act.wait_ge(s["down_done"], f0 + f - 1)
                func((down_hi_ffn if kind == "w" else down_hi_conv)[f % 2][:, :],
                     ring[:, slot, (f % 2) * DM:(f % 2 + 1) * DM], ACT.Copy)

            def hidden_high(f, f0):
                act.wait_ge(s["g_ready"], f0 + f + 1)
                func(hidden_hi[:, f % 2, :], hidden[:, f % 2, :], ACT.Copy).then_inc(s["down_hi"], 1)

            def norm(biases, ffn_kind=None, li=0):
                if biases == 24:
                    need("ycat_ready")
                if ffn_kind:
                    split_high(ffn_kind, li, 0)
                need("x_ready", KB)
                sq = region(0, KB * T)
                tell(func(sq, x[:, :, :].rearrange("p k t -> p (k t)"), ACT.Square), "norm_sq")
                need("norm_sum")
                tell(func(region(2304, T), bank[7][:, 0:T], ACT.Sqrt, scale=1.0 / DM, bias=EPS), "norm_std", 7)
                if biases is not None:
                    for kb in range(KB):
                        need("norm_mul")
                        if ffn_kind:
                            func(h_hi[:, kb, :], h[:, kb, :], ACT.Identity, bias=mod[:, biases + kb:biases + kb + 1])
                        func(h[:, kb, :], h[:, kb, :], ACT.Identity,
                             bias=mod[:, biases + kb:biases + kb + 1]).then_inc(s["h_ready"], 1)

            def mixer1(li):
                v = vcol[:, li, :]
                u = M1["u"].rearrange("p (b t) -> p b t", b=4)
                for g in range(2):
                    need("z_rgx")
                    for i in range(2):
                        b4 = 2 * g + i
                        ins = func(u[:, b4, :], bank[g][:, i * T:(i + 1) * T], ACT.Identity,
                                   scale=v[:, PACK1["conv_w"] + 12 + b4:PACK1["conv_w"] + 13 + b4],
                                   bias=v[:, PACK1["conv_b"] + b4:PACK1["conv_b"] + b4 + 1])
                    tell(ins, "conv1")
                need("z_narrow")
                tell(func(M1["flow"][0:16, :], bank[2][0:16, 0:T], ACT.Copy), "flow_sb", 2)
                need("z_q")
                tell(func(M1["q"], bank[3][:, :], ACT.Copy, scale=0.125), "q_sb", 3)
                need("lf_abs")
                settle(func(M1["lf"], M1["lf"], ACT.Exp, scale=-1.0))
                tell(func(M1["lf"], M1["lf"], ACT.Ln, bias=1.0), "lf_exp")
                need("z_v")
                for tb in range(TB):
                    settle(func(M1["vt"][:, tb * 512:(tb + 1) * 512], bank[6 + tb][:, :], ACT.Copy))
                    act.sem_inc(bank_free[6 + tb], 1)
                act.sem_inc(s["v_sb"], 1)
                need("c8_ready")
                settle(func(small[:, 4:8], small[:, 4:8], ACT.Exp, scale=-1.0))
                tell(func(small[:, 4:8], small[:, 4:8], ACT.Ln, bias=1.0), "sp_exp")
                need("b_ready")
                func(M1["kloc"], M1["qloc"], ACT.Exp, scale=-1.0)
                settle(func(M1["kend"], M1["kend"], ACT.Exp))
                settle(func(M1["qloc"], M1["qloc"], ACT.Exp))
                func(M1["qint"], M1["bb"], ACT.Exp)
                bb = M1["bb"].rearrange("p (c t) -> p c t", t=GLA_CHUNK)
                tell(func(small[:, 16:24], bb[:, :, GLA_CHUNK - 1], ACT.Exp), "exps_sb")
                rr = M1["rr"].rearrange("p (b t) -> p b t", b=4)
                ii = M1["ii"].rearrange("p (b t) -> p b t", b=4)
                for g, (dst, bias) in enumerate(((rr, "ba"), (ii, "bx"))):
                    for half in range(2):
                        need("ri_psum")
                        b = 2 * g + half
                        for i in range(2):
                            b4 = 2 * half + i
                            ins = func(dst[:, b4, :], bank[b][:, i * T:(i + 1) * T], ACT.Sigmoid,
                                       bias=v[:, PACK1[bias] + b4:PACK1[bias] + b4 + 1])
                        tell(ins, None, b)
                need("rgchain_v")
                aa = M1["aa"].rearrange("p (b t) -> p b t", b=4)
                mu = M1["mu"].rearrange("p (b t) -> p b t", b=4)
                for b4 in range(4):
                    func(aa[:, b4, :], rr[:, b4, :], ACT.Exp, scale=small[:, 8 + b4:9 + b4])
                for b4 in range(4):
                    ins = func(mu[:, b4, :], rr[:, b4, :], ACT.Tanh, scale=small[:, 12 + b4:13 + b4])
                tell(ins, "rgchain_m")
                need("kend_psum")
                tell(func(M1["kt"], bank[6][:, :], ACT.Copy), "kt_sb", 6)
                for half, b in enumerate((5, 4)):
                    need("z_gate")
                    tell(func(M1["gg"][:, half * 512:(half + 1) * 512], bank[b][:, :], ACT.Gelu_apprx_tanh),
                         "gelu_sb", b)
                need("rgchain_v")
                tell(func(M1["mu"], M1["mu"], ACT.Sqrt), "mult_sb")
                for half in range(2):
                    need("o_psum")
                    tell(func(M1["osq"][:, half * 512:(half + 1) * 512], bank[6 + half][:, :], ACT.Square),
                         "headsq_sb")
                for half, b in enumerate((5, 4)):
                    need("z_outgate")
                    tell(func(M1["silug"][:, half * 512:(half + 1) * 512], bank[b][:, :], ACT.Silu),
                         "outgate_sb", b)
                for half in range(2):
                    need("headsum_psum")
                    tell(func(M1["ostd"][:, half * 512:(half + 1) * 512], bank[half][:, :], ACT.Sqrt,
                              scale=1.0 / P, bias=EPS), "headstd_sb", half)

            def mixer2(li):
                v = vcol[:, 2 + li, :]
                need("z_narrow")
                tell(func(M2["kr"], bank[3][:, 0:T], ACT.Copy), "kr_sb", 3)
                need("cq_sb", 3)
                tell(func(M2["csq"], region(0, 1280), ACT.Square), "cq_sq")
                need("lf_abs")
                settle(func(grow("lf"), grow("lf"), ACT.Exp, scale=-1.0))
                tell(func(grow("lf"), grow("lf"), ACT.Ln, bias=1.0), "lf_exp")
                qk = M2["qkm"].rearrange("p (b t) -> p b t", b=8)
                for g, b in enumerate((5, 6, 7)):
                    conv_last_tap(v, qk, g, b)
                need("cqsum_psum")
                settle(func(M2["rs"][:, 0:T], bank[0][:, 0:T], ACT.Sqrt, scale=1.0 / 384, bias=EPS))
                tell(func(M2["rs"][:, T:2 * T], bank[0][:, T:2 * T], ACT.Sqrt, scale=1.0 / 256, bias=EPS),
                     "cqstd", 0)
                conv_last_tap(v, qk, 3, 3)
                need("m_rows")
                tell(func(grow("em"), grow("mm"), ACT.Exp, scale=-1.0), "em_row")
                for half, b in enumerate((2, 4)):
                    need("z_uqn")
                    tell(func(M2["qn"][:, half * 512:(half + 1) * 512], bank[b][:, :], ACT.Copy), "qn_sb", b)
                need("z_uqr")
                tell(func(M2["qr"], bank[5][:, :], ACT.Copy), "qr_sb", 5)
                for half, b in enumerate((6, 7)):
                    need("z_ukn")
                    tell(func(M2["kn"][:, half * 512:(half + 1) * 512], bank[b][:, :], ACT.Copy), "kn_sb", b)
                for tb in range(TB):
                    need("z_ukv")
                    tell(func(M2["va"][:, tb * 512:(tb + 1) * 512], bank[tb][:, :], ACT.Copy), "va_sb", tb)
                need("z_v")
                for tb, b in enumerate((2, 4)):
                    tell(func(M2["vt2"][:, tb * 512:(tb + 1) * 512], bank[b][:, :], ACT.Copy), "v_sb", b)
                for half, b in enumerate((5, 6)):
                    need("z_outgate")
                    tell(func(M2["om"][:, half * 512:(half + 1) * 512], bank[b][:, :], ACT.Sigmoid), "outgate_sb", b)
                for g in range(4):
                    need("conv2")
                    tell(func(qk[:, 2 * g:2 * g + 2, :], qk[:, 2 * g:2 * g + 2, :], ACT.Silu), "qkm_sb")
                def exponentials(head):
                    need("att_max")
                    o = (head % 2) * 512
                    col = 96 + 8 * (head % 2)
                    for qb in range(TB):
                        c0, n = (o, P) if qb == 0 else (o + P, T)
                        ins = func(M2["prob"][:, c0:c0 + n], M2["prob"][:, c0:c0 + n], ACT.Exp,
                                   bias=small[:, col + qb:col + qb + 1],
                                   accum_out=small[:, col + 2 + qb:col + 3 + qb])
                    tell(ins, "att_exp")

                def turned(head):
                    need("attT_psum")
                    b = 3 if head % 2 else 7
                    pt = M2["pt"][:, (head % 2) * 384:(head % 2) * 384 + 384]
                    tell(func(pt, bank[b][:, 0:384], ACT.Copy), "attT_sb", b)

                for step in range(9):
                    if step < 8:
                        exponentials(step)
                    if step >= 1:
                        turned(step - 1)
                for head in range(8):
                    need("w_arg")
                    wm = M2["wm"][:, (head % 2) * 384:(head % 2) * 384 + 384]
                    tell(func(wm, wm, ACT.Exp, scale=-1.0), "w_exp")
                need("hm_ready", 4)
                tell(func(M2["hsq"], M2["hm"], ACT.Square), "headsq_sb")
                for j, b in enumerate((0, 1, 6, 7)):
                    need("z_gm")
                    tell(func(M2["gm1"][:, j * 512:(j + 1) * 512], bank[b][:, :], ACT.Sigmoid), "gm_sb", b)
                for half in range(2):
                    need("headsum_psum")
                    b = (2, 4)[half]
                    tell(func(M2["hstd"][:, half * 512:(half + 1) * 512], bank[b][:, :], ACT.Sqrt,
                              scale=1.0 / 64, bias=EPS), "headstd_sb", b)
                for j, b in enumerate((3, 5, 0, 1)):
                    need("z_gm")
                    tell(func(M2["gm2"][:, j * 512:(j + 1) * 512], bank[b][:, :], ACT.Sigmoid), "gm_sb", b)

            def conv_last_tap(v, qk, g, b):
                need("z_qm")
                for i in range(2):
                    b8 = 2 * g + i
                    ins = func(qk[:, b8, :], bank[b][:, i * T:(i + 1) * T], ACT.Identity,
                               scale=v[:, PACK2["conv_w"] + 24 + b8:PACK2["conv_w"] + 25 + b8],
                               bias=v[:, PACK2["conv_b"] + b8:PACK2["conv_b"] + b8 + 1])
                tell(ins, "conv_last")

            def ffn(f0):
                for f in range(FFN_FB):
                    down_rows_high("w", 0, f, f0)
                    act.wait_ge(s["up_done"], f0 + f + 1)
                    if f >= 2:
                        act.wait_ge(s["g_ready"], f0 + f - 1)
                    func(MF["act"][:, (f % 2) * T:(f % 2 + 1) * T], bank[2 * (f % 2)][:, 0:T], ACT.Silu)\
                        .then_inc(s["silu_done"], 1)
                    hidden_high(f, f0)
                    if f % 2 == 0:
                        split_high("w", 0, f // 2 + 1)

            def moe_route():
                need("lgt_exp")
                tell(func(small[:, 48:64], small[:, 48:64], ACT.Exp), "sp_exp")
                for b in range(4):
                    need("htok_psum")
                    func(MS["htok"][:, b * 512:(b + 1) * 512], bank[2 + b][:, :], ACT.Copy)\
                        .then_inc(s["htok_sb"], 1)
                need("route_ready")

            def moe_dense(f0):
                for j in range(4):
                    need("gbc_psum")
                    func(MF["gbc"][:, j * 512:(j + 1) * 512], bank[2 + j][:, :], ACT.Copy)\
                        .then_inc(s["gbc_ready"], 1)
                with act.Fori(0, PAIR_ITERS) as it:
                    for j in range(4):
                        act.wait_ge(s["up_done"], it * 4 + (f0 + j + 1))
                        act.wait_ge(s["g_ready"], it * 4 + (f0 + j - 1))
                        func(MF["act"][:, (j % 2) * T:(j % 2 + 1) * T], bank[2 * (j % 2)][:, 0:T], ACT.Silu)\
                            .then_inc(s["silu_done"], 1)
                act.sem_inc(s["down_hi"], EXPERTS * FFN_FB)

            def moe_gathered(f0):
                for b in range(4):
                    need("spreadT_psum")
                    func(MS["spread_t"][:, b * 512:(b + 1) * 512], bank[b][:, :], ACT.Copy)\
                        .then_inc(s["spreadT_sb"], 1)
                hx = MS["hx"].rearrange("p (k f) -> p k f", k=KB)
                for n in range(0, 16, 2):
                    act.wait_ge(s["hx_psum"], n + 1)
                    ins = func(hx[:, n // 2, 0:512], bank[n % 4][:, :], ACT.Copy)
                    ins.then_inc(s["hx_a"], 1)
                act.wait_ge(s["hx_a"], 8)
                act.wait_ge(s["hx_psum"], 16)
                for i in range(2):
                    func(hxs[i], hx[:, :, i * P:(i + 1) * P], ACT.Copy).then_inc(s["hxs_ready"], 1)
                act.sem_inc(s["y_free_a"], 1)

                def block(pair, n):
                    slot = 3 * ((n // 2) % 2) + 2
                    before = pair * (2 * FFN_FB) + (f0 + n)
                    if n % 2 == 0:
                        act.wait_ge(slot_full[slot], (pair * CHUNKS + (loop_count[slot] + n // 4 + 1)) * 16)
                    act.wait_ge(s["down_done"], before - 1)
                    func(down_hi_moe[n % 2][:, :], ring[:, slot, (n % 2) * DM:(n % 2 + 1) * DM], ACT.Copy)
                    act.wait_ge(s["up_done"], before + 1)
                    act.wait_ge(s["g_ready"], before - 1)
                    func(MS["act"][:, (n % 2) * P:(n % 2 + 1) * P], bank[n % 2][:, 0:P], ACT.Silu)\
                        .then_inc(s["silu_done"], 1)
                    act.wait_ge(s["g_ready"], before + 1)
                    func(hid_hi[:, n % 2, :], MS["hid"][:, (n % 2) * P:(n % 2 + 1) * P], ACT.Copy)\
                        .then_inc(s["down_hi"], 1)

                def expert(pair, i, refill):
                    for n in range(i * FFN_FB, (i + 1) * FFN_FB):
                        block(pair, n)
                    if refill:
                        func(hxs[i], hx[:, :, bass.ds((pair * 2 + (i + 2)) * P, P)], ACT.Copy)\
                            .then_inc(s["hxs_ready"], 1)
                    act.wait_ge(s["down_done"], pair * (2 * FFN_FB) + (f0 + (i + 1) * FFN_FB))
                    act.wait_ge(s["scattered"], pair * 2 + (i + 1))
                    func(MS["y"][:, 0:512], bank[2][:, :], ACT.Copy).then_inc(s["y_free_a"], 1)

                with act.Fori(0, EXPERTS // 2 - 1) as pair:
                    for i in range(2):
                        expert(pair, i, True)
                for i in range(2):
                    expert(EXPERTS // 2 - 1, i, False)

            def moe():
                most = act.value_load(route[0:1, 0:1])
                with act.If(most < P + 1):
                    moe_gathered(F0["moe"])
                with act.Else():
                    moe_dense(F0["moe"])

            def conv_ffn(li, f0):
                t1, t2 = vcol[:, 4 + 2 * li, :], vcol[:, 5 + 2 * li, :]
                s0 = f0 - F0["conv0"]
                def taps(f):
                    act.wait_ge(s["up_done"], f0 + f + 1)
                    if f >= 2:
                        act.wait_ge(s["g_ready"], f0 + f - 1)
                    for w in range(2):
                        blk = w * FFN_FB + f
                        ins = func(MF["cv"][:, (2 * (f % 2) + w) * T:(2 * (f % 2) + w + 1) * T],
                                   bank[2 * (f % 2) + w][:, 0:T], ACT.Identity,
                                   scale=t2[:, blk:blk + 1],
                                   bias=t2[:, 2 * FFN_FB + blk:2 * FFN_FB + blk + 1])
                    ins.then_inc(s["conv_a"], 1)
                def gelu(f):
                    act.wait_ge(s["conv_v"], s0 + f + 1)
                    c0 = 2 * (f % 2) * T
                    func(MF["cv"][:, c0:c0 + T], MF["cv"][:, c0:c0 + T], ACT.Gelu_apprx_tanh)\
                        .then_inc(s["gelu_done"], 1)
                for f in range(FFN_FB):
                    down_rows_high("u", li, f, f0)
                    taps(f)
                    gelu(f)
                    hidden_high(f, f0)
                    if f % 2 == 0:
                        split_high("u", li, f // 2 + 1)

            start()
            norm(0)
            mixer1(0)
            norm(24, "w")
            ffn(0)
            norm(0)
            mixer1(1)
            norm(24)
            moe_route()
            moe()
            norm(None)
            norm(0)
            mixer2(0)
            norm(24, "u", 0)
            conv_ffn(0, F0["conv0"])
            norm(0)
            mixer2(1)
            norm(24, "u", 1)
            conv_ffn(1, F0["conv1"])
            norm(None)

        @block.vector
        def _(dve):
            got = Counter()
            chain = Counter()

            def need(name, n=1):
                got[name] += n
                dve.wait_ge(s[name], got[name])

            def settle(ins):
                chain["dve"] += 1
                ins.then_inc(dve_chain, 1)
                dve.wait_ge(dve_chain, chain["dve"])

            def tell(ins, name, *banks):
                settle(ins)
                if name:
                    dve.sem_inc(s[name], 1)
                for b in banks:
                    dve.sem_inc(bank_free[b], 1)

            def tt(out, a, b, op):
                return nc.vector.tensor_tensor(out, a, b, op)

            def ts(out, a, s1, op0, s2=None, op1=None):
                if op1 is None:
                    return nc.vector.tensor_scalar(out, a, s1, None, op0)
                return nc.vector.tensor_scalar(out, a, s1, s2, op0, op1)

            def stt(out, a, sc, b, op0, op1):
                return nc.vector.scalar_tensor_tensor(out, a, sc, b, op0, op1)

            def ada_piece(n):
                layer, kb, j = ada_place(n)
                slot = n % ADA_SLOTS
                dve.wait_ge(ada_full[slot], 16 * (n // ADA_SLOTS + 1))
                scalar = c_col[:, layer // 2, kb:kb + 1]
                if kb == 0:
                    ins = ts(ada_acc[:, j, :], ada_in[:, slot, :], scalar, ALU.mult)
                else:
                    dve.wait_ge(s["ada_used"], n if layer == 0 else n - ADA_SLOTS + 1)
                    ins = stt(ada_acc[:, j, :], ada_in[:, slot, :], scalar, ada_acc[:, j, :], ALU.mult, ALU.add)
                ins.then_inc(s["ada_used"], 1)

            def ada_finish(layer):
                dve.wait_ge(s["ada_used"], (layer + 1) * ADA_PER_LAYER)
                dve.sem_inc(s["ada_done"], 1)

            late_pieces = iter(range(KB, ADA_PER_LAYER))

            def late(li, count):
                if li == 0:
                    for _ in range(count):
                        ada_piece(next(late_pieces))

            def modulation(layer, part, b):
                need("mod_psum")
                pack = (PACK1, PACK2)[layer // 2]
                g = pack[("norm_mix", "norm_ffn")[part]]
                v = vcol[:, layer, :]
                c0, c1 = MOD_PARTS[part]
                tell(tt(mod[:, c0:c1], bank[b][:, c0:c1], v[:, c0:c1], ALU.add), None, b)
                settle(stt(scale_a[:, part, :], mod[:, 24 * part + 8:24 * part + 16], 1.0, v[:, g:g + 8],
                           ALU.add, ALU.mult))

            def split_low(kind, li, chunk):
                if chunk < CHUNKS:
                    for w in range(2):
                        need("split_hi")
                        slot = plan[(kind + "13"[w], li, chunk)][0]
                        tt(w_low[:, slot, :], ring[:, slot, :],
                           w_hi[(2 * chunk + w) % 4].bitcast(F32), ALU.subtract).then_inc(s["split_lo"], 1)

            def split_down(kind, li, f, f0):
                dve.wait_ge(s["down_hi"], f0 + f + 1)
                slot = plan[(kind + "2", li, f // 2)][0]
                rows_of = slice((f % 2) * DM, (f % 2 + 1) * DM)
                hi = (down_hi_ffn if kind == "w" else down_hi_conv)[f % 2]
                tt(hidden_low[:, f % 2, :], hidden[:, f % 2, :], hidden_hi[:, f % 2, :].bitcast(F32), ALU.subtract)
                tt(w_low[:, slot, rows_of], ring[:, slot, rows_of], hi[:, :].bitcast(F32), ALU.subtract)\
                    .then_inc(s["down_lo"], 1)

            def split_h(norms):
                for kb in range(KB):
                    dve.wait_ge(s["h_ready"], norms * KB + kb + 1)
                    ins = tt(h_low[:, kb, :], h[:, kb, :], h_hi[:, kb, :].bitcast(F32), ALU.subtract)
                ins.then_inc(s["h_lo"], 1)

            def norm(scale, out, inc):
                need("norm_std")
                settle(nc.vector.reciprocal(region(2048, T), region(2304, T)))
                for kb in range(KB):
                    stt(out[:, kb, :], x[:, kb, :], scale[:, kb:kb + 1], region(2048, T), ALU.mult, ALU.mult)\
                        .then_inc(s[inc], 1)

            def start():
                need("c_act")
                for n in range(5):
                    ada_piece(n)
                for g in range(4):
                    need("x_psum")
                    settle(nc.vector.tensor_copy(x[:, 2 * g:2 * g + 2, :],
                                                 bank[2 + g][:, :].rearrange("p (k t) -> p k t", k=2)))
                    dve.sem_inc(bank_free[2 + g], 1)
                    dve.sem_inc(s["x_ready"], 2)
                need("vcol_psum")
                packs = [bank[i][:, :].rearrange("p (k f) -> p k f", k=4) for i in range(2)]
                for k, lo, n in ((0, 0, PACK1_ROWS), (0, 2, PACK2_ROWS), (1, 0, PACKF_ROWS), (1, 2, PACKF_ROWS)):
                    ins = nc.vector.tensor_copy(vcol[:, 4 * k + lo:4 * k + lo + 2, 0:n], packs[k][:, lo:lo + 2, 0:n])
                tell(ins, "vcol_ready", 0, 1)
                posf, ang, turns, cosa, flag = (region(3072 + 256 * i, T) for i in (3, 1, 4, 2, 5))
                settle(nc.vector.tensor_copy(posf, region(3072, T).bitcast(I32)))
                settle(ts(ang, posf, const[:, C_INV:C_INV + 1], ALU.mult))
                settle(ts(turns, ang, float(1.0 / (2.0 * np.pi)), ALU.mult, ROUND_MAGIC, ALU.add))
                settle(ts(turns, turns, ROUND_MAGIC, ALU.subtract))
                settle(stt(ang, turns, -TWO_PI_HI, ang, ALU.mult, ALU.add))
                settle(stt(ang, turns, -TWO_PI_LO, ang, ALU.mult, ALU.add))
                settle(ts(cosa, ang, float(np.pi / 2), ALU.add))
                settle(ts(flag, cosa, float(np.pi), ALU.is_gt))
                settle(stt(cosa, flag, float(-2.0 * np.pi), cosa, ALU.mult, ALU.add))
                tell(ts(cosa, cosa, 3.1415925, ALU.min, -3.1415925, ALU.max), "ang")
                tell(ts(ang, ang, 3.1415925, ALU.min, -3.1415925, ALU.max), "ang")
                for n in range(5, KB):
                    ada_piece(n)
                dve.wait_ge(s["ada_used"], KB)
                dve.sem_inc(s["ada_done"], 1)

            def log_sigmoid(dst, ax, xb, e_name="lf_exp"):
                tell(stt(ax, xb, -1.0, xb, ALU.mult, ALU.max), "lf_abs")
                need(e_name)
                settle(stt(dst, xb, 0.0, ax, ALU.min, ALU.subtract))

            def mixer1(li):
                v = vcol[:, li, :]
                u = M1["u"].rearrange("p (b t) -> p b t", b=4)
                col = lambda name, i: v[:, PACK1[name] + i:PACK1[name] + i + 1]
                nc.vector.memset(M1["sc"], 0.0)
                late(li, 3)
                for g in range(2):
                    need("conv1")
                    need("z_rgx")
                    for lag in (1, 2, 3):
                        for i in range(2):
                            b4 = 2 * g + i
                            ins = stt(u[:, b4, lag:T], bank[g][:, i * T:(i + 1) * T - lag],
                                      col("conv_w", (3 - lag) * 4 + b4), u[:, b4, lag:T], ALU.mult, ALU.add)
                        settle(ins)
                    dve.sem_inc(bank_free[g], 1)
                dve.sem_inc(s["u_ready"], 1)
                late(li, 3)
                need("z_loggate")
                fx = M1["bb"]
                for b2 in range(2):
                    ins = ts(fx[:, b2 * T:(b2 + 1) * T], bank[4][:, b2 * T:(b2 + 1) * T], col("bg", b2), ALU.add)
                tell(ins, None, 4)
                log_sigmoid(M1["lf"], M1["lf"], fx)
                settle(ts(M1["lf"], M1["lf"], 1.0 / 16.0, ALU.mult))
                for b2 in range(2):
                    ins = nc.vector.tensor_tensor_scan(M1["bb"][:, b2 * T:(b2 + 1) * T],
                                                       const[:, C_RESET:C_RESET + T],
                                                       M1["lf"][:, b2 * T:(b2 + 1) * T], 0.0, ALU.mult, ALU.add)
                settle(ins)
                lam = v[:, PACK1["lam"]:PACK1["lam"] + 4]
                tell(stt(small[:, 4:8], lam, -1.0, lam, ALU.mult, ALU.max), "c8_ready")
                bb = M1["bb"].rearrange("p (c t) -> p c t", t=GLA_CHUNK)
                view = lambda name: M1[name].rearrange("p (c t) -> p c t", t=GLA_CHUNK)
                tt(view("qloc"), bb, bb[:, :, GLA_CHUNK // 2 - 1:GLA_CHUNK // 2].to_broadcast([P, 8, GLA_CHUNK]),
                   ALU.subtract)
                tell(stt(view("kend"), bb, -1.0, bb[:, :, GLA_CHUNK - 1:].to_broadcast([P, 8, GLA_CHUNK]),
                         ALU.mult, ALU.add), "b_ready")
                late(li, 3)
                need("sp_exp")
                settle(ts(small[:, 0:4], lam, -1.0, ALU.mult, 0.0, ALU.max))
                settle(tt(small[:, 0:4], small[:, 0:4], small[:, 4:8], ALU.add))
                ts(small[:, 8:12], small[:, 0:4], -8.0, ALU.mult)
                tell(ts(small[:, 12:16], small[:, 0:4], 8.0, ALU.mult), "rgchain_v")
                need("z_k")
                tell(nc.vector.tensor_copy(M1["k"], bank[5][:, :]), None, 5)
                need("exps_sb")
                need("q_sb")
                tell(tt(M1["kend"], M1["kend"], M1["k"], ALU.mult), "kend_sb")
                tt(M1["kloc"], M1["kloc"], M1["k"], ALU.mult)
                tt(M1["qloc"], M1["qloc"], M1["q"], ALU.mult)
                tell(tt(M1["qint"], M1["qint"], M1["q"], ALU.mult), "k_sb")
                need("rgchain_m")
                settle(ts(M1["rec"], M1["mu"], 1.0, ALU.add))
                settle(nc.vector.reciprocal(M1["rec"], M1["rec"]))
                settle(stt(M1["mu"], M1["mu"], 2.0, M1["rec"], ALU.mult, ALU.mult))
                tell(ts(M1["mu"], M1["mu"], 1e-30, ALU.max), "rgchain_v")
                late(li, 4)
                for half, b in enumerate((7, 0)):
                    need("scores_psum")
                    mask = const[:, C_GLA:C_GLA + P].bitcast(U32).unsqueeze(1).to_broadcast([P, 4, P])
                    tell(nc.vector.copy_predicated(
                        M1["sc"].rearrange("p (i q) -> p i q", i=8)[:, 4 * half:4 * half + 4, :], mask,
                        bank[b][:, :].rearrange("p (i q) -> p i q", i=4)), "scores_sb", b)
                st = M1["st"].rearrange("p (n b v) -> p n b v", n=3, b=2)
                for n, b in enumerate((1, 2, 3)):
                    need("heads_psum")
                    for pair in range(2):
                        for hh in range(2):
                            r = slice(64 * hh, 64 * hh + 64)
                            upd = bank[b][r, pair * 256 + hh * P:pair * 256 + (hh + 1) * P]
                            if n == 0:
                                ins = nc.vector.tensor_copy(st[r, 0, pair, :], upd)
                            else:
                                ins = stt(st[r, n, pair, :], st[r, n - 1, pair, :],
                                          small[r, 16 + pair * 4 + n:17 + pair * 4 + n], upd, ALU.mult, ALU.add)
                    tell(ins, None, b)
                dve.sem_inc(s["states_sb"], 1)
                late(li, 3)
                if li == 0:
                    ada_finish(0)
                need("mult_sb")
                mu = M1["mu"].rearrange("p (b t) -> p b t", b=4)
                nc.vector.memset(mu[:, :, 0], 1.0)
                settle(tt(M1["u"], M1["u"], M1["ii"], ALU.mult))
                settle(tt(M1["u"], M1["u"], M1["mu"], ALU.mult))
                for b4 in range(4):
                    sl = slice(b4 * T, (b4 + 1) * T)
                    ins = nc.vector.tensor_tensor_scan(M1["mu"][:, sl], M1["aa"][:, sl], M1["u"][:, sl], 0.0,
                                                       ALU.mult, ALU.add)
                settle(ins)
                need("gelu_sb", 2)
                need("outgate_sb", 2)
                hh1 = h[:, 0:4, :].rearrange("p k t -> p (k t)")
                settle(tt(hh1, M1["mu"], M1["gg"], ALU.mult))
                for hh in range(2):
                    need("headstd_sb")
                    sl = slice(hh * 512, (hh + 1) * 512)
                    settle(nc.vector.reciprocal(M1["ostd"][:, sl], M1["ostd"][:, sl]))
                    tell(stt(M1["on"][:, sl], bank[6 + hh][:, :], col("gla_g", 0), M1["ostd"][:, sl],
                             ALU.mult, ALU.mult), None, 6 + hh)
                    for pair in range(2):
                        head = 2 * pair + hh
                        ins = tt(h[:, 4 + head, :], M1["on"][:, (2 * hh + pair) * T:(2 * hh + pair + 1) * T],
                                 M1["silug"][:, head * T:(head + 1) * T], ALU.mult)
                tell(ins, "ycat_ready")
                modulation(li, 1, 2)
                if li == 0:
                    split_low("w", 0, 0)
                residual((2, 3, 5, 4), 16, "wout_psum")

            def residual(banks, gate_col, name):
                for j, b in enumerate(banks):
                    if name:
                        need(name)
                    for i in range(2):
                        k = 2 * j + i
                        ins = stt(x[:, k, :], bank[b][:, i * T:(i + 1) * T], mod[:, gate_col + k:gate_col + k + 1],
                                  x[:, k, :], ALU.mult, ALU.add)
                    settle(ins)
                    dve.sem_inc(bank_free[b], 1)
                    dve.sem_inc(s["x_ready"], 2)

            def mixer2(li):
                v = vcol[:, 2 + li, :]
                col = lambda name, i: v[:, PACK2[name] + i:PACK2[name] + i + 1]
                for b, dst in ((0, M2["cq"][:, 0:512]), (1, M2["cq"][:, 512:768]), (2, M2["ckv"])):
                    need("z_cq")
                    tell(nc.vector.tensor_copy(dst, bank[b][:, 0:dst.shape[1]]), "cq_sb", b)
                need("z_loggate")
                settle(ts(grow("fb"), bank[4][0:8, T:2 * T], gate_b[:, li, 1:2], ALU.add))
                log_sigmoid(grow("lf"), grow("lf"), grow("fb"))
                one8 = const[0:8, C_ONES:C_ONES + T]
                settle(nc.vector.tensor_tensor_scan(grow("b"), one8, grow("lf"), 0.0, ALU.mult, ALU.add))
                tell(stt(grow("a"), bank[4][0:8, 0:T], gate_b[:, li, 0:1], grow("b"), ALU.add, ALU.subtract), None, 4)
                settle(nc.vector.tensor_tensor_scan(grow("m"), one8, grow("a"), 0.0, ALU.mult, ALU.max))
                tell(tt(grow("mm"), grow("b"), grow("m"), ALU.add), "m_rows")
                qk = M2["qkm"].rearrange("p (b t) -> p b t", b=8)
                for g, b in enumerate((5, 6, 7)):
                    conv_taps(v, qk, g, b)
                need("cqstd")
                settle(nc.vector.reciprocal(M2["rs"], M2["rs"]))
                for b5 in range(5):
                    src = M2["cq"][:, b5 * T:(b5 + 1) * T] if b5 < 3 else M2["ckv"][:, (b5 - 3) * T:(b5 - 2) * T]
                    w = col("q_norm", b5) if b5 < 3 else col("kv_norm", b5 - 3)
                    ins = stt(src, src, w, M2["rs"][:, 0:T] if b5 < 3 else M2["rs"][:, T:2 * T],
                              ALU.mult, ALU.mult)
                tell(ins, "cqn")
                conv_taps(v, qk, 3, 3)
                if li == 0:
                    need("rope_ready")
                need("kr_sb")
                need("rot_psum")
                settle(tt(M2["kro"], M2["kr"], rope_cos[:, :], ALU.mult))
                tell(tt(M2["kr"], bank[1][:, 0:T], rope_sin[:, :], ALU.mult), None, 1)
                tell(tt(M2["kro"], M2["kro"], M2["kr"], ALU.add), "rot_sb")
                need("qr_sb")
                need("rot_psum")
                for g in range(2):
                    sl = slice(g * T, (g + 1) * T)
                    settle(tt(M2["qro"][:, sl], M2["qr"][:, sl], rope_cos[:, :], ALU.mult))
                    ins = tt(M2["qr"][:, sl], bank[3][:, sl], rope_sin[:, :], ALU.mult)
                tell(ins, None, 3)
                tell(tt(M2["qro"], M2["qro"], M2["qr"], ALU.add), "rot_sb")

                def masked(head):
                    need("att_psum")
                    o = (head % 2) * 512
                    b = head % 2
                    c = 96 + 8 * (head % 2)
                    tell(stt(M2["prob"][:, o:o + 384], bank[b][:, 0:384], QK_SCALE,
                             const[:, C_CHUNKMASK:C_CHUNKMASK + 384], ALU.mult, ALU.add), None, b)
                    for qb in range(TB):
                        c0, n = (o, P) if qb == 0 else (o + P, T)
                        ins = nc.vector.tensor_reduce(small[:, c + 4 + qb:c + 5 + qb], M2["prob"][:, c0:c0 + n],
                                                      AX_X, ALU.max)
                    settle(ins)
                    tell(ts(small[:, c:c + 2], small[:, c + 4:c + 6], -1.0, ALU.mult), "att_max")

                def normalised(head):
                    need("att_exp")
                    o = (head % 2) * 512
                    c = 96 + 8 * (head % 2)
                    settle(nc.vector.reciprocal(small[:, c + 6:c + 8], small[:, c + 2:c + 4]))
                    ts(M2["prob"][:, o:o + P], M2["prob"][:, o:o + P], small[:, c + 6:c + 7], ALU.mult)
                    tell(ts(M2["prob"][:, o + P:o + 384], M2["prob"][:, o + P:o + 384], small[:, c + 7:c + 8],
                            ALU.mult), "att_norm")

                def attended(head):
                    if head % 2:
                        pair = head // 2
                        need("att_y")
                        b = (2, 4)[pair % 2]
                        tell(nc.vector.tensor_copy(M2["yla"][:, pair * T:(pair + 1) * T], bank[b][:, 0:T]),
                             "yla_sb", b)

                for step in range(10):
                    if 1 <= step < 9:
                        normalised(step - 1)
                    if step < 8:
                        masked(step)
                    if step >= 2:
                        attended(step - 2)

                modulation(2 + li, 1, 5)
                need("atok_psum")
                tell(nc.vector.tensor_copy(small[:, 112:128], bank[5][:, 0:16]), None, 5)

                def log_weights(head):
                    need("mb_psum")
                    b = head % 2
                    wm = M2["wm"][:, (head % 2) * 384:(head % 2) * 384 + 384]
                    ts(wm[:, 0:T], bank[b][:, 0:T], small[:, 112 + head:113 + head], ALU.subtract, 0.0, ALU.max)
                    tell(ts(wm[:, T:384], bank[b][:, T:384], small[:, 120 + head:121 + head], ALU.subtract,
                            0.0, ALU.max), "w_arg", b)

                def weights(head):
                    need("w_exp")
                    need("scores_psum")
                    wm = M2["wm"][:, (head % 2) * 384:(head % 2) * 384 + 384]
                    sw = M2["sw"][:, (head % 2) * 384:(head % 2) * 384 + 384]
                    b = 6 if head % 2 else 7
                    settle(tt(wm, wm, const[:, C_CAUSAL:C_CAUSAL + 384], ALU.mult))
                    tell(stt(sw, bank[b][:, 0:384], 0.125, wm, ALU.mult, ALU.mult), "scores_sb", b)

                def outputs(pair):
                    need("heads_psum", 2)
                    b, be = (2, 4)[pair % 2], (3, 5)[pair % 2]
                    den, hm = M2["den"], M2["hm"][:, pair * T:(pair + 1) * T]
                    settle(ts(hm, bank[b][:, T:2 * T], -1.0, ALU.mult))
                    settle(tt(den, bank[b][:, T:2 * T], hm, ALU.max))
                    tell(tt(den, den, bank[be][:, 0:T], ALU.max), None, be)
                    settle(nc.vector.reciprocal(den, den))
                    tell(tt(hm, bank[b][:, 0:T], den, ALU.mult), "hm_ready", b)

                for step in range(10):
                    if 1 <= step < 9:
                        weights(step - 1)
                    if step < 8:
                        log_weights(step)
                    if step >= 3 and step % 2 == 1:
                        outputs((step - 3) // 2)
                need("outgate_sb", 2)
                for half in range(2):
                    need("headstd_sb")
                    sl = slice(half * 512, (half + 1) * 512)
                    settle(nc.vector.reciprocal(M2["hstd"][:, sl], M2["hstd"][:, sl]))
                    for i in range(2):
                        pair = 2 * half + i
                        sp2 = slice(pair * T, (pair + 1) * T)
                        ins = stt(M2["yml"][:, sp2], M2["hm"][:, sp2], col("head_norm", pair),
                                  M2["hstd"][:, sp2], ALU.mult, ALU.mult)
                    settle(ins)
                    ins = tt(M2["yml"][:, sl], M2["yml"][:, sl], M2["om"][:, sl], ALU.mult)
                tell(ins, "yml_ready")
                need("gm_sb", 4)
                for j, b in enumerate((2, 4, 6, 7)):
                    need("z_br")
                    sl = slice(j * 512, (j + 1) * 512)
                    tell(tt(M2["brt"][:, sl], bank[b][:, :], M2["gm1"][:, sl], ALU.mult), None, b)
                need("gm_sb", 4)
                for j, b in enumerate((3, 5, 0, 1)):
                    need("z_br")
                    sl = slice(j * 512, (j + 1) * 512)
                    tell(tt(M2["gm2"][:, sl], bank[b][:, :], M2["gm2"][:, sl], ALU.mult), None, b)
                    ins = tt(h[:, 2 * j:2 * j + 2, :].rearrange("p k t -> p (k t)"), M2["gm2"][:, sl],
                             M2["brt"][:, sl], ALU.add)
                tell(ins, "ycat_ready")
                split_low("u", li, 0)
                residual((2, 4, 6, 7), 16, "wout_psum")

            def conv_taps(v, qk, g, b):
                need("conv_last")
                for lag in (1, 2, 3):
                    for i in range(2):
                        b8 = 2 * g + i
                        ins = stt(qk[:, b8, lag:T], bank[b][:, i * T:(i + 1) * T - lag],
                                  v[:, PACK2["conv_w"] + (3 - lag) * 8 + b8:PACK2["conv_w"] + (3 - lag) * 8 + b8 + 1],
                                  qk[:, b8, lag:T], ALU.mult, ALU.add)
                    settle(ins)
                dve.sem_inc(s["conv2"], 1)
                dve.sem_inc(bank_free[b], 1)

            def ffn(f0, ada_layer):
                pieces = iter(range(ada_layer * ADA_PER_LAYER, (ada_layer + 1) * ADA_PER_LAYER))
                for f in range(FFN_FB):
                    dve.wait_ge(s["silu_done"], f0 + f + 1)
                    if f >= 2:
                        dve.wait_ge(s["down_done"], f0 + f - 1)
                    tt(hidden[:, f % 2, :], MF["act"][:, (f % 2) * T:(f % 2 + 1) * T],
                       bank[2 * (f % 2) + 1][:, 0:T], ALU.mult).then_inc(s["g_ready"], 1)
                    split_down("w", 0, f, f0)
                    if f % 2 == 0:
                        split_low("w", 0, f // 2 + 1)
                    for n in range(ADA_AT[f]):
                        ada_piece(next(pieces))
                ada_finish(ada_layer)
                dve.wait_ge(s["down_done"], f0 + FFN_FB)
                residual((4, 5, 6, 7), 40, None)

            def moe_route():
                need("router_psum")
                L = small[:, 32:48]
                tell(nc.vector.tensor_copy(L, bank[0][:, 0:16]), None, 0)
                ltm = const[:, C_LT:C_LT + 64].rearrange("p (e j) -> p e j", e=8)
                for tb in range(TB):
                    l = small[:, 32 + 8 * tb:40 + 8 * tb]
                    lj = l.unsqueeze(1).to_broadcast([P, 8, 8])
                    le = l.unsqueeze(2).to_broadcast([P, 8, 8])
                    gt = small[:, 128:192].rearrange("p (e j) -> p e j", e=8)
                    eq = small[:, 192:256].rearrange("p (e j) -> p e j", e=8)
                    tt(gt, lj, le, ALU.is_gt)
                    settle(tt(eq, lj, le, ALU.is_equal))
                    settle(tt(eq, eq, ltm, ALU.mult))
                    settle(tt(gt, gt, eq, ALU.add))
                    settle(nc.vector.tensor_reduce(small[:, 80:88], gt, AX_X, ALU.add))
                    settle(ts(small[:, 96 + 8 * tb:104 + 8 * tb], small[:, 80:88], 1.5, ALU.is_lt))
                    settle(nc.vector.tensor_reduce(small[:, 88:89], l, AX_X, ALU.max))
                    settle(ts(small[:, 48 + 8 * tb:56 + 8 * tb], l, small[:, 88:89], ALU.subtract))
                dve.sem_inc(s["lgt_exp"], 1)
                dve.sem_inc(s["mask_sb"], 1)
                need("sp_exp")
                settle(tt(small[:, 64:80], small[:, 96:112], small[:, 48:64], ALU.mult))
                settle(nc.vector.tensor_reduce(small[:, 88:90], small[:, 64:80].rearrange("p (b e) -> p b e", b=2),
                                               AX_X, ALU.add))
                settle(nc.vector.reciprocal(small[:, 90:92], small[:, 88:90]))
                for tb in range(TB):
                    g = small[:, 64 + 8 * tb:72 + 8 * tb]
                    ins = ts(g, g, small[:, 90 + tb:91 + tb], ALU.mult)
                tell(ins, "gates_sb")
                need("rank_psum")
                settle(nc.vector.tensor_copy(small[:, 112:136], bank[1][:, 0:24]))
                dve.sem_inc(bank_free[1], 1)
                settle(nc.vector.tensor_reduce(small[:, 92:93], small[:, 128:136], AX_X, ALU.max))
                tell(nc.vector.tensor_copy(route[0:1, 0:1], small[0:1, 92:93]), "route_ready")

            def moe():
                most = dve.value_load(route[0:1, 0:1])
                with dve.If(most < P + 1):
                    moe_gathered(F0["moe"])
                with dve.Else():
                    moe_dense(F0["moe"])
                residual((4, 5, 6, 7), 40, None)

            def moe_gathered(f0):
                n0 = 2 * ADA_PER_LAYER
                rank_row = const[:, C_RANK:C_RANK + P]

                def slots_of(scale_col, inc):
                    for tb in range(TB):
                        for e in range(EXPERTS):
                            k = tb * 8 + e
                            ins = ts(by_slot[:, tb, e * P:(e + 1) * P], rank_row, small[:, 112 + k:113 + k],
                                     ALU.is_equal, small[:, scale_col + k:scale_col + k + 1], ALU.mult)
                    ins.then_inc(s[inc], 1)

                need("htok_psum", 4)
                slots_of(64, "spread_ready")
                need("spreadT_psum", 4)
                slots_of(96, "pick_ready")
                hx = MS["hx"].rearrange("p (k f) -> p k f", k=KB)
                for n in range(1, 16, 2):
                    dve.wait_ge(s["hx_psum"], n + 1)
                    nc.vector.tensor_copy(hx[:, n // 2, 512:1024], bank[n % 4][:, :]).then_inc(s["hx_d"], 1)
                for n in range(ADA_SLOTS):
                    ada_piece(n0 + n)
                dve.sem_inc(s["y_free_d"], 1)

                def block(pair, n):
                    slot = 3 * ((n // 2) % 2) + 2
                    before = pair * (2 * FFN_FB) + (f0 + n)
                    cols, rows_of = slice((n % 2) * P, (n % 2 + 1) * P), slice((n % 2) * DM, (n % 2 + 1) * DM)
                    dve.wait_ge(s["silu_done"], before + 1)
                    dve.wait_ge(s["down_done"], before - 1)
                    tt(MS["hid"][:, cols], MS["act"][:, cols], bank[n % 2][:, P:2 * P], ALU.mult)\
                        .then_inc(s["g_ready"], 1)
                    dve.wait_ge(s["down_hi"], before + 1)
                    tt(hid_low[:, n % 2, :], MS["hid"][:, cols], hid_hi[:, n % 2, :].bitcast(F32), ALU.subtract)
                    tt(w_low[:, slot, rows_of], ring[:, slot, rows_of], down_hi_moe[n % 2][:, :].bitcast(F32),
                       ALU.subtract).then_inc(s["down_lo"], 1)

                def expert(pair, i, ada=True):
                    for f in range(FFN_FB):
                        block(pair, i * FFN_FB + f)
                        if ada and f in (7, 15, 21):
                            add_piece(pair * 2 + (i + 1), f // 8)
                    dve.wait_ge(s["down_done"], pair * (2 * FFN_FB) + (f0 + (i + 1) * FFN_FB))
                    dve.wait_ge(s["scattered"], pair * 2 + (i + 1))
                    nc.vector.tensor_copy(MS["y"][:, 512:1024], bank[3][:, :]).then_inc(s["y_free_d"], 1)

                with dve.Fori(0, EXPERTS // 2 - 1) as pair:
                    for i in range(2):
                        expert(pair, i)
                for i in range(2):
                    expert(EXPERTS // 2 - 1, i, ada=(i == 0))
                ada_finish(2)
                dve.wait_ge(s["scattered"], EXPERTS + 1)

            def add_piece(kb, j):
                n0 = 2 * ADA_PER_LAYER
                dve.wait_ge(ada_full[j], (kb + (2 * KB + 1)) * 16)
                dve.wait_ge(s["ada_used"], kb * ADA_SLOTS + (n0 + j - ADA_SLOTS + 1))
                nc.vector.scalar_tensor_tensor(
                    ada_acc[:, j, :], ada_in[:, j, :], c_col[:, 1, bass.ds(kb, 1)],
                    ada_acc[:, j, :], ALU.mult, ALU.add).then_inc(s["ada_used"], 1)

            def moe_dense(f0):
                n0 = 2 * ADA_PER_LAYER
                need("gatesT_psum")
                nc.vector.tensor_copy(MF["gates_t"][0:8, :], bank[1][0:8, 0:T]).then_inc(s["gatesT_sb"], 1)
                need("gbc_ready", 4)

                def one_pass(pair, c, ada_kb=None):
                    it = pair * CHUNKS + c
                    for j in range(4):
                        dve.wait_ge(s["silu_done"], it * 4 + (f0 + j + 1))
                        act_j = MF["act"][:, (j % 2) * T:(j % 2 + 1) * T]
                        nc.vector.tensor_tensor(act_j, act_j, MF["gbc"][:, bass.ds((pair * 2 + j // 2) * T, T)],
                                                ALU.mult).then_inc(s["gated"], 1)
                        dve.wait_ge(s["gated"], it * 4 + (j + 1))
                        dve.wait_ge(s["down_done"], it * 4 + (f0 + j - 1))
                        nc.vector.tensor_tensor(hidden[:, j % 2, :], act_j, bank[2 * (j % 2) + 1][:, 0:T],
                                                ALU.mult).then_inc(s["g_ready"], 1)
                        if ada_kb is not None and j < ADA_SLOTS:
                            add_piece(ada_kb, j)

                for n in range(ADA_SLOTS):
                    ada_piece(n0 + n)
                with dve.Fori(0, KB - 1) as c:
                    one_pass(0, c, c + 1)
                with dve.Fori(KB - 1, CHUNKS) as c:
                    one_pass(0, c)
                with dve.Fori(1, EXPERTS // 2) as pair:
                    with dve.Fori(0, CHUNKS) as c:
                        one_pass(pair, c)
                ada_finish(2)
                dve.wait_ge(s["down_done"], f0 + PAIR_ITERS * 4)
                dve.sem_inc(s["down_lo"], EXPERTS * FFN_FB)

            def conv_ffn(li, f0, ada_layer):
                t1, t2 = vcol[:, 4 + 2 * li, :], vcol[:, 5 + 2 * li, :]
                c0 = f0 - F0["conv0"]
                pieces = iter(range(0) if ada_layer is None else
                              range(ada_layer * ADA_PER_LAYER, (ada_layer + 1) * ADA_PER_LAYER))

                def taps(f):
                    dve.wait_ge(s["conv_a"], c0 + f + 1)
                    for lag in (1, 2):
                        for w in range(2):
                            i = 2 * (f % 2) + w
                            blk = (2 - lag) * 2 * FFN_FB + w * FFN_FB + f
                            ins = stt(MF["cv"][:, i * T + lag:(i + 1) * T], bank[i][:, 0:T - lag],
                                      t1[:, blk:blk + 1], MF["cv"][:, i * T + lag:(i + 1) * T],
                                      ALU.mult, ALU.add)
                        if lag == 1:
                            settle(ins)
                    ins.then_inc(s["conv_v"], 1)

                for f in range(FFN_FB):
                    taps(f)
                    for n in range(ADA_AT[f] if ada_layer is not None else 0):
                        ada_piece(next(pieces))
                    dve.wait_ge(s["gelu_done"], c0 + f + 1)
                    if f >= 2:
                        dve.wait_ge(s["down_done"], f0 + f - 1)
                    i = 2 * (f % 2)
                    tt(hidden[:, f % 2, :], MF["cv"][:, i * T:(i + 1) * T], MF["cv"][:, (i + 1) * T:(i + 2) * T],
                       ALU.mult).then_inc(s["g_ready"], 1)
                    split_down("u", li, f, f0)
                    if f % 2 == 0:
                        split_low("u", li, f // 2 + 1)
                if ada_layer is not None:
                    ada_finish(ada_layer)
                dve.wait_ge(s["down_done"], f0 + FFN_FB)
                residual((4, 5, 6, 7), 40, None)

            start()
            modulation(0, 0, 0)
            norm(scale_a[:, 0, :], h, "norm_mul")
            mixer1(0)
            norm(scale_a[:, 1, :], h, "norm_mul")
            split_h(1)
            ffn(0, 1)
            modulation(1, 0, 0)
            norm(scale_a[:, 0, :], h, "norm_mul")
            mixer1(1)
            norm(scale_a[:, 1, :], h, "norm_mul")
            moe_route()
            moe()
            norm(vcol[:, 1, PACK1["final"]:PACK1["final"] + KB], x, "x_ready")
            modulation(2, 0, 0)
            norm(scale_a[:, 0, :], h, "norm_mul")
            mixer2(0)
            norm(scale_a[:, 1, :], h, "norm_mul")
            split_h(5)
            conv_ffn(0, F0["conv0"], 3)
            modulation(3, 0, 0)
            norm(scale_a[:, 0, :], h, "norm_mul")
            mixer2(1)
            norm(scale_a[:, 1, :], h, "norm_mul")
            split_h(7)
            conv_ffn(1, F0["conv1"], None)
            norm(vcol[:, 3, PACK2["final"]:PACK2["final"] + KB], x, "x_ready")
            for b in range(4):
                need("outT_psum")
                tell(nc.vector.tensor_copy(region(2560 + b * 512, 512), bank[b][:, :]), "out_sb", b)


def kernel(**inputs):
    import concourse.bacc as bacc
    from concourse.bass_utils import run_bass_kernel_spmd

    nc = bacc.Bacc("TRN2", target_bir_lowering=False, num_devices=1)
    arrays = {name: np.ascontiguousarray(inputs[name]) for name in INPUTS}
    arrays["const_table"], arrays["const_sel"] = constants()
    aps = {}
    for name, a in arrays.items():
        aps[name] = nc.dram_tensor("in_" + name, a.shape, mybir.dt.from_np(a.dtype), kind="ExternalInput").ap()
    out = nc.dram_tensor("result", (1, T, DM), F32, kind="ExternalOutput").ap()
    two_blocks(nc, aps, out)
    r = run_bass_kernel_spmd(nc, [{"in_" + name: a for name, a in arrays.items()}], core_ids=[0])
    return r.results[0]["result"]
```
